# Optimizing a Trainium2 kernel written in Bass

```python
import math
import jax, jax.numpy as jnp
from jax import lax
import numpy as np

D_MODEL = 2048
BATCH = 1
SEQ = 256
DEPTH = 1

HEAD_DIM = 128
MIX_WIDTH = D_MODEL
A_HEADS = MIX_WIDTH // (2 * HEAD_DIM)
B_HEADS = MIX_WIDTH // (2 * HEAD_DIM)
A_WIDTH = A_HEADS * HEAD_DIM
B_WIDTH = B_HEADS * HEAD_DIM
DIFF_DIM = HEAD_DIM // 2
IN_WIDTH = 3 * A_WIDTH + 3 * B_WIDTH
DILATED_CONFIGS = ((128, 1), (512, 4), (2048, 16))
ROPE_THETA = 500000.0
ROPE_FRACTION = 4
D_FF = ((-(-8 * D_MODEL // 3) + 255) // 256) * 256
Q_BLOCK = 128
RMS_EPS = 1e-6
SUBLN_EPS = 1e-5
NEG_INF = -1e30


def rmsnorm(x, g, eps=RMS_EPS):
    xf = x.astype(jnp.float32)
    y = xf * lax.rsqrt(jnp.mean(xf * xf, axis=-1, keepdims=True) + eps)
    return (y * g.astype(jnp.float32)).astype(x.dtype)

def rope_tables(seq, rot_dim):
    inv_freq = ROPE_THETA ** (-jnp.arange(0, rot_dim, 2, dtype=jnp.float32) / rot_dim)
    ang = jnp.arange(seq, dtype=jnp.float32)[:, None] * inv_freq[None, :]
    return jnp.cos(ang), jnp.sin(ang)

def rope(x, cos, sin):
    r2 = cos.shape[-1]
    shape = (x.shape[1],) + (1,) * (x.ndim - 3) + (r2,)
    c, s = cos.reshape(shape), sin.reshape(shape)
    x1, x2 = x[..., :r2], x[..., r2:2 * r2]
    return jnp.concatenate([x1 * c - x2 * s, x2 * c + x1 * s, x[..., 2 * r2:]], axis=-1).astype(x.dtype)

def dilated_branch(q, k, v, dil, half):
    B, S, H, Dh = q.shape
    L = S // dil
    nb = -(-L // half)
    Lp = nb * half

    def by_residue(a):
        return a.reshape(B, L, dil, H, Dh).transpose(0, 2, 3, 1, 4)

    qs = jnp.pad(by_residue(q), ((0, 0), (0, 0), (0, 0), (0, Lp - L), (0, 0))).reshape(B, dil, H, nb, half, Dh)
    kpad = ((0, 0), (0, 0), (0, 0), (half, Lp - L + half), (0, 0))
    kp = jnp.pad(by_residue(k), kpad).reshape(B, dil, H, nb + 2, half, Dh)
    vp = jnp.pad(by_residue(v), kpad).reshape(B, dil, H, nb + 2, half, Dh)

    def band(a):
        return jnp.concatenate([a[:, :, :, :-2], a[:, :, :, 1:-1], a[:, :, :, 2:]], axis=4)

    kb, vb = band(kp), band(vp)
    s = jnp.einsum('brhnqe,brhnke->brhnqk', qs, kb, preferred_element_type=jnp.float32) * (Dh ** -0.5)
    blk = jnp.arange(nb)[:, None, None]
    qa = jnp.arange(half)[None, :, None]
    kj = jnp.arange(3 * half)[None, None, :]
    kpos = blk * half - half + kj
    dist = kj - half - qa
    mask = (jnp.abs(dist) <= half) & (kpos >= 0) & (kpos < L)
    s = jnp.where(mask, s, NEG_INF)
    m = jnp.max(s, axis=-1, keepdims=True)
    p = jnp.exp(s - m)
    den = jnp.sum(p, axis=-1)
    o = jnp.einsum('brhnqk,brhnke->brhnqe', p, vb.astype(jnp.float32)) / den[..., None]
    lse = m[..., 0] + jnp.log(den)
    o = o.reshape(B, dil, H, Lp, Dh)[:, :, :, :L].transpose(0, 3, 1, 2, 4).reshape(B, S, H, Dh)
    lse = lse.reshape(B, dil, H, Lp)[:, :, :, :L].transpose(0, 3, 1, 2).reshape(B, S, H)
    return o, lse

def dilated_attention(q, k, v):
    outs, lses = [], []
    for window, dil in DILATED_CONFIGS:
        o, lse = dilated_branch(q, k, v, dil, window // (2 * dil))
        outs.append(o)
        lses.append(lse)
    w = jax.nn.softmax(jnp.stack(lses, axis=0), axis=0)
    return jnp.einsum('gbsh,gbshe->bshe', w, jnp.stack(outs, axis=0))

def diff_attention(q, k, v, lam):
    B, S, H, _, d = q.shape
    nqb = S // Q_BLOCK
    qb = q.reshape(B, nqb, Q_BLOCK, H, 2, d).transpose(1, 0, 3, 4, 2, 5)
    kt = k.transpose(0, 2, 3, 1, 4)
    vt = v.transpose(0, 2, 1, 3)

    def one_block(qblk):
        s = jnp.einsum('bhcqe,bhcke->bhcqk', qblk, kt, preferred_element_type=jnp.float32) * (d ** -0.5)
        p = jax.nn.softmax(s, axis=-1)
        a = p[:, :, 0] - lam * p[:, :, 1]
        return jnp.einsum('bhqk,bhke->bhqe', a, vt.astype(jnp.float32))

    o = lax.map(one_block, qb)
    return o.transpose(1, 0, 3, 2, 4).reshape(B, S, H, 2 * d)

def first_inputs(seed: int = 0) -> dict:
    key = jax.random.key(seed)
    ks = jax.random.split(key, 11)
    f32 = jnp.float32

    def dense(k, shape):
        return jax.random.normal(k, shape, f32) * (shape[-2] ** -0.5)

    def gain(k, shape):
        return 1.0 + 0.02 * jax.random.normal(k, shape, f32)

    return {
        'x': jax.random.normal(ks[0], (BATCH, SEQ, D_MODEL), f32),
        'norm_attn': gain(ks[1], (DEPTH, D_MODEL)),
        'w_in': dense(ks[2], (DEPTH, D_MODEL, IN_WIDTH)),
        'lambda_qk': 0.1 * jax.random.normal(ks[3], (DEPTH, 4, DIFF_DIM), f32),
        'subln': gain(ks[4], (DEPTH, 2 * DIFF_DIM)),
        'w_out': dense(ks[5], (DEPTH, MIX_WIDTH, D_MODEL)),
        'norm_ffn': gain(ks[6], (DEPTH, D_MODEL)),
        'w_gate': dense(ks[7], (DEPTH, D_MODEL, D_FF)),
        'w_up': dense(ks[8], (DEPTH, D_MODEL, D_FF)),
        'w_down': dense(ks[9], (DEPTH, D_FF, D_MODEL)),
        'norm_final': gain(ks[10], (D_MODEL,)),
    }

def first_block(x, norm_attn, w_in, lambda_qk, subln, w_out, norm_ffn, w_gate, w_up, w_down, norm_final):
    B, S, _ = x.shape
    cos_a, sin_a = rope_tables(S, HEAD_DIM // ROPE_FRACTION)
    cos_b, sin_b = rope_tables(S, DIFF_DIM // ROPE_FRACTION)
    splits = [A_WIDTH, 2 * A_WIDTH, 3 * A_WIDTH, 3 * A_WIDTH + B_WIDTH, 3 * A_WIDTH + 2 * B_WIDTH]
    for l in range(DEPTH):
        h = rmsnorm(x, norm_attn[l])
        proj = h @ w_in[l]
        qa, ka, va, qb, kb, vb = jnp.split(proj, splits, axis=-1)
        qa = rope(qa.reshape(B, S, A_HEADS, HEAD_DIM), cos_a, sin_a)
        ka = rope(ka.reshape(B, S, A_HEADS, HEAD_DIM), cos_a, sin_a)
        va = va.reshape(B, S, A_HEADS, HEAD_DIM)
        ya = dilated_attention(qa, ka, va).astype(x.dtype).reshape(B, S, A_WIDTH)
        lam_init = 0.8 - 0.6 * math.exp(-0.3 * l)
        lq = lambda_qk[l].astype(jnp.float32)
        lam = jnp.exp(jnp.sum(lq[0] * lq[1])) - jnp.exp(jnp.sum(lq[2] * lq[3])) + lam_init
        qb = rope(qb.reshape(B, S, B_HEADS, 2, DIFF_DIM), cos_b, sin_b)
        kb = rope(kb.reshape(B, S, B_HEADS, 2, DIFF_DIM), cos_b, sin_b)
        vb = vb.reshape(B, S, B_HEADS, 2 * DIFF_DIM)
        yb = diff_attention(qb, kb, vb, lam)
        yb = (rmsnorm(yb, subln[l], SUBLN_EPS) * (1.0 - lam_init)).astype(x.dtype).reshape(B, S, B_WIDTH)
        x = x + jnp.concatenate([ya, yb], axis=-1) @ w_out[l]
        h = rmsnorm(x, norm_ffn[l])
        x = x + (jax.nn.silu(h @ w_gate[l]) * (h @ w_up[l])) @ w_down[l]
    return rmsnorm(x, norm_final)


FOX_HEADS = 8
FOX_HD = 128
FOX_WIDTH = FOX_HEADS * FOX_HD
MLSTM_HEADS = 4
MLSTM_DQK = 128
MLSTM_DV = 256
MLSTM_QK_WIDTH = MLSTM_HEADS * MLSTM_DQK
MLSTM_V_WIDTH = MLSTM_HEADS * MLSTM_DV
MLSTM_CHUNK = 64
D_FF_2 = 5632
CONV_W = 3
EPS = 1e-6

OFF_FQ = 0
OFF_FK = OFF_FQ + FOX_WIDTH
OFF_FV = OFF_FK + FOX_WIDTH
OFF_FF = OFF_FV + FOX_WIDTH
OFF_MQ = OFF_FF + FOX_HEADS
OFF_MK = OFF_MQ + MLSTM_QK_WIDTH
OFF_MV = OFF_MK + MLSTM_QK_WIDTH
OFF_MO = OFF_MV + MLSTM_V_WIDTH
OFF_MI = OFF_MO + MLSTM_V_WIDTH
OFF_MF = OFF_MI + MLSTM_HEADS
OFF_GA = OFF_MF + MLSTM_HEADS
OFF_GM = OFF_GA + D_MODEL
D_IN = OFF_GM + D_MODEL


def rmsnorm_2(x, g):
    x32 = x.astype(jnp.float32)
    y = x32 * lax.rsqrt(jnp.mean(x32 * x32, axis=-1, keepdims=True) + EPS)
    return (y * g.astype(jnp.float32)).astype(x.dtype)

def forgetting_attention(q, k, v, log_f):
    B, S, H, D = q.shape
    F = jnp.cumsum(log_f, axis=1).transpose(0, 2, 1)
    scale = D ** -0.5
    outs = []
    for blk in range(S // Q_BLOCK):
        q0, q1 = blk * Q_BLOCK, (blk + 1) * Q_BLOCK
        qb = q[:, q0:q1].astype(jnp.float32)
        kb = k[:, :q1].astype(jnp.float32)
        vb = v[:, :q1]
        logits = jnp.einsum('bqhd,bkhd->bhqk', qb, kb) * scale
        logits = logits + F[:, :, q0:q1, None] - F[:, :, None, :q1]
        q_pos = q0 + jnp.arange(Q_BLOCK)
        k_pos = jnp.arange(q1)
        causal = k_pos[None, :] <= q_pos[:, None]
        logits = jnp.where(causal, logits, -jnp.inf)
        p = jax.nn.softmax(logits, axis=-1)
        outs.append(jnp.einsum('bhqk,bkhd->bqhd', p.astype(vb.dtype), vb))
    return jnp.concatenate(outs, axis=1)

def mlstm_chunkwise(q, k, v, i_pre, log_f):
    B, S, H, DK = q.shape
    DV = v.shape[-1]
    L = MLSTM_CHUNK
    NC = S // L
    f32 = jnp.float32

    def chunks(a):
        return a.astype(f32).reshape(B, NC, L, H, a.shape[-1]).transpose(1, 0, 3, 2, 4)

    def gchunks(a):
        return a.astype(f32).reshape(B, NC, L, H).transpose(1, 0, 3, 2)

    qc = chunks(q) * (DK ** -0.5)
    kc, vc = chunks(k), chunks(v)
    ic, fc = gchunks(i_pre), gchunks(log_f)
    causal = jnp.tril(jnp.ones((L, L), dtype=bool))

    def step(carry, inp):
        C, n, m = carry
        qt, kt, vt, it, ft = inp
        b = jnp.cumsum(ft, axis=-1)
        dlog = b[..., :, None] - b[..., None, :] + it[..., None, :]
        dlog = jnp.where(causal, dlog, -jnp.inf)
        inter = b + m[..., None]
        m_row = jnp.maximum(inter, dlog.max(axis=-1))
        s = jnp.einsum('bhtd,bhsd->bhts', qt, kt) * jnp.exp(dlog - m_row[..., None])
        inter_w = jnp.exp(inter - m_row)
        num = inter_w[..., None] * jnp.einsum('bhtd,bhde->bhte', qt, C) + jnp.einsum('bhts,bhse->bhte', s, vt)
        den = inter_w * jnp.einsum('bhtd,bhd->bht', qt, n) + s.sum(axis=-1)
        h = num / jnp.maximum(jnp.abs(den), jnp.exp(-m_row))[..., None]
        bL = b[..., -1]
        w_log = bL[..., None] - b + it
        m_new = jnp.maximum(bL + m, w_log.max(axis=-1))
        decay = jnp.exp(bL + m - m_new)
        ws = jnp.exp(w_log - m_new[..., None])
        C_new = decay[..., None, None] * C + jnp.einsum('bhs,bhsd,bhse->bhde', ws, kt, vt)
        n_new = decay[..., None] * n + jnp.einsum('bhs,bhsd->bhd', ws, kt)
        return (C_new, n_new, m_new), h

    init = (jnp.zeros((B, H, DK, DV), f32), jnp.zeros((B, H, DK), f32), jnp.zeros((B, H), f32))
    _, hs = lax.scan(step, init, (qc, kc, vc, ic, fc))
    return hs.transpose(1, 0, 3, 2, 4).reshape(B, S, H, DV).astype(v.dtype)

def causal_dwconv(u, w, b):
    S = u.shape[1]
    up = jnp.pad(u, ((0, 0), (CONV_W - 1, 0), (0, 0)))
    out = b
    for j in range(CONV_W):
        out = out + up[:, j:j + S] * w[j]
    return out

def second_inputs(seed: int = 0) -> dict:
    key = jax.random.key(seed)
    ks = jax.random.split(key, 20)
    nrm = lambda k, shape, s: jax.random.normal(k, shape, jnp.float32) * s
    L = DEPTH
    return {
        "x": nrm(ks[0], (BATCH, SEQ, D_MODEL), 1.0),
        "norm1_g": 1.0 + nrm(ks[1], (L, D_MODEL), 0.1),
        "w_in": nrm(ks[2], (L, D_MODEL, D_IN), D_MODEL ** -0.5),
        "fox_f_bias": jnp.linspace(1.0, 4.0, FOX_HEADS, dtype=jnp.float32)[None] + nrm(ks[3], (L, FOX_HEADS), 0.1),
        "q_norm_g": 1.0 + nrm(ks[4], (L, FOX_HD), 0.1),
        "k_norm_g": 1.0 + nrm(ks[5], (L, FOX_HD), 0.1),
        "m_i_bias": nrm(ks[6], (L, MLSTM_HEADS), 0.1),
        "m_f_bias": jnp.linspace(3.0, 6.0, MLSTM_HEADS, dtype=jnp.float32)[None] + nrm(ks[7], (L, MLSTM_HEADS), 0.1),
        "m_norm_g": 1.0 + nrm(ks[8], (L, MLSTM_HEADS, MLSTM_DV), 0.1),
        "w_proj_a": nrm(ks[9], (L, FOX_WIDTH, D_MODEL), FOX_WIDTH ** -0.5),
        "w_proj_m": nrm(ks[10], (L, MLSTM_V_WIDTH, D_MODEL), MLSTM_V_WIDTH ** -0.5),
        "w_out": nrm(ks[11], (L, D_MODEL, D_MODEL), D_MODEL ** -0.5),
        "norm2_g": 1.0 + nrm(ks[12], (L, D_MODEL), 0.1),
        "w_up": nrm(ks[13], (L, D_MODEL, 2 * D_FF_2), D_MODEL ** -0.5),
        "conv_w": nrm(ks[14], (L, CONV_W, 2 * D_FF_2), CONV_W ** -0.5),
        "conv_b": nrm(ks[15], (L, 2 * D_FF_2), 0.02),
        "w_down": nrm(ks[16], (L, D_FF_2, D_MODEL), D_FF_2 ** -0.5),
    }

def second_block(x, norm1_g, w_in, fox_f_bias, q_norm_g, k_norm_g, m_i_bias, m_f_bias,
              m_norm_g, w_proj_a, w_proj_m, w_out, norm2_g, w_up, conv_w, conv_b, w_down):
    B, S, _ = x.shape

    for l in range(DEPTH):
        h = rmsnorm_2(x, norm1_g[l])
        z = jnp.einsum('bsd,de->bse', h, w_in[l])

        fq = rmsnorm_2(z[..., OFF_FQ:OFF_FK].reshape(B, S, FOX_HEADS, FOX_HD), q_norm_g[l])
        fk = rmsnorm_2(z[..., OFF_FK:OFF_FV].reshape(B, S, FOX_HEADS, FOX_HD), k_norm_g[l])
        fv = z[..., OFF_FV:OFF_FF].reshape(B, S, FOX_HEADS, FOX_HD)
        f_logf = jax.nn.log_sigmoid((z[..., OFF_FF:OFF_MQ] + fox_f_bias[l]).astype(jnp.float32))
        a_out = forgetting_attention(fq, fk, fv, f_logf).reshape(B, S, FOX_WIDTH)

        mq = z[..., OFF_MQ:OFF_MK].reshape(B, S, MLSTM_HEADS, MLSTM_DQK)
        mk = z[..., OFF_MK:OFF_MV].reshape(B, S, MLSTM_HEADS, MLSTM_DQK)
        mv = z[..., OFF_MV:OFF_MO].reshape(B, S, MLSTM_HEADS, MLSTM_DV)
        m_o = jax.nn.sigmoid(z[..., OFF_MO:OFF_MI]).reshape(B, S, MLSTM_HEADS, MLSTM_DV)
        m_ipre = (z[..., OFF_MI:OFF_MF] + m_i_bias[l]).astype(jnp.float32)
        m_logf = jax.nn.log_sigmoid((z[..., OFF_MF:OFF_GA] + m_f_bias[l]).astype(jnp.float32))
        hm = mlstm_chunkwise(mq, mk, mv, m_ipre, m_logf)
        m_out = (rmsnorm_2(hm, m_norm_g[l]) * m_o).reshape(B, S, MLSTM_V_WIDTH)

        g_a = jax.nn.sigmoid(z[..., OFF_GA:OFF_GM])
        g_m = jax.nn.sigmoid(z[..., OFF_GM:D_IN])
        merged = (g_a * jnp.einsum('bse,ed->bsd', a_out, w_proj_a[l])
                  + g_m * jnp.einsum('bse,ed->bsd', m_out, w_proj_m[l]))
        x = x + jnp.einsum('bsd,de->bse', merged, w_out[l])

        h2 = rmsnorm_2(x, norm2_g[l])
        u = causal_dwconv(jnp.einsum('bsd,df->bsf', h2, w_up[l]), conv_w[l], conv_b[l])
        u_gate, u_val = u[..., :D_FF_2], u[..., D_FF_2:]
        x = x + jnp.einsum('bsf,fd->bsd', jax.nn.silu(u_gate) * u_val, w_down[l])
    return x


def setup_inputs(seed=0):
    out = dict(first_inputs(seed))
    for name, value in second_inputs(seed + 1).items():
        if name != "x":
            out[name + "_2"] = value
    return out


def reference(
    x, norm_attn, w_in, lambda_qk, subln, w_out, norm_ffn, w_gate, w_up, w_down, norm_final,
    norm1_g_2, w_in_2, fox_f_bias_2, q_norm_g_2, k_norm_g_2, m_i_bias_2, m_f_bias_2, m_norm_g_2,
    w_proj_a_2, w_proj_m_2, w_out_2, norm2_g_2, w_up_2, conv_w_2, conv_b_2, w_down_2,
):
    x = first_block(
        x, norm_attn, w_in, lambda_qk, subln, w_out, norm_ffn, w_gate, w_up, w_down, norm_final,
    )
    return second_block(
        x, norm1_g_2, w_in_2, fox_f_bias_2, q_norm_g_2, k_norm_g_2, m_i_bias_2, m_f_bias_2,
        m_norm_g_2, w_proj_a_2, w_proj_m_2, w_out_2, norm2_g_2, w_up_2, conv_w_2, conv_b_2,
        w_down_2,
    )


_drawn_inputs = setup_inputs


def setup_inputs(seed=0):
    import zlib

    import numpy as np

    out = dict(_drawn_inputs(seed))
    spreads = {}
    factors = {'lambda_qk': 8.0,
     'subln': 3.917,
     'norm_ffn': 3.302,
     'q_norm_g_2': 4.08,
     'k_norm_g_2': 3.201,
     'm_i_bias_2': 64.0,
     'conv_b_2': 4.135}
    for name, (base, spread) in spreads.items():
        noise = np.random.default_rng([zlib.crc32(name.encode()), seed]).standard_normal(out[name].shape)
        drawn = base * np.exp(spread * noise) if base else spread * noise
        out[name] = __import__('jax').numpy.asarray(drawn.astype(out[name].dtype))
    for name, factor in factors.items():
        out[name] = (out[name] * factor).astype(out[name].dtype)
    return out
```

```python
from contextlib import ExitStack
import math

import concourse.bass as bass
from concourse import mybir

F32 = mybir.dt.float32
F32R = mybir.dt.float32r
ALU = mybir.AluOpType
ACT = mybir.ActivationFunctionType
X = mybir.AxisListType.X

P = 128
D = 2048
S = 256
NT = S // P
KT = D // P
HEADS = 8
M_HEADS = 4
M_DV = 256
HALF = HEADS * P
FF = 5632
RMS_EPS = 1e-6
SUBLN_EPS = 1e-5
LAM_INIT = 0.8 - 0.6 * math.exp(-0.3 * 0)
B_SCALE = 64 ** -0.5
HEAD_SCALE = 128 ** -0.5

UK = 2
W = 512
NS = 4
WH = 384
C3 = 3 * HALF
THIRDS = (2048, 2048, FF - 4096)

OFF_GATES_F = C3
OFF_M = OFF_GATES_F + HEADS
OFF_GATES_IF = OFF_M + C3
OFF_GA = OFF_GATES_IF + 2 * M_HEADS
OFF_GM = OFF_GA + D
NG = HEADS + 2 * M_HEADS

G_ATTN, G_FFN, G_FINAL, G_NORM1, G_NORM2 = (KT * j for j in range(5))
G_SUBLN, G_Q, G_K, G_M = 5 * KT, 5 * KT + 1, 5 * KT + 2, 5 * KT + 3
N_GAIN = G_M + 2 * M_HEADS
CONV_T = 2 * FF // P


def plan():
    phases, unit, group, by_act, by_dve = {}, 0, 0, 0, 0

    def add(name, units, groups, act, dve):
        nonlocal unit, group, by_act, by_dve
        phases[name] = (unit, group, by_act, by_dve)
        unit, group, by_act, by_dve = unit + units, group + groups, by_act + act, by_dve + dve

    def ffn(name):
        for t, width in enumerate(THIRDS):
            n = width // W
            add(f"{name}_up{t}", 16 * n, 2 * n, 0, 4 * n)
            add(f"{name}_down{t}", 4 * (width // (UK * P)), 4, 0, 8)

    add("in_b", 48, 6, 12, 0)
    add("in_a", 64, 8, 16, 0)
    add("out_b", 16, 4, 0, 8)
    add("out_a", 16, 4, 0, 8)
    ffn("ffn1")
    add("in_m", 48, 6, 12, 0)
    add("in_f", 64, 8, 16, 0)
    add("gate_m", 48, 8, 8, 8)
    add("gate_a", 32, 4, 8, 0)
    add("proj_a", 16, 4, 0, 8)
    add("out2", 32, 4, 0, 8)
    ffn("ffn2")
    add("end", 0, 0, 0, 0)
    return phases


PH = plan()
FOX_UNITS = ((1, 2, 4, 5, 6), (7, 8, 10, 11, 11))
FOX_SQ = (0, 5)
N_SMALL = 17
START_BANKS = (4, 5, 6, 7, 2, 3, 4, 5)
FREE = 2


def at(i, c, step):
    return c if i is None else i * step + c


class Head:

    def __init__(self, i, first, per):
        self.i, self.first, self.per = i, first, per

    def num(self, scale=1, c=0):
        return at(self.i, self.first * scale + c, self.per * scale)

    def upto(self, n=1, k=None):
        return self.num(n, n if k is None else k)


class HeadSems:

    def __init__(self, sem, kind):
        self.staged = sem(kind + "_staged")
        self.rope = sem(kind + "_rope")
        self.qk_T = sem(kind + "_qk_T")
        self.qkT = sem(kind + "_qkT")
        self.scores = sem(kind + "_scores")
        self.masked = sem(kind + "_masked")
        self.raw_max = sem(kind + "_raw_max")
        self.row_max = sem(kind + "_row_max")
        self.exps = sem(kind + "_exps")
        self.rden = sem(kind + "_rden")
        self.coef = sem(kind + "_coef")
        self.mixed = sem(kind + "_mixed")
        self.p_T = sem(kind + "_p_T")
        self.pT = sem(kind + "_pT")
        self.pv = sem(kind + "_pv")
        self.sq = sem(kind + "_sq")
        self.ms = sem(kind + "_ms")
        self.rstd = sem(kind + "_rstd")
        self.y = sem(kind + "_y")
        self.y_T = sem(kind + "_y_T")
        self.y_hi = sem(kind + "_y_hi")
        self.y_lo = sem(kind + "_y_lo")


def two_blocks(nc, a, out):
    ctx = ExitStack()
    with ctx:
        def sb(name, shape, dt=F32):
            return ctx.enter_context(nc.sbuf_tensor(name, [P, *shape], dt))

        def sem(name):
            return ctx.enter_context(nc.semaphore(name))

        x = sb("x", [NT, D])
        xT_hi, xT_lo = sb("xT_hi", [KT * S], F32R), sb("xT_lo", [KT * S], F32R)
        yT_hi, yT_lo = sb("yT_hi", [KT * S], F32R), sb("yT_lo", [KT * S], F32R)
        raw = [sb(f"raw{j}", [UK, W]) for j in range(NS)]
        w_hi = [sb(f"w_hi{j}", [UK, W], F32R) for j in range(NS)]
        w_lo = [sb(f"w_lo{j}", [UK, W], F32R) for j in range(NS)]
        z1, z2 = sb("z1", [NT, C3]), sb("z2", [NT, C3])
        ident, tri, ones = sb("ident", [P]), sb("tri", [P]), sb("ones", [P])
        causal = sb("causal", [3 * P])
        ln_count = sb("ln_count", [NT * S])
        rope_a = sb("rope_a", [2, NT * 2, 32])
        rope_b = sb("rope_b", [2, NT * 4, 16])
        gain = sb("gain", [N_GAIN])
        gain_qk = sb("gain_qk", [2])
        conv = sb("conv", [4 * CONV_T])
        gate_w = sb("gate_w", [KT, NG])
        gate_w_hi, gate_w_lo = sb("gate_w_hi", [KT, NG], F32R), sb("gate_w_lo", [KT, NG], F32R)
        gate_bias = sb("gate_bias", [NG])
        lam_t, minus_lam = sb("lam_t", [8]), sb("minus_lam", [1])
        minus_half = sb("minus_half", [NG])
        stage = sb("stage", [NT, 2, P])
        rot_u, rot_v = sb("rot_u", [P]), sb("rot_v", [P])
        qkT = sb("qkT", [2, S])
        prob = sb("prob", [NT * 2 * S])
        mix = sb("mix", [NT * S])
        pT = sb("pT", [2 * S])
        y = sb("y", [NT, S])
        junk = sb("junk", [W])
        neg_max, top = sb("neg_max", [NT, 2]), sb("top", [NT])
        den, rden = sb("den", [2, NT]), sb("rden", [2, NT])
        coef, floor = sb("coef", [NT]), sb("floor", [NT])
        head_ss, head_ms, head_rstd = sb("head_ss", [4]), sb("head_ms", [4]), sb("head_rstd", [4])
        eps_diff, eps_mlstm, eps_fox = (sb(n, [4]) for n in ("eps_diff", "eps_mlstm", "eps_fox"))
        part_ss = sb("part_ss", [NT, 4])
        ss, ms = sb("ss", [NT]), sb("ms", [NT])
        rstd, rstd_n, rstd2, half_rstd2 = sb("rstd", [NT]), sb("rstd_n", [NT]), sb("rstd2", [NT]), sb("half_rstd2", [NT])
        r_bc = prob[:, 0:S]
        diag = sb("diag", [NT, P])
        gz, lf, f_sum = sb("gz", [NT, NG]), sb("lf", [NT, NG]), sb("f_sum", [NT, NG])
        gt, a_gate = sb("gt", [NT, NG]), sb("a_gate", [NT, M_HEADS])
        h_norm = prob[:, 2 * S:4 * S].rearrange("p (t n) -> p t n", t=NT)
        ps = [ctx.enter_context(nc.psum_tensor(f"ps{j}", [P, W], F32)) for j in range(8)]
        pair = (ps[0:2], ps[2:4])

        z1f, z2f = (z[:, :, :].rearrange("p t n -> p (t n)") for z in (z1, z2))
        PAD = 2

        def tiles4(v, n):
            return v.rearrange("p (f s) -> p f s", f=4, s=n)
        gate_u = tiles4(z1f[:, 0:4 * (S + PAD)], S + PAD)
        up_u = tiles4(z1f[:, 4 * (S + PAD):8 * (S + PAD)], S + PAD)
        gate_z = tiles4(z1f[:, 8 * (S + PAD):8 * (S + PAD) + 4 * S], S)
        up_z = tiles4(z2f[:, 0:4 * S], S)
        tanh_z = tiles4(z2f[:, 4 * S:8 * S], S)
        gain_final_bc = z2f[:, 8 * S:8 * S + D]
        fresh = [z2f[:, 2 * D + g * NT * W:2 * D + (g + 1) * NT * W].rearrange("p (t n) -> p t n", t=NT) for g in range(2)]
        merged = z1f[:, 0:NT * D].rearrange("p (t n) -> p t n", t=NT)
        gm_buf = z1f[:, NT * D:NT * (D + W)].rearrange("p (t n) -> p t n", t=NT)
        ga_buf = z2f[:, 0:NT * D].rearrange("p (t n) -> p t n", t=NT)
        conv_rows = z2f[0:CONV_T, 0:4 * P].rearrange("p (j c) -> p j c", j=4)
        lam_in = z2f[:, 4 * P:6 * P].rearrange("p (j c) -> p j c", j=4)
        lam_prod = z2f[:, 6 * P:7 * P].rearrange("p (j c) -> p j c", j=2)
        gain_rows = z2f[:, 7 * P:9 * P].rearrange("p (j c) -> p j c", j=2)
        sq_out0, sq_out1 = (v[:, D:3 * D].rearrange("p (t n) -> p t n", t=NT) for v in (z2f, z1f))

        raw_landed = [sem(f"raw_landed{j}") for j in range(NS)]
        hi_ready, lo_ready = sem("hi_ready"), sem("lo_ready")
        slot_used = sem("slot_used")
        by_act, by_dve = sem("evac_by_act"), sem("evac_by_dve")
        x_landed, rows_landed, ident_landed = sem("x_landed"), sem("rows_landed"), sem("ident_landed")
        small_landed, gate_w_landed, final_landed = sem("small_landed"), sem("gate_w_landed"), sem("final_landed")
        const_set = sem("const_set")
        rows_T, gain_ready, gain_step = sem("rows_T"), sem("gain_ready"), sem("gain_step")
        kt_T, kt_hi, kt_lo = sem("kt_T"), sem("kt_hi"), sem("kt_lo")
        x_sq, part_sq, ss_ready = sem("x_sq"), sem("part_sq"), sem("ss_ready")
        ms_ready, rstd_ready, norm1_step = sem("ms_ready"), sem("rstd_ready"), sem("norm1_step")
        x_kept, fresh_part, fresh_ready = sem("x_kept"), sem("fresh_part"), sem("fresh_ready")
        lam_step, lam_exp, lam_ready = sem("lam_step"), sem("lam_exp"), sem("lam_ready")
        r_diag, r_bc_T, r_bc_ready = sem("r_diag"), sem("r_bc_T"), sem("r_bc_ready")
        tanh_ready, silu_step, act_hi, act_lo = sem("tanh_ready"), sem("silu_step"), sem("act_hi"), sem("act_lo")
        conv_step, pad_set = sem("conv_step"), sem("pad_set")
        gate_hi, gate_lo = sem("gate_hi"), sem("gate_lo")
        gates_done, gates_evac, gates_step, gates_act, log_f = (sem(n) for n in (
            "gates_done", "gates_evac", "gates_step", "gates_act", "log_f"))
        cum_done, cum_read, decay_ready = sem("cum_done"), sem("cum_read"), sem("decay_ready")
        diag_ready, decay_bc, den_part, floor_ready = sem("diag_ready"), sem("decay_bc"), sem("den_part"), sem("floor_ready")
        norm_step = sem("norm_step")
        x2_ready = sem("x2_ready")
        stored = sem("stored")
        hb, ha, hm, hf = (HeadSems(sem, k) for k in ("diff", "dil", "mlstm", "fox"))

        block = ctx.enter_context(nc.Block())
        ds = bass.ds

        def rows(w, k0=0, k1=None):
            r = w[k0:w.shape[0] if k1 is None else k1].rearrange("(u k p) n -> u p k n", k=UK, p=P)
            return [r[j] for j in range(r.shape[0])]

        def multiplied(name, i, units, step):
            return slot_used, at(i, NS + PH[name][0] + units, step)

        def evac_free(sem_, name, col, i, g):
            return sem_, at(i, FREE + PH[name][col] + 2 * g - 2, 4)

        BY_ACT, BY_DVE = 2, 3

        @block.sync
        def _(sp):
            for j, name in enumerate(("norm_attn", "norm_ffn", "norm_final", "norm1_g_2", "norm2_g_2")):
                v = a[name] if name == "norm_final" else a[name][0]
                sp.dma_start(gain_rows[j * KT:(j + 1) * KT, 0, :], v.rearrange("(k c) -> k c", c=P)).then_inc(rows_landed, 16)
            sp.dma_start(ident[:], a["c_ident"]).then_inc(ident_landed, 16)
            for t in range(NT):
                sp.dma_start(x[:, t, :], a["x"][0, t * P:(t + 1) * P, :]).then_inc(x_landed, 16)

            def stream(name, loops, parts):
                step = sum(len(units) for units, _, _ in parts)
                with sp.Fori(0, loops) as i:
                    n = PH[name][0]
                    for units, col, width in parts:
                        c = col(i)
                        for u in units:
                            src = u[:, :, ds(c, width)]
                            sp.wait_ge(lo_ready, at(i, n + 1, step))
                            sp.dma_start(raw[n % NS][:, :, 0:width], src)\
                              .then_inc(raw_landed[n % NS], 16)
                            n += 1

            def pairs(name, loops, units, c0, width):
                stream(name, loops, [(units, lambda i, g=g: i * (2 * width) + (c0 + g * width), width) for g in range(2)])

            w_in, w_out, w_in2 = a["w_in"][0], a["w_out"][0], a["w_in_2"][0]
            pairs("in_b", 3, rows(w_in), C3, W)
            small = [(tri[:], a["c_tri"]), (causal[:], a["c_causal"]),
                     (ln_count[:], a["c_count"].rearrange("p t s -> p (t s)")),
                     (rope_a[:], a["c_rope_a"]), (rope_b[:], a["c_rope_b"]),
                     (gain_rows[0:1, 1, :], a["subln"]), (gain_rows[1:2, 1, :], a["q_norm_g_2"]),
                     (gain_rows[2:3, 1, :], a["k_norm_g_2"]),
                     (gain_rows[3:3 + 2 * M_HEADS, 1, :], a["m_norm_g_2"][0].rearrange("h (e c) -> (h e) c", c=P)),
                     (lam_in, a["lambda_qk"][0].partition_broadcast(P)),
                     (gate_bias[:, 0:HEADS], a["fox_f_bias_2"][0].partition_broadcast(P)),
                     (gate_bias[:, HEADS:HEADS + M_HEADS], a["m_i_bias_2"][0].partition_broadcast(P)),
                     (gate_bias[:, HEADS + M_HEADS:NG], a["m_f_bias_2"][0].partition_broadcast(P))]
            small += [(conv_rows[:, j, :], a["conv_w_2"][0, j].rearrange("(k c) -> k c", c=P)) for j in range(3)]
            small += [(conv_rows[:, 3, :], a["conv_b_2"][0].rearrange("(k c) -> k c", c=P))]
            assert len(small) == N_SMALL
            for dst, src in small:
                sp.dma_start(dst, src).then_inc(small_landed, 16)
            pairs("in_a", 4, rows(w_in), 0, WH)
            pairs("out_b", 2, rows(w_out, HALF, D), 0, W)
            pairs("out_a", 2, rows(w_out, 0, HALF), 0, W)
            with nc.allow_non_contiguous_dma("a few gate columns"):
                for c, off, n in ((0, OFF_GATES_F, HEADS), (HEADS, OFF_GATES_IF, 2 * M_HEADS)):
                    sp.dma_start(gate_w[:, :, c:c + n], w_in2[:, off:off + n].rearrange("(k p) n -> p k n", p=P))\
                      .then_inc(gate_w_landed, 16)

            def ffn(name, w_gate, w_up, up0, w_down):
                f0 = 0
                for t, width in enumerate(THIRDS):
                    stream(f"{name}_up{t}", width // W, [
                        (rows(w_gate), lambda i: i * W + f0, W), (rows(w_up), lambda i: i * W + (up0 + f0), W)])
                    pairs(f"{name}_down{t}", 2, rows(w_down, f0, f0 + width), 0, W)
                    f0 += width

            ffn("ffn1", a["w_gate"][0], a["w_up"][0], 0, a["w_down"][0])
            sp.dma_start(gain_final_bc, a["norm_final"].partition_broadcast(P)).then_inc(final_landed, 16)
            pairs("in_m", 3, rows(w_in2), OFF_M, W)
            pairs("in_f", 4, rows(w_in2), 0, WH)
            stream("gate_m", 4, [(rows(w_in2), lambda i: i * W + OFF_GM, W),
                                 (rows(a["w_proj_m_2"][0]), lambda i: (i + 1) * W - W, W)])
            pairs("gate_a", 2, rows(w_in2), OFF_GA, W)
            pairs("proj_a", 2, rows(a["w_proj_a_2"][0]), 0, W)
            pairs("out2", 2, rows(a["w_out_2"][0]), 0, W)
            ffn("ffn2", a["w_up_2"][0], a["w_up_2"][0], FF, a["w_down_2"][0])
            out_v = out[0].rearrange("(t p) n -> p t n", p=P)
            for g in range(4):
                cols = slice(g * W, (g + 1) * W)
                sp.wait_ge(by_dve, FREE + PH["ffn2_down2"][BY_DVE] + 2 * g + 2)
                sp.dma_start(out_v[:, :, cols], x[:, :, cols]).then_inc(stored, 16)
            sp.wait_ge(stored, 16 * 4)

        @block.tensor
        def _(pe):
            def by_token(acc, src, kt, n, k, width, first, last):
                hi, lo = src
                for t in range(NT):
                    q = slice(kt * S + t * P, kt * S + (t + 1) * P)
                    o = acc[t][:, 0:width]
                    pe.matmul(o, hi[:, q], w_hi[n % NS][:, k, 0:width], start=first, stop=False)
                    pe.matmul(o, hi[:, q], w_lo[n % NS][:, k, 0:width], start=False, stop=False)
                    mm = pe.matmul(o, lo[:, q], w_hi[n % NS][:, k, 0:width], start=False, stop=last)
                return mm

            def by_feature(acc, src, kt, n, k, first, last):
                hi, lo = (v[:, kt * S:(kt + 1) * S] for v in src)
                for f in range(4):
                    c = slice(f * P, (f + 1) * P)
                    o = acc[f // 2][:, (f % 2) * S:(f % 2 + 1) * S]
                    pe.matmul(o, w_hi[n % NS][:, k, c], hi, start=first and f % 2 == 0, stop=False)
                    pe.matmul(o, w_hi[n % NS][:, k, c], lo, start=False, stop=False)
                    mm = pe.matmul(o, w_lo[n % NS][:, k, c], hi, start=False, stop=last and f % 2 == 1)
                return mm

            def group(name, i, step, g, units, src, kt0, free, width=W, feature=False, ready=None, after={}, u0=None):
                u0 = g * units if u0 is None else u0
                pe.wait_ge(*free)
                for u in range(units):
                    n = PH[name][0] + u0 + u
                    if ready:
                        ready(u)
                    pe.wait_ge(lo_ready, at(i, NS + n + 1, step))
                    for k in range(UK):
                        j = u * UK + k
                        if feature:
                            mm = by_feature(pair[g], src, kt0 + j, n, k, j == 0, j == units * UK - 1)
                        else:
                            mm = by_token(pair[g], src, kt0 + j, n, k, width, j == 0, j == units * UK - 1)
                    mm.then_inc(slot_used, 1)
                    for step_ in after.get(u0 + u, ()):
                        step_()

            def tiles_ready(base):
                return lambda u: pe.wait_ge(kt_lo, base + UK * (u + 1))

            def turn_qk(s, h):
                pe.wait_ge(s.staged, h.upto())
                pe.wait_ge(s.y_lo, h.num(2 if s is hm else 1, FREE))
                for c in range(2):
                    for t in range(NT):
                        mm = pe.transpose(ps[4][:, c * S + t * P:c * S + (t + 1) * P], stage[:, t, c, :], ident[:])
                mm.then_inc(s.qk_T, 1)

            def turn_p(s, src, blocks):
                for j, c in enumerate(blocks):
                    mm = pe.transpose(ps[4][:, j * P:(j + 1) * P], src[:, c:c + P], ident[:])
                mm.then_inc(s.p_T, 1)

            def values(s, h, z, col, width, blocks):
                pe.wait_ge(s.pT, h.upto())
                for t in range(NT):
                    keys = [kt for kt in range(2) if (t, kt) in blocks]
                    for kt in keys:
                        j = blocks[t, kt]
                        mm = pe.matmul(ps[7][:, t * width:(t + 1) * width], pT[:, j * P:(j + 1) * P],
                                       z[:, kt, ds(col, width)], start=kt == keys[0], stop=kt == keys[-1])
                mm.then_inc(s.pv, 1)

            def turn_y(s, h, bank, c0, tiles):
                pe.wait_ge(s.y, h.upto(2))
                for e in range(tiles):
                    for t in range(NT):
                        c = c0 + e * S + t * P
                        mm = pe.transpose(bank[:, c:c + P], y[:, t, e * P:(e + 1) * P], ident[:])
                mm.then_inc(s.y_T, 1)

            FULL = {(t, kt): 2 * kt + t for t in range(NT) for kt in range(2)}
            FULL_SRC = [t * S + kt * P for kt in range(2) for t in range(NT)]
            CAUSAL = {(0, 0): 0, (1, 0): 1, (1, 1): 2}
            CAUSAL_SRC = [0, P, 2 * P]

            pe.wait_ge(rows_landed, 16 * 5)
            pe.wait_ge(ident_landed, 16)
            pe.transpose(ps[0][:, 0:5 * KT], gain_rows[0:5 * KT, 0, :], ident[0:5 * KT, 0:5 * KT]).then_inc(rows_T, 1)
            pe.wait_ge(x_landed, 16 * NT)
            for j, b in enumerate(START_BANKS):
                if j >= 6:
                    pe.wait_ge(kt_lo, 2 * (j - 6) + 2)
                for c in range(2):
                    for t in range(NT):
                        kt = 2 * j + c
                        mm = pe.transpose(ps[b][:, c * S + t * P:c * S + (t + 1) * P], x[:, t, kt * P:(kt + 1) * P], ident[:])
                mm.then_inc(kt_T, 1)

            xT, yT = (xT_hi, xT_lo), (yT_hi, yT_lo)
            pe.wait_ge(gain_ready, 1)
            with pe.Fori(0, 3) as i:
                for g in range(2):
                    group("in_b", i, 16, g, 8, xT, 0, evac_free(by_act, "in_b", BY_ACT, i, g), ready=tiles_ready(0))
            pe.wait_ge(small_landed, 16 * N_SMALL)
            n_late = N_GAIN - G_SUBLN
            pe.transpose(ps[4][:, 0:n_late], gain_rows[0:n_late, 1, :], ident[0:n_late, 0:n_late]).then_inc(rows_T, 1)
            for j in range(4):
                mm = pe.transpose(ps[5][:, j * CONV_T:(j + 1) * CONV_T], conv_rows[:, j, :], ident[0:CONV_T, 0:CONV_T])
            mm.then_inc(rows_T, 1)
            pe.wait_ge(gain_ready, 3)

            with pe.Fori(0, 4) as i:
                for g in range(2):
                    h = Head(i, g, 2)

                    def scores_diff(h=h):
                        pe.wait_ge(hb.qkT, h.upto(2))
                        for t in range(NT):
                            for c in range(2):
                                e = slice(c * 64, (c + 1) * 64)
                                mm = pe.matmul(ps[5 + c][:, t * S:(t + 1) * S], qkT[e, 0, t * P:(t + 1) * P], qkT[e, 1, :],
                                               start=True, stop=True)
                                if t == NT - 1:
                                    mm.then_inc(hb.scores, 1)

                    def turn_mix(h=h):
                        pe.wait_ge(hb.mixed, h.upto(2))
                        turn_p(hb, mix, FULL_SRC)
                    u0 = 8 * g
                    group("in_a", i, 16, g, 8, xT, 0, evac_free(by_act, "in_a", BY_ACT, i, g), WH, after={
                        u0: [lambda h=h: turn_qk(hb, h)], u0 + 1: [scores_diff], u0 + 3: [turn_mix],
                        u0 + 4: [lambda h=h: values(hb, h, z1, h.num(P, 2 * HALF), P, FULL)],
                        u0 + 6: [lambda h=h: turn_y(hb, h, ps[7], S, 1)]})

            pe.wait_ge(by_act, FREE + PH["out_b"][BY_ACT])
            pe.wait_ge(hb.y_lo, FREE + HEADS)
            with pe.Fori(0, 2) as i:
                for g in range(2):
                    steps = {}
                    for j in range(2):
                        h = Head(i, 2 * g + j, 4)

                        def scores_dil(h=h):
                            pe.wait_ge(ha.qkT, h.upto(2))
                            for t in range(NT):
                                mm = pe.matmul(ps[5][:, t * S:(t + 1) * S], qkT[:, 0, t * P:(t + 1) * P], qkT[:, 1, :],
                                               start=True, stop=True)
                            mm.then_inc(ha.scores, 1)

                        def turn_prob(h=h):
                            pe.wait_ge(ha.exps, h.upto(2))
                            turn_p(ha, prob, FULL_SRC)
                        steps[4 * g + 2 * j] = [lambda h=h: turn_qk(ha, h), scores_dil]
                        steps[4 * g + 2 * j + 1] = [
                            turn_prob, lambda h=h: values(ha, h, z2, h.num(P, 2 * HALF), P, FULL),
                            lambda h=h: turn_y(ha, h, ps[7], S, 1)]
                    group("out_b", i, 8, g, 4, yT, HEADS, evac_free(by_dve, "out_b", BY_DVE, i, g), after=steps)

            def turn_x(i, g, base, summed):
                pe.wait_ge(*summed)
                pe.wait_ge(kt_lo, at(i, base + 4 * g - 4, 8))
                for b in range(2):
                    for c in range(2):
                        for t in range(NT):
                            kt = 2 * b + c
                            mm = pe.transpose(ps[4 + 2 * g + b][:, c * S + t * P:c * S + (t + 1) * P],
                                              fresh[g][:, t, kt * P:(kt + 1) * P], ident[:])
                    mm.then_inc(kt_T, 1)

            def residual(name, units, src, kt0, base, sem_=by_dve, count=None, ready=None, loops=2):
                c0 = FREE + PH[name][BY_DVE] if count is None else count
                with pe.Fori(0, loops) as i:
                    for g in range(2):
                        after = {units + 1: [lambda: turn_x(i, 0, base, (sem_, at(i, c0 + 2, 4)))],
                                 2 * units - 1: [lambda: turn_x(i, 1, base, (sem_, at(i, c0 + 4, 4)))]}
                        group(name, i, 2 * units, g, units, src, kt0, evac_free(by_dve, name, BY_DVE, i, g),
                              ready=ready, after=after)

            pe.wait_ge(ha.y_lo, FREE + HEADS)
            residual("out_a", 4, yT, 0, KT)

            def broadcast_rstd(n):
                pe.wait_ge(r_diag, 2 * n)
                for t in range(NT):
                    mm = pe.matmul(ps[4][:, t * P:(t + 1) * P], ones[:], diag[:, t, :], start=True, stop=True)
                mm.then_inc(r_bc_T, 1)

            def ffn(name, src, act, base, n_norm, fg0, last_base):
                for t, width in enumerate(THIRDS):
                    up, down, n_fg = f"{name}_up{t}", f"{name}_down{t}", width // W

                    def up_groups(i, after={}):
                        for g in range(2):
                            group(up, i, 16, g, 8, src, 0, evac_free(by_dve, up, BY_DVE, i, g), feature=True,
                                  ready=tiles_ready(base), after=after)
                    start = 0
                    if t == 0:
                        up_groups(None, {3: [lambda: broadcast_rstd(n_norm)]})
                        start = 1

                    def up_turn(i, start=start):
                        up_groups(i)
                    with pe.Fori(start, n_fg) as i:
                        up_turn(i)
                    units = width // (UK * P)

                    def act_ready(u, f=fg0):
                        pe.wait_ge(act_lo, f + u // 2 + 1)
                    fg0 += n_fg
                    if t == 2 and last_base is not None:
                        residual(down, units, act, 0, last_base, ready=act_ready)
                    else:
                        with pe.Fori(0, 2) as i:
                            for g in range(2):
                                group(down, i, 2 * units, g, units, act, 0, evac_free(by_dve, down, BY_DVE, i, g), ready=act_ready)

            ffn("ffn1", xT, yT, KT, 1, 0, 2 * KT)

            pe.wait_ge(by_dve, FREE + PH["in_m"][BY_DVE])
            base2 = 2 * KT
            with pe.Fori(0, 2) as i:
                for g in range(2):
                    group("in_m", i, 16, g, 8, xT, 0, evac_free(by_act, "in_m", BY_ACT, i, g), ready=tiles_ready(base2))
            pe.wait_ge(gate_lo, 1)
            for t in range(NT):
                o = ps[4][:, t * NG:(t + 1) * NG]
                for kt in range(KT):
                    q = slice(kt * S + t * P, kt * S + (t + 1) * P)
                    pe.matmul(o, xT_hi[:, q], gate_w_hi[:, kt, :], start=kt == 0, stop=False)
                    pe.matmul(o, xT_hi[:, q], gate_w_lo[:, kt, :], start=False, stop=False)
                    mm = pe.matmul(o, xT_lo[:, q], gate_w_hi[:, kt, :], start=False, stop=kt == KT - 1)
            mm.then_inc(gates_done, 1)

            def cumulate():
                pe.wait_ge(log_f, 1)
                pe.matmul(ps[5][:, 0:NG], tri[:], lf[:, 0, :], start=True, stop=True)
                pe.matmul(ps[5][:, NG:2 * NG], ones[:], lf[:, 0, :], start=True, stop=False)
                pe.matmul(ps[5][:, NG:2 * NG], tri[:], lf[:, 1, :], start=False, stop=True).then_inc(cum_done, 1)
            for g in range(2):
                group("in_m", 2, 16, g, 8, xT, 0, evac_free(by_act, "in_m", BY_ACT, 2, g), after={5: [cumulate]})
            pe.wait_ge(cum_read, 1)

            with pe.Fori(0, 4) as i:
                h = Head(i, 0, 1)

                def decay_rows():
                    pe.wait_ge(diag_ready, h.upto(2))
                    for kt in range(2):
                        mm = pe.matmul(ps[5][:, kt * P:(kt + 1) * P], ones[:], diag[:, kt, :], start=True, stop=True)
                    mm.then_inc(decay_bc, 1)

                def scores_mlstm():
                    pe.wait_ge(hm.qkT, h.upto(2))
                    for t, c, n in ((0, 0, P), (1, P, S)):
                        mm = pe.matmul(ps[6][:, c:c + n], qkT[:, 0, t * P:(t + 1) * P], qkT[:, 1, 0:n], start=True, stop=True)
                    mm.then_inc(hm.scores, 1)

                def turn_weights():
                    pe.wait_ge(hm.mixed, h.upto(2))
                    turn_p(hm, mix, CAUSAL_SRC)
                steps = {1: [lambda: turn_qk(hm, h)], 2: [decay_rows], 3: [scores_mlstm], 6: [turn_weights],
                         7: [lambda: values(hm, h, z1, h.num(M_DV, HALF), M_DV, CAUSAL)],
                         10: [lambda: turn_y(hm, h, ps[4], 0, 2)]}
                for g in range(2):
                    group("in_f", i, 16, g, 8, xT, 0, evac_free(by_act, "in_f", BY_ACT, i, g), WH, after=steps)

            pe.wait_ge(hm.y_lo, FREE + 2 * M_HEADS)
            with pe.Fori(0, 4) as i:
                steps = {}
                for j, (u_qk, u_s, u_p, u_v, u_y) in enumerate(FOX_UNITS):
                    h = Head(i, j, 2)

                    def scores_fox(h=h):
                        pe.wait_ge(hf.qkT, h.upto(2))
                        pe.wait_ge(diag_ready, h.upto(2, 2 * M_HEADS + 2))
                        for t, c, n in ((0, 0, P), (1, P, S)):
                            pe.matmul(ps[6][:, c:c + n], qkT[:, 0, t * P:(t + 1) * P], qkT[:, 1, 0:n], start=True, stop=False)
                            for kt in range(t + 1):
                                mm = pe.matmul(ps[6][:, c + kt * P:c + (kt + 1) * P], ones[:], diag[:, kt, :],
                                               start=False, stop=kt == t)
                        mm.then_inc(hf.scores, 1)

                    def turn_fox(h=h):
                        pe.wait_ge(hf.exps, h.upto(2))
                        turn_p(hf, prob, CAUSAL_SRC)
                    for u, step in ((u_qk, lambda h=h: turn_qk(hf, h)), (u_s, scores_fox), (u_p, turn_fox),
                                    (u_v, lambda h=h: values(hf, h, z2, h.num(P, 2 * HALF), P, CAUSAL)),
                                    (u_y, lambda h=h: turn_y(hf, h, ps[7], S, 1))):
                        steps.setdefault(u, []).append(step)
                group("gate_m", i, 12, 0, 8, xT, 0, (by_act, at(i, FREE + PH["gate_m"][BY_ACT], 2)), after=steps)
                group("gate_m", i, 12, 1, 4, yT, HEADS, (by_dve, at(i, FREE + PH["gate_m"][BY_DVE], 2)), after=steps, u0=8)

            pe.wait_ge(by_act, FREE + PH["gate_a"][BY_ACT])
            pe.wait_ge(by_dve, FREE + PH["gate_a"][BY_DVE])
            with pe.Fori(0, 2) as i:
                for g in range(2):
                    group("gate_a", i, 16, g, 8, xT, 0, evac_free(by_act, "gate_a", BY_ACT, i, g))
            pe.wait_ge(by_act, FREE + PH["proj_a"][BY_ACT])
            pe.wait_ge(hf.y_lo, FREE + HEADS)
            residual("proj_a", 4, yT, 0, 3 * KT, fresh_ready, 0)
            residual("out2", 8, xT, 0, 4 * KT, ready=tiles_ready(3 * KT))
            ffn("ffn2", yT, xT, 4 * KT, 2, FF // W, None)

        @block.scalar
        def _(act):
            def split(n, i, step, width=W):
                act.wait_ge(raw_landed[n % NS], at(i, 16 * (n // NS + 1), 16 * step // NS))
                act.wait_ge(slot_used, at(i, n + 1, step))
                nc.scalar.activation(w_hi[n % NS][:, :, 0:width], raw[n % NS][:, :, 0:width], ACT.Copy).then_inc(hi_ready, 1)

            def turn(name, i, units, steps={}, width=W, ahead=True):
                for u in range(units):
                    if ahead or u + NS < units:
                        split(PH[name][0] + NS + u, i, units, width if u + NS < units else W)
                    for step in steps.get(u, ()):
                        step()

            def start_tile(kt):
                act.wait_ge(kt_T, kt // 2 + 1)
                if kt == 0:
                    act.wait_ge(gain_ready, 1)
                nc.scalar.activation(xT_hi[:, kt * S:(kt + 1) * S], ps[START_BANKS[kt // 2]][:, kt % 2 * S:(kt % 2 + 1) * S],
                                     ACT.Copy, scale=gain[:, G_ATTN + kt:G_ATTN + kt + 1]).then_inc(kt_hi, 1)
            for kt in range(KT):
                start_tile(kt)
                if kt % 4 == 3:
                    split(kt // 4, None, 0)
            for t in range(NT):
                nc.scalar.activation(sq_out0[:, t, :], x[:, t, :], ACT.Square, accum_out=ss[:, t:t + 1]).then_inc(x_sq, 1)

            def evac(name, i, g, dst, col, width, scale, func=ACT.Copy, step=16):
                act.wait_ge(*multiplied(name, i, 8 * (g + 1), step))
                for t in range(NT):
                    nc.scalar.activation(dst[:, t, ds(col, width)], pair[g][t][:, 0:width], func,
                                         scale=scale[:, t:t + 1]).then_inc(by_act, 1)

            act.wait_ge(rstd_ready, 1)
            with act.Fori(0, 3) as i:
                turn("in_b", i, 16, {
                    7: [lambda: evac("in_b", i, 0, z1, i * (2 * W), W, rstd)],
                    15: [lambda: evac("in_b", i, 1, z1, i * (2 * W) + W, W, rstd)]})
            act.wait_ge(lam_step, 2)
            nc.scalar.activation(lam_t[:, 2:4], lam_t[:, 0:2], ACT.Exp).then_inc(lam_exp, 1)
            act.wait_ge(gain_ready, 3)

            def qk_out(s, h, scale):
                act.wait_ge(s.qk_T, h.num(1, FREE + 1))
                nc.scalar.activation(qkT[:, 0, :], ps[4][:, 0:S], ACT.Copy, scale=scale).then_inc(s.qkT, 1)
                nc.scalar.activation(qkT[:, 1, :], ps[4][:, S:2 * S], ACT.Copy).then_inc(s.qkT, 1)

            def p_out(s, h, n):
                act.wait_ge(s.p_T, h.upto())
                nc.scalar.activation(pT[:, 0:n], ps[4][:, 0:n], ACT.Copy).then_inc(s.pT, 1)

            def squares(s, h, width, scale):
                act.wait_ge(s.rden, h.upto())
                act.wait_ge(s.pv, h.upto())
                for t in range(NT):
                    nc.scalar.activation(junk[:, t * width:(t + 1) * width], ps[7][:, t * width:(t + 1) * width], ACT.Square,
                                         scale=scale[:, t:t + 1], accum_out=head_ss[:, t:t + 1]).then_inc(s.sq, 1)

            def y_hi(s, h, bank, c0, tile0, tiles, scale):
                act.wait_ge(s.y_T, h.upto())
                for e in range(tiles):
                    nc.scalar.activation(yT_hi[:, ds(h.num(tiles * S, (tile0 + e) * S), S)], bank[:, c0 + e * S:c0 + (e + 1) * S],
                                         ACT.Copy, scale=scale(e)).then_inc(s.y_hi, 1)

            with act.Fori(0, 4) as i:
                steps = {}
                for g in range(2):
                    h = Head(i, g, 2)

                    def exps(h=h):
                        for c in range(2):
                            act.wait_ge(hb.row_max, h.upto(2, c + 1))
                            for t in range(NT):
                                nc.scalar.activation(prob[:, (2 * t + c) * S:(2 * t + c + 1) * S], ps[5 + c][:, t * S:(t + 1) * S],
                                                     ACT.Exp, bias=neg_max[:, t, c:c + 1],
                                                     accum_out=den[:, c, t:t + 1]).then_inc(hb.exps, 1)
                    steps.update({
                        8 * g: [lambda h=h: qk_out(hb, h, B_SCALE)], 8 * g + 1: [exps],
                        8 * g + 3: [lambda h=h: p_out(hb, h, 2 * S)], 8 * g + 4: [lambda h=h: squares(hb, h, P, rden[:, 0])],
                        8 * g + 6: [lambda h=h: y_hi(hb, h, ps[7], S, HEADS, 1, lambda e: gain[:, G_SUBLN:G_SUBLN + 1])],
                        8 * g + 7: [lambda g=g: evac("in_a", i, g, z2, i * (2 * WH) + g * WH, WH, rstd)]})
                turn("in_a", i, 16, steps, WH)

            with act.Fori(0, 2) as i:
                steps = {}
                for j in range(4):
                    h = Head(i, j, 4)

                    def exps(h=h):
                        act.wait_ge(ha.row_max, h.upto())
                        for t in range(NT):
                            nc.scalar.activation(prob[:, t * S:(t + 1) * S], mix[:, t * S:(t + 1) * S], ACT.Exp,
                                                 bias=neg_max[:, 0, t:t + 1], accum_out=den[:, 0, t:t + 1]).then_inc(ha.exps, 1)
                    steps[2 * j] = [lambda h=h: qk_out(ha, h, 1.0), exps]
                    steps[2 * j + 1] = [lambda h=h: p_out(ha, h, 2 * S),
                                        lambda h=h: y_hi(ha, h, ps[7], S, 0, 1, lambda e: 1.0)]
                turn("out_b", i, 8, steps)

            def row_squares(i, g, e, summed):
                act.wait_ge(*summed)
                for t in range(NT):
                    act.wait_ge(part_sq, at(i, FREE + 8 * e + 2 * g + t, 4))
                    nc.scalar.activation(junk[:], fresh[g][:, t, :], ACT.Square,
                                         accum_out=part_ss[:, t, ds(at(i, g, 2), 1)]).then_inc(part_sq, 1)

            def x_hi(i, g, base, dst, gain0):
                for j in range(4):
                    act.wait_ge(kt_T, at(i, (base + 4 * g) // 2 + j // 2 + 1, 4))
                    scale = 0.5 if gain0 is None else gain[:, ds(at(i, gain0 + 4 * g + j, 8), 1)]
                    nc.scalar.activation(dst[:, ds(at(i, (4 * g + j) * S, 8 * S), S)],
                                         ps[4 + 2 * g + j // 2][:, j % 2 * S:(j % 2 + 1) * S], ACT.Copy, scale=scale)\
                      .then_inc(kt_hi, 1)

            def residual(name, units, base, dst, gain0, e=None):
                with act.Fori(0, 2) as i:
                    def sq(g):
                        if e is not None:
                            row_squares(i, g, e, (by_dve, at(i, FREE + PH[name][BY_DVE] + 2 * g + 2, 4)))
                    turn(name, i, 2 * units, {
                        units - 1: [lambda: sq(0)], units + 1: [lambda: x_hi(i, 0, base, dst, gain0)],
                        2 * units - 1: [lambda: sq(1), lambda: x_hi(i, 1, base, dst, gain0)]})

            residual("out_a", 4, KT, xT_hi, G_FFN, 0)

            def ffn(name, dst, fg0, conv_too, last_base):
                for t, width in enumerate(THIRDS):
                    up, down, n_fg, units = f"{name}_up{t}", f"{name}_down{t}", width // W, width // (UK * P)
                    f = fg0 - (FF // W if conv_too else 0)
                    with act.Fori(0, n_fg) as i:
                        def gate_tanh():
                            if conv_too:
                                act.wait_ge(conv_step, at(i, 24 * f + 12, 24))
                            else:
                                act.wait_ge(by_dve, at(i, FREE + PH[up][BY_DVE] + 2, 4))
                            nc.scalar.activation(tanh_z, gate_z, ACT.Tanh, scale=0.5).then_inc(tanh_ready, 1)

                        def hi_part():
                            if conv_too:
                                act.wait_ge(silu_step, at(i, 2 * (fg0 + 1), 2))
                            else:
                                act.wait_ge(by_dve, at(i, FREE + PH[up][BY_DVE] + 4, 4))
                            nc.scalar.activation(tiles4(dst[:, ds(i * (4 * S), 4 * S)], S), up_z, ACT.Copy, scale=0.5).then_inc(act_hi, 1)
                        turn(up, i, 16, {9 if conv_too else 8: [gate_tanh], 15: [hi_part]})
                    fg0 += n_fg
                    if t == 2 and last_base is not None:
                        residual(down, units, last_base, xT_hi, G_NORM1, 1)
                    elif t == 2:
                        for i in range(2):
                            turn(down, i, 2 * units, ahead=i == 0)
                    else:
                        with act.Fori(0, 2) as i:
                            turn(down, i, 2 * units)

            ffn("ffn1", yT_hi, 0, False, 2 * KT)

            act.wait_ge(gate_w_landed, 32)
            nc.scalar.activation(gate_w_hi[:], gate_w[:], ACT.Copy).then_inc(gate_hi, 1)
            act.wait_ge(x2_ready, 2)
            for t in range(NT):
                nc.scalar.activation(sq_out1[:, t, :], x[:, t, :], ACT.Square, accum_out=ss[:, t:t + 1]).then_inc(x_sq, 1)
            act.wait_ge(rstd_ready, 4)
            with act.Fori(0, 2) as i:
                turn("in_m", i, 16, {
                    7: [lambda: evac("in_m", i, 0, z1, i * (2 * W), W, rstd2)],
                    15: [lambda: evac("in_m", i, 1, z1, i * (2 * W) + W, W, rstd2)]})

            def gates_out():
                act.wait_ge(gates_done, 1)
                for t in range(NT):
                    nc.scalar.activation(gz[:, t, :], ps[4][:, t * NG:(t + 1) * NG], ACT.Copy, scale=rstd2[:, t:t + 1]).then_inc(gates_evac, 1)

            def softplus():
                act.wait_ge(gates_step, 2)
                nc.scalar.activation(gt[:], gt[:], ACT.Exp, scale=-1.0).then_inc(gates_act, 1)
                act.wait_ge(gates_act, 1)
                nc.scalar.activation(gt[:], gt[:], ACT.Ln, bias=1.0).then_inc(gates_act, 1)
            turn("in_m", 2, 16, {
                0: [gates_out], 1: [softplus],
                7: [lambda: evac("in_m", 2, 0, z1, 4 * W, W, half_rstd2, ACT.Tanh)],
                15: [lambda: evac("in_m", 2, 1, z1, 5 * W, W, half_rstd2, ACT.Tanh)]})

            with act.Fori(0, 4) as i:
                h = Head(i, 0, 1)

                def decay():
                    act.wait_ge(hm.row_max, h.upto())
                    for t, c, n in ((0, 0, P), (1, P, S)):
                        nc.scalar.activation(prob[:, c:c + n], mix[:, c:c + n], ACT.Exp, bias=neg_max[:, 0, t:t + 1]).then_inc(hm.exps, 1)
                    for t in range(NT):
                        nc.scalar.activation(floor[:, t:t + 1], f_sum[:, t, ds(h.num(1, HEADS + M_HEADS), 1)], ACT.Exp, scale=-1.0,
                                             bias=neg_max[:, 0, t:t + 1]).then_inc(floor_ready, 1)
                turn("in_f", i, 16, {
                    1: [lambda: qk_out(hm, h, HEAD_SCALE)], 4: [decay], 6: [lambda: p_out(hm, h, 3 * P)],
                    8: [lambda: squares(hm, h, M_DV, rden[:, 0])],
                    7: [lambda: evac("in_f", i, 0, z2, i * (2 * WH), WH, rstd2)],
                    10: [lambda: y_hi(hm, h, ps[4], 0, HEADS, 2, lambda e: gain[:, ds(h.num(2, G_M + e), 1)])],
                    15: [lambda: evac("in_f", i, 1, z2, i * (2 * WH) + WH, WH, rstd2)]}, WH)

            with act.Fori(0, 4) as i:
                steps = {}

                def then(u, f):
                    steps.setdefault(u, []).append(f)
                for j, (u_qk, u_s, u_p, u_v, u_y) in enumerate(FOX_UNITS):
                    h = Head(i, j, 2)

                    def qk_squares(h=h):
                        act.wait_ge(hf.ms, h.num(1, FREE))
                        for t in range(NT):
                            for c in range(2):
                                nc.scalar.activation(junk[:, (2 * t + c) * P:(2 * t + c + 1) * P], z2[:, t, ds(h.num(P, c * HALF), P)], ACT.Square,
                                                     accum_out=head_ss[:, 2 * t + c:2 * t + c + 1]).then_inc(hf.sq, 1)

                    def exps(h=h):
                        act.wait_ge(hf.raw_max, h.upto(2))
                        for t, c, n in ((0, 0, P), (1, P, S)):
                            nc.scalar.activation(prob[:, c:c + n], mix[:, c:c + n], ACT.Exp, bias=neg_max[:, 0, t:t + 1],
                                                 accum_out=den[:, 0, t:t + 1]).then_inc(hf.exps, 1)
                    then(FOX_SQ[j], qk_squares)
                    then(u_qk, lambda h=h: qk_out(hf, h, gain_qk[:, 1:2]))
                    then(u_s, exps)
                    then(u_p, lambda h=h: p_out(hf, h, 3 * P))
                    then(u_y, lambda h=h: y_hi(hf, h, ps[7], S, 0, 1, lambda e: 1.0))

                def gate_out():
                    act.wait_ge(by_dve, at(i, FREE + PH["gate_m"][BY_DVE], 2))
                    evac("gate_m", i, 0, gm_buf, 0, W, half_rstd2, ACT.Tanh, 12)
                then(7, gate_out)
                turn("gate_m", i, 12, steps)

            with act.Fori(0, 2) as i:
                turn("gate_a", i, 16, {
                    7: [lambda: evac("gate_a", i, 0, ga_buf, i * (2 * W), W, half_rstd2, ACT.Tanh)],
                    15: [lambda: evac("gate_a", i, 1, ga_buf, i * (2 * W) + W, W, half_rstd2, ACT.Tanh)]})
            residual("proj_a", 4, 3 * KT, xT_hi, None)
            residual("out2", 8, 4 * KT, yT_hi, G_NORM2, 2)
            ffn("ffn2", xT_hi, FF // W, True, None)

        @block.vector
        def _(dve):
            v = nc.vector

            def f32(t):
                return t.bitcast(F32)

            def split(n, i, step, width=W):
                dve.wait_ge(hi_ready, at(i, n + 1, step))
                v.tensor_tensor(w_lo[n % NS][:, :, 0:width], raw[n % NS][:, :, 0:width], f32(w_hi[n % NS][:, :, 0:width]),
                                ALU.subtract).then_inc(lo_ready, 1)

            def turn(name, i, units, steps={}, width=W, ahead=True):
                for u in range(units):
                    if ahead or u + NS < units:
                        split(PH[name][0] + NS + u, i, units, width if u + NS < units else W)
                    for step in steps.get(u, ()):
                        step()

            dve.wait_ge(rows_T, 1)
            v.tensor_copy(gain[:, 0:5 * KT], ps[0][:, 0:5 * KT]).then_inc(gain_ready, 1)
            dve.wait_ge(gain_ready, 1)
            v.tensor_tensor(gain[:, G_NORM1:G_NORM1 + KT], gain[:, G_NORM1:G_NORM1 + KT], gain[:, G_FINAL:G_FINAL + KT],
                            ALU.mult).then_inc(gain_step, 1)
            for kt in range(KT):
                dve.wait_ge(kt_hi, kt // 2 * 2 + 2)
                c = slice(kt * S, (kt + 1) * S)
                v.scalar_tensor_tensor(xT_lo[:, c], ps[START_BANKS[kt // 2]][:, kt % 2 * S:(kt % 2 + 1) * S],
                                       gain[:, G_ATTN + kt:G_ATTN + kt + 1], f32(xT_hi[:, c]), ALU.mult, ALU.subtract).then_inc(kt_lo, 1)
                if kt % 4 == 3:
                    split(kt // 4, None, 0)
            with dve.Fori(0, 3) as i:
                turn("in_b", i, 16)

            dve.wait_ge(small_landed, 16 * N_SMALL)
            v.tensor_tensor(lam_prod, lam_in[:, 0:4:2, :], lam_in[:, 1:4:2, :], ALU.mult).then_inc(lam_step, 1)
            dve.wait_ge(rows_T, 2)
            v.tensor_copy(gain[:, G_SUBLN:N_GAIN], ps[4][:, 0:N_GAIN - G_SUBLN]).then_inc(gain_ready, 1)
            dve.wait_ge(rows_T, 3)
            v.tensor_copy(conv[:], ps[5][:, 0:4 * CONV_T]).then_inc(gain_ready, 1)
            dve.wait_ge(lam_step, 1)
            v.tensor_reduce(lam_t[:, 0:2], lam_prod, X, ALU.add).then_inc(lam_step, 1)
            dve.wait_ge(gain_ready, 3)
            v.tensor_scalar(gain[:, G_SUBLN:G_SUBLN + 1], gain[:, G_SUBLN:G_SUBLN + 1], 1.0 - LAM_INIT, None, ALU.mult).then_inc(gain_step, 1)
            v.tensor_tensor(gain_qk[:, 0:1], gain[:, G_Q:G_Q + 1], gain[:, G_K:G_K + 1], ALU.mult).then_inc(gain_step, 1)
            v.tensor_scalar(gain[:, G_M:N_GAIN], gain[:, G_M:N_GAIN], 0.5, None, ALU.mult).then_inc(gain_step, 1)
            dve.wait_ge(gain_step, 4)
            v.tensor_scalar(gain_qk[:, 1:2], gain_qk[:, 0:1], P * HEAD_SCALE, None, ALU.mult).then_inc(gain_step, 1)
            dve.wait_ge(lam_exp, 1)
            v.tensor_tensor(lam_t[:, 4:5], lam_t[:, 3:4], lam_t[:, 2:3], ALU.subtract).then_inc(lam_step, 1)
            dve.wait_ge(lam_step, 3)
            v.tensor_scalar(minus_lam[:], lam_t[:, 4:5], -LAM_INIT, None, ALU.add).then_inc(lam_ready, 1)
            dve.wait_ge(lam_ready, 1)
            dve.wait_ge(gain_step, 5)

            def y_out(s, h, width, scale):
                for t in range(NT):
                    v.tensor_scalar(y[:, t, 0:width], ps[7][:, t * width:(t + 1) * width], scale[:, t:t + 1], None, ALU.mult).then_inc(s.y, 1)

            def y_lo(s, h, bank, c0, tile0, tiles, scale):
                dve.wait_ge(s.y_hi, h.upto(tiles))
                for e in range(tiles):
                    c = ds(h.num(tiles * S, (tile0 + e) * S), S)
                    v.scalar_tensor_tensor(yT_lo[:, c], bank[:, c0 + e * S:c0 + (e + 1) * S], scale(e), f32(yT_hi[:, c]),
                                           ALU.mult, ALU.subtract).then_inc(s.y_lo, 1)

            with dve.Fori(0, 4) as i:
                steps = {}
                for g in range(2):
                    h = Head(i, g, 2)

                    def maxima(h=h):
                        for c in range(2):
                            dve.wait_ge(hb.scores, h.upto(2, c + 1))
                            v.tensor_reduce(neg_max[:, :, c], ps[5 + c][:, :].rearrange("p (t s) -> p t s", t=NT), X, ALU.max,
                                            negate=True).then_inc(hb.row_max, 1)

                    def mix_parts(h=h):
                        dve.wait_ge(hb.exps, h.upto(4))
                        v.reciprocal(rden[:], den[:]).then_inc(hb.rden, 1)
                        dve.wait_ge(hb.rden, h.upto())
                        v.scalar_tensor_tensor(coef[:], rden[:, 1, :], minus_lam[:], den[:, 0, :], ALU.mult, ALU.mult).then_inc(hb.coef, 1)
                        dve.wait_ge(hb.coef, h.upto(2, 1))
                        for t in range(NT):
                            c0, c1 = (prob[:, (2 * t + c) * S:(2 * t + c + 1) * S] for c in range(2))
                            v.scalar_tensor_tensor(mix[:, t * S:(t + 1) * S], c1, coef[:, t:t + 1], c0, ALU.mult, ALU.add).then_inc(hb.mixed, 1)

                    def result(h=h):
                        dve.wait_ge(hb.rstd, h.upto())
                        v.scalar_tensor_tensor(coef[:], rden[:, 0, :], P ** 0.5, head_rstd[:, 0:NT], ALU.mult, ALU.mult).then_inc(hb.coef, 1)
                        dve.wait_ge(hb.coef, h.upto(2))
                        y_out(hb, h, P, coef)
                    steps.update({8 * g + 1: [maxima], 8 * g + 2: [mix_parts], 8 * g + 5: [result],
                                  8 * g + 6: [lambda h=h: y_lo(hb, h, ps[7], S, HEADS, 1, lambda e: gain[:, G_SUBLN:G_SUBLN + 1])]})
                turn("in_a", i, 16, steps, WH)

            def add_in_place(name, i, g, units):
                dve.wait_ge(*multiplied(name, i, units * (g + 1), 2 * units))
                for t in range(NT):
                    c = ds(at(i, g * W, 2 * W), W)
                    v.tensor_tensor(x[:, t, c], x[:, t, c], pair[g][t][:], ALU.add).then_inc(by_dve, 1)

            with dve.Fori(0, 2) as i:
                steps = {}
                for j in range(4):
                    h = Head(i, j, 4)

                    def masked_max(h=h):
                        dve.wait_ge(ha.scores, h.upto())
                        v.scalar_tensor_tensor(mix[:], ps[5][:], HEAD_SCALE, ln_count[:], ALU.mult, ALU.add).then_inc(ha.masked, 1)
                        dve.wait_ge(ha.masked, h.upto())
                        v.tensor_reduce(neg_max[:, 0, :], mix[:].rearrange("p (t s) -> p t s", t=NT), X, ALU.max,
                                        negate=True).then_inc(ha.row_max, 1)

                    def result(h=h):
                        dve.wait_ge(ha.exps, h.upto(2))
                        v.reciprocal(rden[:, 0, :], den[:, 0, :]).then_inc(ha.rden, 1)
                        dve.wait_ge(ha.rden, h.upto())
                        dve.wait_ge(ha.pv, h.upto())
                        y_out(ha, h, P, rden[:, 0])
                    steps[2 * j] = [masked_max]
                    steps[2 * j + 1] = [result, lambda h=h: y_lo(ha, h, ps[7], S, 0, 1, lambda e: 1.0)]
                steps[3].append(lambda: add_in_place("out_b", i, 0, 4))
                steps[7].append(lambda: add_in_place("out_b", i, 1, 4))
                turn("out_b", i, 8, steps)

            def add_fresh(name, i, g, e, units):
                dve.wait_ge(*multiplied(name, i, units * (g + 1), 2 * units))
                dve.wait_ge(x_kept, at(i, FREE + 4 * e, 2))
                dve.wait_ge(part_sq, at(i, FREE + 8 * e, 4))
                for t in range(NT):
                    v.tensor_tensor(fresh[g][:, t, :], x[:, t, ds(at(i, g * W, 2 * W), W)], pair[g][t][:], ALU.add).then_inc(by_dve, 1)

            def x_lo(i, g, base, hi, lo, gain0):
                for j in range(4):
                    dve.wait_ge(kt_hi, at(i, base + 4 * g + j // 2 * 2 + 2, 8))
                    c = ds(at(i, (4 * g + j) * S, 8 * S), S)
                    scale = 0.5 if gain0 is None else gain[:, ds(at(i, gain0 + 4 * g + j, 8), 1)]
                    v.scalar_tensor_tensor(lo[:, c], ps[4 + 2 * g + j // 2][:, j % 2 * S:(j % 2 + 1) * S], scale, f32(hi[:, c]),
                                           ALU.mult, ALU.subtract).then_inc(kt_lo, 1)

            def residual(name, units, base, hi, lo, gain0, add):
                with dve.Fori(0, 2) as i:
                    turn(name, i, 2 * units, {
                        units - 1: [lambda: add(i, 0)], units + 1: [lambda: x_lo(i, 0, base, hi, lo, gain0)],
                        2 * units - 1: [lambda: add(i, 1), lambda: x_lo(i, 1, base, hi, lo, gain0)]})

            def sum_squares(e):
                dve.wait_ge(part_sq, FREE + 8 * (e + 1))
                v.tensor_reduce(ss[:], part_ss[:], X, ALU.add).then_inc(ss_ready, 1)

            residual("out_a", 4, KT, xT_hi, xT_lo, G_FFN, lambda i, g: add_fresh("out_a", i, g, 0, 4))
            sum_squares(0)

            def rstd_diag(n):
                dve.wait_ge(rstd_ready, n)
                for t in range(NT):
                    v.tensor_scalar(diag[:, t, :], ident[:], rstd[:, t:t + 1], None, ALU.mult).then_inc(r_diag, 1)

            def ffn(name, hi, lo, fg0, conv_too, n_norm, n_rstd, last):
                rstd_diag(n_rstd)
                r_both = r_bc.unsqueeze(1).to_broadcast([P, 2, S])

                def copy_r():
                    dve.wait_ge(r_bc_T, n_norm)
                    v.tensor_copy(r_bc, ps[4][:, 0:S]).then_inc(r_bc_ready, 1)
                    dve.wait_ge(r_bc_ready, n_norm)
                for t, width in enumerate(THIRDS):
                    up, down, n_fg, units = f"{name}_up{t}", f"{name}_down{t}", width // W, width // (UK * P)
                    f0 = fg0 - (FF // W if conv_too else 0)

                    def scaled(i, g, dst, factor):
                        dve.wait_ge(*multiplied(up, i, 8 * (g + 1), 16))
                        for b in range(2):
                            o = dst[:, 2 * b:2 * b + 2, PAD:PAD + S] if conv_too else dst[:, 2 * b:2 * b + 2, :]
                            v.tensor_tensor(o, pair[g][b][:].rearrange("p (f s) -> p f s", f=2), factor(b), ALU.mult).then_inc(by_dve, 1)

                    def convolve(i, g, u, z):
                        dve.wait_ge(by_dve, at(i, FREE + PH[up][BY_DVE] + 2 * g + 2, 4))
                        n = 24 * f0 + 12 * g
                        for j, tap in enumerate((2, 1, 0)):
                            for f in range(4):
                                col = at(i, 4 * f0 + f + g * (CONV_T // 2), 4)
                                w = conv[:, ds(col + tap * CONV_T, 1)]
                                if j == 0:
                                    v.tensor_scalar(z[:, f, :], u[:, f, PAD:PAD + S], w, conv[:, ds(col + 3 * CONV_T, 1)],
                                                    ALU.mult, ALU.add).then_inc(conv_step, 1)
                                else:
                                    dve.wait_ge(conv_step, at(i, n + 4 * (j - 1) + f + 1, 24))
                                    v.scalar_tensor_tensor(z[:, f, :], u[:, f, tap:tap + S], w, z[:, f, :], ALU.mult, ALU.add).then_inc(conv_step, 1)

                    def gate(i):
                        if conv_too:
                            scaled(i, 0, gate_u, lambda b: r_both)
                            convolve(i, 0, gate_u, gate_z)
                        else:
                            scaled(i, 0, gate_z, lambda b: r_both)

                    def silu(i):
                        dve.wait_ge(tanh_ready, at(i, fg0 + 1, 1))
                        v.scalar_tensor_tensor(gate_z, tanh_z, 1.0, gate_z, ALU.add, ALU.mult).then_inc(silu_step, 1)
                        dve.wait_ge(silu_step, at(i, 2 * fg0 + 1, 2))
                        if not conv_too:
                            r4 = r_bc.unsqueeze(1).to_broadcast([P, 4, S])
                            v.tensor_tensor(gate_z, gate_z, r4, ALU.mult).then_inc(silu_step, 1)
                            dve.wait_ge(silu_step, at(i, 2 * fg0 + 2, 2))

                    def up_part(i):
                        if conv_too:
                            scaled(i, 1, up_u, lambda b: r_both)
                            convolve(i, 1, up_u, up_z)
                            dve.wait_ge(conv_step, at(i, 24 * f0 + 24, 24))
                            v.tensor_tensor(up_z, up_z, gate_z, ALU.mult).then_inc(silu_step, 1)
                        else:
                            scaled(i, 1, up_z, lambda b: gate_z[:, 2 * b:2 * b + 2, :])
                            dve.wait_ge(by_dve, at(i, FREE + PH[up][BY_DVE] + 4, 4))
                        dve.wait_ge(act_hi, at(i, fg0 + 1, 1))
                        c = ds(at(i, 0, 4 * S), 4 * S)
                        v.scalar_tensor_tensor(tiles4(lo[:, c], S), up_z, 0.5, tiles4(f32(hi[:, c]), S), ALU.mult, ALU.subtract).then_inc(act_lo, 1)

                    def up_turn(i, more={}):
                        steps = {7: [lambda: gate(i)], 10 if conv_too else 9: [lambda: silu(i)], 15: [lambda: up_part(i)]}
                        turn(up, i, 16, {**steps, **more})
                    if t == 0:
                        up_turn(0, {4: [copy_r]})
                    with dve.Fori(1 if t == 0 else 0, n_fg) as i:
                        up_turn(i)
                    fg0 += n_fg
                    last(down, units) if t == 2 else plain(down, units)

            def plain(name, units):
                with dve.Fori(0, 2) as i:
                    turn(name, i, 2 * units, {units - 1: [lambda: add_in_place(name, i, 0, units)], 2 * units - 1: [lambda: add_in_place(name, i, 1, units)]})

            dve.wait_ge(x_kept, FREE + 4)
            ffn("ffn1", yT_hi, yT_lo, 0, False, 1, 2,
                lambda name, units: residual(name, units, 2 * KT, xT_hi, xT_lo, G_NORM1, lambda i, g: add_fresh(name, i, g, 1, units)))

            sum_squares(1)
            dve.wait_ge(gate_hi, 1)
            v.tensor_tensor(gate_w_lo[:], gate_w[:], f32(gate_w_hi[:]), ALU.subtract).then_inc(gate_lo, 1)
            dve.wait_ge(x_kept, FREE + 8)
            dve.wait_ge(final_landed, 16)
            dve.wait_ge(rstd_ready, 3)
            for t in range(NT):
                v.scalar_tensor_tensor(x[:, t, :], x[:, t, :], rstd[:, t:t + 1], gain_final_bc, ALU.mult, ALU.mult).then_inc(x2_ready, 1)
            with dve.Fori(0, 2) as i:
                turn("in_m", i, 16)

            F_COLS, I_COL, MF_COL = HEADS, HEADS, HEADS + M_HEADS

            def gates_bias():
                dve.wait_ge(gates_evac, 2)
                v.tensor_tensor(gz[:], gz[:], gate_bias[:].unsqueeze(1).to_broadcast([P, NT, NG]), ALU.add).then_inc(gates_step, 1)
                dve.wait_ge(gates_step, 1)
                v.scalar_tensor_tensor(gt[:], gz[:], -1.0, gz[:], ALU.mult, ALU.max).then_inc(gates_step, 1)

            def log_sigmoid():
                dve.wait_ge(gates_act, 2)
                v.scalar_tensor_tensor(lf[:], gz[:], 0.0, gt[:], ALU.min, ALU.subtract).then_inc(log_f, 1)

            def decays():
                dve.wait_ge(cum_done, 1)
                v.tensor_copy(f_sum[:], ps[5][:, 0:2 * NG].rearrange("p (t n) -> p t n", t=NT)).then_inc(cum_read, 1)
                dve.wait_ge(cum_read, 1)
                v.tensor_tensor(a_gate[:], gz[:, :, I_COL:I_COL + M_HEADS], f_sum[:, :, MF_COL:NG], ALU.subtract).then_inc(decay_ready, 1)
                dve.wait_ge(decay_ready, 1)
            turn("in_m", 2, 16, {0: [gates_bias], 2: [log_sigmoid], 5: [decays]})

            with dve.Fori(0, 4) as i:
                h = Head(i, 0, 1)

                def decay_diag():
                    for t in range(NT):
                        v.tensor_scalar(diag[:, t, :], ident[:], a_gate[:, t, ds(h.num(), 1)], None, ALU.mult).then_inc(diag_ready, 1)

                def decay_max():
                    dve.wait_ge(decay_bc, h.upto())
                    for t, c, n in ((0, 0, P), (1, P, S)):
                        v.tensor_tensor(mix[:, c:c + n], ps[5][:, 0:n], causal[:, c:c + n], ALU.add).then_inc(hm.masked, 1)
                    for t, c, n in ((0, 0, P), (1, P, S)):
                        dve.wait_ge(hm.masked, h.upto(2, t + 1))
                        v.tensor_reduce(top[:, t:t + 1], mix[:, c:c + n], X, ALU.max).then_inc(hm.raw_max, 1)
                    dve.wait_ge(hm.raw_max, h.upto(2))
                    v.tensor_scalar(neg_max[:, 0, :], top[:], 0.0, -1.0, ALU.max, ALU.mult).then_inc(hm.row_max, 1)

                def weigh():
                    dve.wait_ge(hm.exps, h.upto(2))
                    dve.wait_ge(hm.scores, h.upto())
                    for t, c, n in ((0, 0, P), (1, P, S)):
                        v.tensor_tensor_reduce(out=mix[:, c:c + n], in0=ps[6][:, c:c + n], in1=prob[:, c:c + n], scale=1.0, scalar=0.0,
                                               op0=ALU.mult, op1=ALU.add, accum_out=den[:, 0, t:t + 1]).then_inc(hm.mixed, 1)
                    dve.wait_ge(hm.mixed, h.upto(2))
                    dve.wait_ge(floor_ready, h.upto(2))
                    v.scalar_tensor_tensor(den[:, 1, :], den[:, 0, :], -1.0, den[:, 0, :], ALU.mult, ALU.max).then_inc(den_part, 1)
                    dve.wait_ge(den_part, h.upto(2, 1))
                    v.tensor_tensor(den[:, 0, :], den[:, 1, :], floor[:], ALU.max).then_inc(den_part, 1)
                    dve.wait_ge(den_part, h.upto(2))
                    v.reciprocal(rden[:, 0, :], den[:, 0, :]).then_inc(hm.rden, 1)

                def result():
                    dve.wait_ge(hm.rstd, h.upto())
                    v.scalar_tensor_tensor(coef[:], rden[:, 0, :], M_DV ** 0.5, head_rstd[:, 0:NT], ALU.mult, ALU.mult).then_inc(hm.coef, 1)
                    dve.wait_ge(hm.coef, h.upto())
                    for t in range(NT):
                        v.tensor_scalar(h_norm[:, t, :], ps[7][:, t * M_DV:(t + 1) * M_DV], coef[:, t:t + 1], None, ALU.mult).then_inc(norm_step, 1)
                    for t in range(NT):
                        dve.wait_ge(norm_step, h.upto(2, t + 1))
                        v.scalar_tensor_tensor(y[:, t, :], z1[:, t, ds(h.num(M_DV, D), M_DV)], 1.0, h_norm[:, t, :], ALU.add, ALU.mult).then_inc(hm.y, 1)
                turn("in_f", i, 16, {
                    0: [decay_diag], 3: [decay_max], 5: [weigh], 9: [result],
                    10: [lambda: y_lo(hm, h, ps[4], 0, HEADS, 2, lambda e: gain[:, ds(h.num(2, G_M + e), 1)])]}, WH)

            with dve.Fori(0, 4) as i:
                steps = {}

                def then(u, f):
                    steps.setdefault(u, []).append(f)
                for j, (u_qk, u_s, u_p, u_v, u_y) in enumerate(FOX_UNITS):
                    h = Head(i, j, 2)

                    def forget_diag(h=h):
                        for t in range(NT):
                            v.tensor_scalar(diag[:, t, :], ident[:], f_sum[:, t, ds(h.num(), 1)], -1.0, ALU.mult, ALU.mult).then_inc(diag_ready, 1)

                    def masked_max(h=h):
                        dve.wait_ge(hf.scores, h.upto())
                        for t, c, n in ((0, 0, P), (1, P, S)):
                            v.scalar_tensor_tensor(mix[:, c:c + n], ps[6][:, c:c + n], f_sum[:, t, ds(h.num(), 1)], causal[:, c:c + n],
                                                   ALU.add, ALU.add).then_inc(hf.masked, 1)
                        for t, c, n in ((0, 0, P), (1, P, S)):
                            dve.wait_ge(hf.masked, h.upto(2, t + 1))
                            v.tensor_reduce(neg_max[:, 0, t:t + 1], mix[:, c:c + n], X, ALU.max, negate=True).then_inc(hf.raw_max, 1)

                    def result(h=h):
                        dve.wait_ge(hf.exps, h.upto(2))
                        v.reciprocal(rden[:, 0, :], den[:, 0, :]).then_inc(hf.rden, 1)
                        dve.wait_ge(hf.rden, h.upto())
                        dve.wait_ge(hf.pv, h.upto())
                        y_out(hf, h, P, rden[:, 0])
                    then(FOX_SQ[j], forget_diag)
                    then(u_s, masked_max)
                    then(u_v, result)
                    then(u_y, lambda h=h: y_lo(hf, h, ps[7], S, 0, 1, lambda e: 1.0))

                def merge_m():
                    dve.wait_ge(*multiplied("gate_m", i, 12, 12))
                    dve.wait_ge(by_act, at(i, FREE + PH["gate_m"][BY_ACT] + 2, 2))
                    for t in range(NT):
                        v.scalar_tensor_tensor(merged[:, t, ds(i * W, W)], gm_buf[:, t, :], 1.0, pair[1][t][:], ALU.add, ALU.mult).then_inc(by_dve, 1)
                then(11, merge_m)
                turn("gate_m", i, 12, steps)

            with dve.Fori(0, 2) as i:
                turn("gate_a", i, 16)

            def merge_a(i, g):
                dve.wait_ge(*multiplied("proj_a", i, 4 * (g + 1), 8))
                for t in range(NT):
                    c = ds(at(i, g * W, 2 * W), W)
                    v.scalar_tensor_tensor(fresh[g][:, t, :], ga_buf[:, t, c], 1.0, pair[g][t][:], ALU.add, ALU.mult).then_inc(by_dve, 1)
                for t in range(NT):
                    c = ds(at(i, g * W, 2 * W), W)
                    dve.wait_ge(by_dve, at(i, FREE + PH["proj_a"][BY_DVE] + 2 * g + t + 1, 4))
                    v.tensor_tensor(fresh[g][:, t, :], fresh[g][:, t, :], merged[:, t, c], ALU.add).then_inc(fresh_ready, 1)
            dve.wait_ge(by_act, FREE + PH["proj_a"][BY_ACT])
            residual("proj_a", 4, 3 * KT, xT_hi, xT_lo, None, merge_a)
            residual("out2", 8, 4 * KT, yT_hi, yT_lo, G_NORM2, lambda i, g: add_fresh("out2", i, g, 2, 8))
            sum_squares(2)
            for u in (gate_u, up_u):
                v.memset(u[:, :, 0:PAD], 0.0).then_inc(pad_set, 1)
            dve.wait_ge(pad_set, 2)
            dve.wait_ge(x_kept, FREE + 12)

            def last_groups(name, units):
                for i in range(2):
                    turn(name, i, 2 * units, {units - 1: [lambda: add_in_place(name, i, 0, units)], 2 * units - 1: [lambda: add_in_place(name, i, 1, units)]},
                         ahead=i == 0)
            ffn("ffn2", xT_hi, xT_lo, FF // W, True, 2, 5, last_groups)

        @block.gpsimd
        def _(pool):
            g_ = nc.gpsimd
            g_.memset(ones[:], 1.0).then_inc(const_set, 1)
            g_.memset(minus_half[:], -0.5).then_inc(const_set, 1)
            for dst, eps in ((eps_diff, P * SUBLN_EPS), (eps_mlstm, M_DV * RMS_EPS), (eps_fox, P * RMS_EPS)):
                g_.memset(dst[:], eps).then_inc(const_set, 1)
            pool.sem_inc(lo_ready, NS)
            pool.sem_inc(slot_used, NS)
            for s in (by_act, by_dve, part_sq, x_kept, *(k for h in (hb, ha, hm, hf) for k in (h.qk_T, h.ms, h.y_lo))):
                pool.sem_inc(s, FREE)
            pool.wait_ge(const_set, 5)

            def factor(n, dst):
                g_.tensor_scalar(ms[:], ss[:], 1.0 / D, RMS_EPS, ALU.mult, ALU.add).then_inc(ms_ready, 1)
                pool.wait_ge(ms_ready, n)
                return g_.tensor_tensor(dst[:], ms[:], minus_half[:, 0:NT], ALU.pow)

            pool.wait_ge(x_sq, 2)
            factor(1, rstd).then_inc(rstd_ready, 1)

            def rope_head(s, h, z, table, heads4, rot):
                half = rot // 2
                pool.wait_ge(s.qk_T, h.num(1, FREE))
                src = z[:, :, :].rearrange("p t (c n) -> p t c n", c=3)[:, :, 0:2, ds(h.num(P), P)]
                g_.tensor_copy(stage[:], src).then_inc(s.rope, 1)
                pool.wait_ge(s.rope, h.upto(4, 1))
                r = stage[:].rearrange("p t c (e n) -> p (t c e) n", e=heads4)
                u = rot_u[:].rearrange("p (k n) -> p k n", n=rot)
                w = rot_v[:].rearrange("p (k n) -> p k n", n=rot)
                g_.tensor_tensor(u, r[:, :, 0:rot], table[:, 0], ALU.mult).then_inc(s.rope, 1)
                g_.tensor_tensor(w[:, :, 0:half], r[:, :, half:rot], table[:, 1, :, 0:half], ALU.mult).then_inc(s.rope, 1)
                g_.tensor_tensor(w[:, :, half:rot], r[:, :, 0:half], table[:, 1, :, half:rot], ALU.mult).then_inc(s.rope, 1)
                pool.wait_ge(s.rope, h.upto(4))
                g_.tensor_tensor(r[:, :, 0:rot], u, w, ALU.add).then_inc(s.staged, 1)

            def head_factor(s, h, n, sq, eps):
                pool.wait_ge(s.sq, h.upto(sq))
                g_.tensor_tensor(head_ms[:, 0:n], head_ss[:, 0:n], eps[:, 0:n], ALU.add).then_inc(s.ms, 1)
                pool.wait_ge(s.ms, h.num(1, FREE + 1))
                g_.tensor_tensor(head_rstd[:, 0:n], head_ms[:, 0:n], minus_half[:, 0:n], ALU.pow).then_inc(s.rstd, 1)

            pool.wait_ge(small_landed, 16 * N_SMALL)
            pool.wait_ge(by_act, FREE + PH["in_a"][BY_ACT])
            with pool.Fori(0, 8) as i:
                h = Head(i, 0, 1)
                rope_head(hb, h, z1, rope_b, 2, 16)
                head_factor(hb, h, NT, 2, eps_diff)
            pool.wait_ge(hb.qk_T, FREE + HEADS)
            pool.wait_ge(by_act, FREE + PH["out_b"][BY_ACT])
            with pool.Fori(0, 8) as i:
                rope_head(ha, Head(i, 0, 1), z2, rope_a, 1, 32)

            def keep(name):
                with pool.Fori(0, 2) as i:
                    for g in range(2):
                        pool.wait_ge(by_dve, at(i, FREE + PH[name][BY_DVE] + 2 * g + 2, 4))
                        g_.tensor_copy(x[:, :, ds(i * (2 * W) + g * W, W)], fresh[g]).then_inc(x_kept, 1)
            keep("out_a")
            pool.wait_ge(ss_ready, 1)
            factor(2, rstd).then_inc(rstd_ready, 1)
            keep("ffn1_down2")
            pool.wait_ge(ss_ready, 2)
            factor(3, rstd).then_inc(rstd_ready, 1)

            pool.wait_ge(x_sq, 4)
            factor(4, rstd_n).then_inc(norm1_step, 1)
            pool.wait_ge(norm1_step, 1)
            g_.tensor_tensor(rstd2[:], rstd[:], rstd_n[:], ALU.mult).then_inc(norm1_step, 1)
            pool.wait_ge(norm1_step, 2)
            g_.tensor_scalar(half_rstd2[:], rstd2[:], 0.5, None, ALU.mult).then_inc(rstd_ready, 1)
            pool.wait_ge(by_act, FREE + PH["in_f"][BY_ACT])
            pool.wait_ge(ha.qk_T, FREE + HEADS)
            with pool.Fori(0, 4) as i:
                h = Head(i, 0, 1)
                pool.wait_ge(hm.qk_T, h.num(1, FREE))
                src = z1[:, :, 0:2 * M_HEADS * P].rearrange("p t (c n) -> p t c n", c=2)[:, :, :, ds(h.num(P), P)]
                g_.tensor_copy(stage[:], src).then_inc(hm.staged, 1)
                head_factor(hm, h, NT, 2, eps_mlstm)
            pool.wait_ge(hm.qk_T, FREE + M_HEADS)
            with pool.Fori(0, 8) as i:
                h = Head(i, 0, 1)
                head_factor(hf, h, 4, 4, eps_fox)
                pool.wait_ge(hf.rstd, h.upto())
                pool.wait_ge(hf.qk_T, h.num(1, FREE))
                z = z2[:, :, :].rearrange("p t (c n) -> p t c n", c=3)[:, :, 0:2, ds(h.num(P), P)]
                r = head_rstd[:].rearrange("p (t c) -> p t c", t=NT).unsqueeze(3).to_broadcast([P, NT, 2, P])
                g_.tensor_tensor(stage[:], z, r, ALU.mult).then_inc(hf.staged, 1)
            keep("out2")
            pool.wait_ge(ss_ready, 3)
            factor(5, rstd).then_inc(rstd_ready, 1)


_INS = ['x', 'norm_attn', 'w_in', 'lambda_qk', 'subln', 'w_out', 'norm_ffn', 'w_gate', 'w_up', 'w_down', 'norm_final',
        'norm1_g_2', 'w_in_2', 'fox_f_bias_2', 'q_norm_g_2', 'k_norm_g_2', 'm_i_bias_2', 'm_f_bias_2', 'm_norm_g_2',
        'w_proj_a_2', 'w_proj_m_2', 'w_out_2', 'norm2_g_2', 'w_up_2', 'conv_w_2', 'conv_b_2', 'w_down_2']


def _tables():
    import numpy as np
    f = np.float32
    tok = np.arange(S)
    far = f(-1e30)
    dist = tok[:, None] - tok[None, :]
    count = (np.abs(dist) <= 64).astype(f) + (dist % 4 == 0) + (dist % 16 == 0)
    log_count = np.where(count > 0, np.log(np.maximum(count, 1)), far).astype(f)
    mask = np.where(dist >= 0, f(0), far).astype(f)

    def by_tile(m):
        return m.reshape(NT, P, -1).transpose(1, 0, 2)

    def rope(rot, copies):
        inv = np.power(f(500000.0), -np.arange(0, rot, 2, dtype=f) / f(rot), dtype=f)
        ang = tok.astype(f)[:, None] * inv[None, :]
        c, s = np.cos(ang), np.sin(ang)
        both = [np.concatenate([c, c], 1), np.concatenate([-s, s], 1)]
        return np.stack([np.repeat(by_tile(b)[:, :, None], copies, 2).reshape(P, NT * copies, rot) for b in both], 1).astype(f)

    return {
        "c_ident": np.eye(P, dtype=f),
        "c_tri": np.triu(np.ones((P, P), f)),
        "c_causal": np.ascontiguousarray(np.concatenate([mask[:P, :P], mask[P:, :]], 1)),
        "c_count": np.ascontiguousarray(by_tile(log_count)),
        "c_rope_a": np.ascontiguousarray(rope(32, 2)),
        "c_rope_b": np.ascontiguousarray(rope(16, 4)),
    }


def kernel(**inputs):
    import numpy as np
    import concourse.bacc as bacc
    from concourse.bass_utils import run_bass_kernel_spmd

    nc = bacc.Bacc("TRN2", target_bir_lowering=False, num_devices=1)
    arrays = {f"in_{name}": np.ascontiguousarray(inputs[name]) for name in _INS}
    arrays.update(_tables())
    aps = {}
    for name, v in arrays.items():
        aps[name.removeprefix("in_")] = nc.dram_tensor(name, v.shape, mybir.dt.from_np(v.dtype), kind="ExternalInput").ap()
    out = nc.dram_tensor("out_x", (1, S, D), F32, kind="ExternalOutput").ap()
    two_blocks(nc, aps, out)
    r = run_bass_kernel_spmd(nc, [arrays], core_ids=[0])
    return r.results[0]["out_x"]
```

```python
from contextlib import ExitStack
import math

import concourse.bass as bass
from concourse import mybir

F32 = mybir.dt.float32
F32R = mybir.dt.float32r
ALU = mybir.AluOpType
ACT = mybir.ActivationFunctionType
X = mybir.AxisListType.X

P = 128
D = 2048
S = 256
NT = S // P
KT = D // P
HEADS = 8
M_HEADS = 4
M_DV = 256
HALF = HEADS * P
FF = 5632
RMS_EPS = 1e-6
SUBLN_EPS = 1e-5
LAM_INIT = 0.8 - 0.6 * math.exp(-0.3 * 0)
B_SCALE = 64 ** -0.5
HEAD_SCALE = 128 ** -0.5

UK = 2
W = 512
NS = 4
WH = 384
C3 = 3 * HALF
THIRDS = (2048, 2048, FF - 4096)

OFF_GATES_F = C3
OFF_M = OFF_GATES_F + HEADS
OFF_GATES_IF = OFF_M + C3
OFF_GA = OFF_GATES_IF + 2 * M_HEADS
OFF_GM = OFF_GA + D
NG = HEADS + 2 * M_HEADS

G_ATTN, G_FFN, G_FINAL, G_NORM1, G_NORM2 = (KT * j for j in range(5))
G_SUBLN, G_Q, G_K, G_M = 5 * KT, 5 * KT + 1, 5 * KT + 2, 5 * KT + 3
N_GAIN = G_M + 2 * M_HEADS
CONV_T = 2 * FF // P


def plan():
    phases, unit, group, by_act, by_dve = {}, 0, 0, 0, 0

    def add(name, units, groups, act, dve):
        nonlocal unit, group, by_act, by_dve
        phases[name] = (unit, group, by_act, by_dve)
        unit, group, by_act, by_dve = unit + units, group + groups, by_act + act, by_dve + dve

    def ffn(name):
        for t, width in enumerate(THIRDS):
            n = width // W
            add(f"{name}_up{t}", 16 * n, 2 * n, 0, 4 * n)
            add(f"{name}_down{t}", 4 * (width // (UK * P)), 4, 0, 8)

    add("in_b", 64, 8, 16, 0)
    add("in_a", 64, 8, 16, 0)
    add("out_b", 16, 4, 0, 8)
    add("out_a", 16, 4, 0, 8)
    ffn("ffn1")
    add("in_m", 48, 6, 12, 0)
    add("in_f", 64, 8, 16, 0)
    add("gate_m", 48, 8, 8, 8)
    add("gate_a", 32, 4, 8, 0)
    add("proj_a", 16, 4, 0, 8)
    add("out2", 32, 4, 0, 8)
    ffn("ffn2")
    add("end", 0, 0, 0, 0)
    return phases


PH = plan()
HEAD_STEPS = (0, 1, 4, 5, 8)
LAST_DIL_STEPS = (1, 2, 4, 5, 7)
MLSTM_STEPS = (1, 3, 7, 8, 12)
FOX_M_STEPS, FOX_A_STEPS = (2, 3, 6, 7, 9), (2, 3, 5, 6, 7)
N_SPLIT = PH["out_b"][0] + NS
N_CONST = 5 + NS
N_SMALL = 21
X_BEHIND = (0, 2, 3)
START_BANKS = (4, 5, 6, 7, 2, 3, 4, 5)
FREE = 3


def at(i, c, step):
    return c if i is None else i * step + c


class Head:

    def __init__(self, i, first, per):
        self.i, self.first, self.per = i, first, per

    def num(self, scale=1, c=0):
        return at(self.i, self.first * scale + c, self.per * scale)

    def upto(self, n=1, k=None):
        return self.num(n, n if k is None else k)


class HeadSems:

    def __init__(self, sem, kind):
        self.staged = sem(kind + "_staged")
        self.rope = sem(kind + "_rope")
        self.qk_T = sem(kind + "_qk_T")
        self.qkT = sem(kind + "_qkT")
        self.scores = sem(kind + "_scores")
        self.masked = sem(kind + "_masked")
        self.raw_max = sem(kind + "_raw_max")
        self.row_max = sem(kind + "_row_max")
        self.exps = sem(kind + "_exps")
        self.rden = sem(kind + "_rden")
        self.coef = sem(kind + "_coef")
        self.mixed = sem(kind + "_mixed")
        self.p_T = sem(kind + "_p_T")
        self.pT = sem(kind + "_pT")
        self.pv = sem(kind + "_pv")
        self.sq = sem(kind + "_sq")
        self.ms = sem(kind + "_ms")
        self.rstd = sem(kind + "_rstd")
        self.y = sem(kind + "_y")
        self.y_T = sem(kind + "_y_T")
        self.y_hi = sem(kind + "_y_hi")
        self.y_lo = sem(kind + "_y_lo")


def two_blocks(nc, a, out):
    ctx = ExitStack()
    with ctx:
        def sb(name, shape, dt=F32):
            return ctx.enter_context(nc.sbuf_tensor(name, [P, *shape], dt))

        def sem(name):
            return ctx.enter_context(nc.semaphore(name))

        x = sb("x", [NT, D])
        xT_hi, xT_lo = sb("xT_hi", [KT * S], F32R), sb("xT_lo", [KT * S], F32R)
        yT_hi, yT_lo = sb("yT_hi", [KT * S], F32R), sb("yT_lo", [KT * S], F32R)
        raw = [sb(f"raw{j}", [UK, W]) for j in range(NS)]
        w_hi = [sb(f"w_hi{j}", [UK, W], F32R) for j in range(NS)]
        w_lo = [sb(f"w_lo{j}", [UK, W], F32R) for j in range(NS)]
        z1, z2 = sb("z1", [NT, C3]), sb("z2", [NT, C3])
        ident, tri, ones = sb("ident", [P]), sb("tri", [P]), sb("ones", [P])
        causal = sb("causal", [3 * P])
        ln_count = sb("ln_count", [NT * S])
        rope_a = sb("rope_a", [2, NT * 2, 32])
        rope_b = sb("rope_b", [2, NT * 4, 16])
        gain = sb("gain", [N_GAIN])
        gain_qk = sb("gain_qk", [2])
        conv = sb("conv", [4 * CONV_T])
        gate_w = sb("gate_w", [KT, NG])
        gate_w_hi, gate_w_lo = sb("gate_w_hi", [KT, NG], F32R), sb("gate_w_lo", [KT, NG], F32R)
        gate_bias = sb("gate_bias", [NG])
        lam_t, minus_lam = sb("lam_t", [8]), sb("minus_lam", [1])
        minus_half = sb("minus_half", [NG])
        stage = sb("stage", [NT, 2, P])
        rot_u, rot_v = sb("rot_u", [P]), sb("rot_v", [P])
        qkT = sb("qkT", [2, S])
        prob = sb("prob", [NT * 2 * S])
        mix = sb("mix", [NT * S])
        pT = sb("pT", [2 * S])
        y = sb("y", [NT, S])
        junk = sb("junk", [W])
        neg_max, top = sb("neg_max", [NT, 2]), sb("top", [NT])
        den, rden = sb("den", [2, NT]), sb("rden", [2, NT])
        coef, floor = sb("coef", [NT]), sb("floor", [NT])
        head_ss, head_ms, head_rstd = sb("head_ss", [4]), sb("head_ms", [4]), sb("head_rstd", [4])
        eps_diff, eps_mlstm, eps_fox = (sb(n, [4]) for n in ("eps_diff", "eps_mlstm", "eps_fox"))
        part_ss = sb("part_ss", [NT, 4])
        ss, ms = sb("ss", [NT]), sb("ms", [NT])
        rstd, rstd_n, rstd2, half_rstd2 = sb("rstd", [NT]), sb("rstd_n", [NT]), sb("rstd2", [NT]), sb("half_rstd2", [NT])
        r_bc = prob[:, 0:S]
        diag = sb("diag", [NT, P])
        gz, lf, f_sum = sb("gz", [NT, NG]), sb("lf", [NT, NG]), sb("f_sum", [NT, NG])
        gt, a_gate = sb("gt", [NT, NG]), sb("a_gate", [NT, M_HEADS])
        gates_T = y[0:NG, 0, :]
        h_norm = prob[:, 2 * S:4 * S].rearrange("p (t n) -> p t n", t=NT)
        ps = [ctx.enter_context(nc.psum_tensor(f"ps{j}", [P, W], F32)) for j in range(8)]
        pair = (ps[0:2], ps[2:4])

        z1f, z2f = (z[:, :, :].rearrange("p t n -> p (t n)") for z in (z1, z2))
        PAD = 2

        def tiles4(v, n):
            return v.rearrange("p (f s) -> p f s", f=4, s=n)
        gate_u = tiles4(z1f[:, 0:4 * (S + PAD)], S + PAD)
        up_u = tiles4(z1f[:, 4 * (S + PAD):8 * (S + PAD)], S + PAD)
        gate_z = tiles4(z1f[:, 8 * (S + PAD):8 * (S + PAD) + 4 * S], S)
        up_z = tiles4(z2f[:, 0:4 * S], S)
        tanh_z = tiles4(z2f[:, 4 * S:8 * S], S)
        gain_final_bc = z2f[:, 8 * S:8 * S + D]
        fresh = [z2f[:, 2 * D + g * NT * W:2 * D + (g + 1) * NT * W].rearrange("p (t n) -> p t n", t=NT) for g in range(2)]
        merged = z1f[:, 0:NT * D].rearrange("p (t n) -> p t n", t=NT)
        gm_buf = z1f[:, NT * D:NT * (D + W)].rearrange("p (t n) -> p t n", t=NT)
        ga_buf = [[z2[:, 0, 0:W], z2[:, 1, 0:W]], [z2[:, 0, HALF:HALF + W], z2[:, 0, 2 * HALF:2 * HALF + W]],
                  [z1f[:, NT * (D + W):][:, t * W:(t + 1) * W] for t in range(NT)], [gm_buf[:, t, :] for t in range(NT)]]
        conv_rows = z2f[0:CONV_T, 0:4 * P].rearrange("p (j c) -> p j c", j=4)
        lam_in = z2f[:, 4 * P:6 * P].rearrange("p (j c) -> p j c", j=4)
        lam_prod = z2f[:, 6 * P:7 * P].rearrange("p (j c) -> p j c", j=2)
        gain_rows = z2f[:, 7 * P:9 * P].rearrange("p (j c) -> p j c", j=2)
        sq_out0, sq_out1 = (v[:, D:3 * D].rearrange("p (t n) -> p t n", t=NT) for v in (z2f, z1f))

        raw_landed = [sem(f"raw_landed{j}") for j in range(NS)]
        hi_ready, lo_ready = sem("hi_ready"), sem("lo_ready")
        slot_used = sem("slot_used")
        by_act, by_dve = sem("evac_by_act"), sem("evac_by_dve")
        x_landed = [sem(f"x_landed{j}") for j in range(4)]
        rows_landed, ident_landed = sem("rows_landed"), sem("ident_landed")
        small_landed, gate_w_landed, final_landed = sem("small_landed"), sem("gate_w_landed"), sem("final_landed")
        const_set = sem("const_set")
        rows_T, gain_ready, gain_step = sem("rows_T"), sem("gain_ready"), sem("gain_step")
        kt_T, kt_hi, kt_lo = sem("kt_T"), sem("kt_hi"), sem("kt_lo")
        x_sq, part_sq, ss_ready = sem("x_sq"), sem("part_sq"), sem("ss_ready")
        ms_ready, rstd_ready, norm1_step = sem("ms_ready"), sem("rstd_ready"), sem("norm1_step")
        x_kept, fresh_part, fresh_ready = sem("x_kept"), sem("fresh_part"), sem("fresh_ready")
        lam_step, lam_exp, lam_ready = sem("lam_step"), sem("lam_exp"), sem("lam_ready")
        r_diag, r_bc_T, r_bc_ready = sem("r_diag"), sem("r_bc_T"), sem("r_bc_ready")
        tanh_ready, silu_step, act_hi, act_lo = sem("tanh_ready"), sem("silu_step"), sem("act_hi"), sem("act_lo")
        conv_start, conv_step, pad_set = sem("conv_start"), sem("conv_step"), sem("pad_set")
        gate_hi, gate_lo = sem("gate_hi"), sem("gate_lo")
        gates_done, gates_evac, gates_step, gates_act, log_f = (sem(n) for n in (
            "gates_done", "gates_evac", "gates_step", "gates_act", "log_f"))
        cum_done, cum_read, decay_ready = sem("cum_done"), sem("cum_read"), sem("decay_ready")
        diag_ready, decay_bc, den_part, floor_ready = sem("diag_ready"), sem("decay_bc"), sem("den_part"), sem("floor_ready")
        norm_step, gates_copied = sem("norm_step"), sem("gates_copied")
        x2_ready, warm = sem("x2_ready"), sem("warm")
        stored = sem("stored")
        hb, ha, hm, hf = (HeadSems(sem, k) for k in ("diff", "dil", "mlstm", "fox"))

        block = ctx.enter_context(nc.Block())
        ds = bass.ds

        def rows(w, k0=0, k1=None):
            r = w[k0:w.shape[0] if k1 is None else k1].rearrange("(u k p) n -> u p k n", k=UK, p=P)
            return [r[j] for j in range(r.shape[0])]

        def add_steps(steps, u0, units, parts):
            for u, part in zip(units, parts):
                steps.setdefault(u0 + u, []).append(part)

        def multiplied(name, i, units, step):
            return slot_used, at(i, NS + PH[name][0] + units, step)

        def evac_free(sem_, name, col, i, g):
            return sem_, at(i, FREE + PH[name][col] + 2 * g - 2, 4)

        BY_ACT, BY_DVE = 2, 3

        @block.sync
        def _(sp):
            sp.dma_start(gain_rows[0:KT, 0, :], a["norm_attn"][0].rearrange("(k c) -> k c", c=P)).then_inc(rows_landed, 16)
            sp.dma_start(ident[:], a["c_ident"]).then_inc(ident_landed, 16)
            x_in = a["x"][0].rearrange("(t p) n -> p t n", p=P)

            def load_x(j):
                cols = slice(j * W, (j + 1) * W)
                sp.dma_start(x[:, :, cols], x_in[:, :, cols]).then_inc(x_landed[j], 16)
            load_x(0)

            def load(n, i, step, src, width):
                sp.wait_ge(lo_ready, at(i, n + 1, step))
                sp.dma_start(raw[n % NS][:, :, 0:width], src).then_inc(raw_landed[n % NS], 16)

            def heads_turn(name, i, c0, behind=None):
                cols = a["w_in"][0][:, c0:c0 + C3].rearrange("(u k p) (c n) -> u k p c n", k=UK, p=P, c=3)
                n = PH[name][0]
                for g in range(2):
                    for u in range(8):
                        src = [cols[u][k][:, :, ds(at(i, g * P, 2 * P), P)] for k in range(UK)]
                        sp.wait_ge(lo_ready, at(i, n + 1, 16))
                        for k in range(UK):
                            sp.dma_start(raw[n % NS][:, k, 0:WH].rearrange("p (c n) -> p c n", c=3), src[k])\
                              .then_inc(raw_landed[n % NS], 16)
                        n += 1
                        if behind:
                            behind(8 * g + u)

            def stream(name, loops, parts):
                step = sum(len(units) for units, _, _ in parts)
                with sp.Fori(0, loops) as i:
                    n = PH[name][0]
                    for units, col, width in parts:
                        c = col(i)
                        for u in units:
                            src = u[:, :, ds(c, width)]
                            load(n, i, step, src, width)
                            n += 1

            def pairs(name, loops, units, c0, width):
                stream(name, loops, [(units, lambda i, g=g: i * (2 * width) + (c0 + g * width), width) for g in range(2)])

            w_in, w_out, w_in2 = a["w_in"][0], a["w_out"][0], a["w_in_2"][0]
            small = [(gain_rows[j * KT:(j + 1) * KT, 1, :], (a[name] if name == "norm_final" else a[name][0]).rearrange("(k c) -> k c", c=P))
                     for j, name in enumerate(("norm_ffn", "norm_final", "norm1_g_2", "norm2_g_2"))]
            late = G_SUBLN - G_FFN
            small += [(gain_rows[late:late + 1, 1, :], a["subln"]), (gain_rows[late + 1:late + 2, 1, :], a["q_norm_g_2"]),
                     (gain_rows[late + 2:late + 3, 1, :], a["k_norm_g_2"]),
                     (gain_rows[late + 3:late + 3 + 2 * M_HEADS, 1, :], a["m_norm_g_2"][0].rearrange("h (e c) -> (h e) c", c=P)),
                     (rope_a[:], a["c_rope_a"]), (rope_b[:], a["c_rope_b"]),
                     (tri[:], a["c_tri"]), (causal[:], a["c_causal"]),
                     (ln_count[:], a["c_count"].rearrange("p t s -> p (t s)")),
                     (lam_in, a["lambda_qk"][0].partition_broadcast(P)),
                     (gate_bias[:, 0:HEADS], a["fox_f_bias_2"][0].partition_broadcast(P)),
                     (gate_bias[:, HEADS:HEADS + M_HEADS], a["m_i_bias_2"][0].partition_broadcast(P)),
                     (gate_bias[:, HEADS + M_HEADS:NG], a["m_f_bias_2"][0].partition_broadcast(P))]
            small += [(conv_rows[:, j, :], a["conv_w_2"][0, j].rearrange("(k c) -> k c", c=P)) for j in range(3)]
            small += [(conv_rows[:, 3, :], a["conv_b_2"][0].rearrange("(k c) -> k c", c=P))]
            assert len(small) == N_SMALL

            def load_small(u):
                if u in X_BEHIND:
                    load_x(X_BEHIND.index(u) + 1)
                for dst, src in small[4 * (u - NS):4 * (u - NS) + 4] if u >= NS else ():
                    sp.dma_start(dst, src).then_inc(small_landed, 16)
            heads_turn("in_b", 0, C3, load_small)
            with sp.Fori(1, 4) as i:
                heads_turn("in_b", i, C3)
            with sp.Fori(0, 4) as i:
                heads_turn("in_a", i, 0)
            for i in range(2):
                for j in range(8):
                    n = PH["out_b"][0] + j
                    src, c = rows(w_out, HALF, D)[j % 4], (2 * i + j // 4) * W
                    if n < N_SPLIT and i == 0:
                        sp.wait_ge(lo_ready, n + 1)
                        for k in range(UK):
                            sp.dma_start(raw[n % NS][:, k, :], src[:, k, c:c + W]).then_inc(raw_landed[n % NS], 16)
                    else:
                        load(n, i, 8, src[:, :, c:c + W], W)
            pairs("out_a", 2, rows(w_out, 0, HALF), 0, W)
            with nc.allow_non_contiguous_dma("a few gate columns"):
                for c, off, n in ((0, OFF_GATES_F, HEADS), (HEADS, OFF_GATES_IF, 2 * M_HEADS)):
                    sp.dma_start(gate_w[:, :, c:c + n], w_in2[:, off:off + n].rearrange("(k p) n -> p k n", p=P))\
                      .then_inc(gate_w_landed, 16)

            def ffn(name, w_gate, w_up, up0, w_down):
                f0 = 0
                for t, width in enumerate(THIRDS):
                    stream(f"{name}_up{t}", width // W, [
                        (rows(w_gate), lambda i: i * W + f0, W), (rows(w_up), lambda i: i * W + (up0 + f0), W)])
                    pairs(f"{name}_down{t}", 2, rows(w_down, f0, f0 + width), 0, W)
                    f0 += width

            ffn("ffn1", a["w_gate"][0], a["w_up"][0], 0, a["w_down"][0])
            sp.dma_start(gain_final_bc, a["norm_final"].partition_broadcast(P)).then_inc(final_landed, 16)
            pairs("in_m", 3, rows(w_in2), OFF_M, W)
            pairs("in_f", 4, rows(w_in2), 0, WH)
            stream("gate_m", 4, [(rows(w_in2), lambda i: i * W + OFF_GM, W),
                                 (rows(a["w_proj_m_2"][0]), lambda i: (i + 1) * W - W, W)])
            pairs("gate_a", 2, rows(w_in2), OFF_GA, W)
            pairs("proj_a", 2, rows(a["w_proj_a_2"][0]), 0, W)
            pairs("out2", 2, rows(a["w_out_2"][0]), 0, W)
            ffn("ffn2", a["w_up_2"][0], a["w_up_2"][0], FF, a["w_down_2"][0])
            out_v = out[0].rearrange("(t p) n -> p t n", p=P)
            for g in range(4):
                cols = slice(g * W, (g + 1) * W)
                sp.wait_ge(by_dve, FREE + PH["ffn2_down2"][BY_DVE] + 2 * g + 2)
                sp.dma_start(out_v[:, :, cols], x[:, :, cols]).then_inc(stored, 16)
            sp.wait_ge(stored, 16 * 4)

        @block.tensor
        def _(pe):
            def by_token(acc, src, kt, n, k, width, first, last):
                hi, lo = src
                for t in range(NT):
                    q = slice(kt * S + t * P, kt * S + (t + 1) * P)
                    o = acc[t][:, 0:width]
                    pe.matmul(o, hi[:, q], w_hi[n % NS][:, k, 0:width], start=first, stop=False)
                    pe.matmul(o, hi[:, q], w_lo[n % NS][:, k, 0:width], start=False, stop=False)
                    mm = pe.matmul(o, lo[:, q], w_hi[n % NS][:, k, 0:width], start=False, stop=last)
                return mm

            def by_feature(acc, src, kt, n, k, first, last):
                hi, lo = (v[:, kt * S:(kt + 1) * S] for v in src)
                for f in range(4):
                    c = slice(f * P, (f + 1) * P)
                    o = acc[f // 2][:, (f % 2) * S:(f % 2 + 1) * S]
                    pe.matmul(o, w_hi[n % NS][:, k, c], hi, start=first and f % 2 == 0, stop=False)
                    pe.matmul(o, w_hi[n % NS][:, k, c], lo, start=False, stop=False)
                    mm = pe.matmul(o, w_lo[n % NS][:, k, c], hi, start=False, stop=last and f % 2 == 1)
                return mm

            def group(name, i, step, g, units, src, kt0, free, width=W, feature=False, ready=None, after={}, u0=None, also=None):
                u0 = g * units if u0 is None else u0
                pe.wait_ge(*free)
                if also:
                    pe.wait_ge(*also)
                for u in range(units):
                    n = PH[name][0] + u0 + u
                    if ready:
                        ready(u)
                    pe.wait_ge(lo_ready, at(i, NS + n + 1, step))
                    for k in range(UK):
                        j = u * UK + k
                        if feature:
                            mm = by_feature(pair[g], src, kt0 + j, n, k, j == 0, j == units * UK - 1)
                        else:
                            mm = by_token(pair[g], src, kt0 + j, n, k, width, j == 0, j == units * UK - 1)
                    mm.then_inc(slot_used, 1)
                    for step_ in after.get(u0 + u, ()):
                        step_()

            def tiles_ready(base):
                return lambda u: pe.wait_ge(kt_lo, base + UK * (u + 1))

            def turn_qk(s, h):
                pe.wait_ge(s.staged, h.upto())
                if s is hm:
                    pe.wait_ge(hm.y_lo, h.num(2, FREE))
                for c in range(2):
                    for t in range(NT):
                        mm = pe.transpose(ps[4][:, c * S + t * P:c * S + (t + 1) * P], stage[:, t, c, :], ident[:])
                mm.then_inc(s.qk_T, 1)

            def turn_p(s, src, blocks):
                for j, c in enumerate(blocks):
                    mm = pe.transpose(ps[4][:, j * P:(j + 1) * P], src[:, c:c + P], ident[:])
                mm.then_inc(s.p_T, 1)

            def values(s, h, z, col, width, blocks):
                pe.wait_ge(s.pT, h.upto())
                if s is not hm:
                    pe.wait_ge(s.y_lo, h.num(1, FREE))
                for t in range(NT):
                    keys = [kt for kt in range(2) if (t, kt) in blocks]
                    for kt in keys:
                        j = blocks[t, kt]
                        mm = pe.matmul(ps[7][:, t * width:(t + 1) * width], pT[:, j * P:(j + 1) * P],
                                       z[:, kt, ds(col, width)], start=kt == keys[0], stop=kt == keys[-1])
                mm.then_inc(s.pv, 1)

            def turn_y(s, h, bank, c0, tiles):
                pe.wait_ge(s.y, h.upto(2))
                for e in range(tiles):
                    for t in range(NT):
                        c = c0 + e * S + t * P
                        mm = pe.transpose(bank[:, c:c + P], y[:, t, e * P:(e + 1) * P], ident[:])
                mm.then_inc(s.y_T, 1)

            FULL = {(t, kt): 2 * kt + t for t in range(NT) for kt in range(2)}
            FULL_SRC = [t * S + kt * P for kt in range(2) for t in range(NT)]
            CAUSAL = {(0, 0): 0, (1, 0): 1, (1, 1): 2}
            CAUSAL_SRC = [0, P, 2 * P]

            def start_T(j):
                for c in range(2):
                    for t in range(NT):
                        kt = 2 * j + c
                        mm = pe.transpose(ps[START_BANKS[j]][:, c * S + t * P:c * S + (t + 1) * P], x[:, t, kt * P:(kt + 1) * P], ident[:])
                mm.then_inc(kt_T, 1)

            def start_more(j):
                pe.wait_ge(x_landed[j // 2], 16)
                if START_BANKS[j] in START_BANKS[:j]:
                    pe.wait_ge(kt_lo, 2 * START_BANKS.index(START_BANKS[j]) + 2)
                start_T(j)
            pe.wait_ge(rows_landed, 16)
            pe.wait_ge(ident_landed, 16)
            pe.transpose(ps[0][:, 0:KT], gain_rows[0:KT, 0, :], ident[0:KT, 0:KT]).then_inc(rows_T, 1)
            pe.wait_ge(x_landed[0], 16)
            for j in range(2):
                start_T(j)
            pe.wait_ge(gain_ready, 1)

            def diff_begin(steps, u0, h):
                def scores():
                    pe.wait_ge(hb.qkT, h.upto(2))
                    for t in range(NT):
                        for c in range(2):
                            e = slice(c * 64, (c + 1) * 64)
                            mm = pe.matmul(ps[5 + c][:, t * S:(t + 1) * S], qkT[e, 0, t * P:(t + 1) * P], qkT[e, 1, :],
                                           start=True, stop=True)
                            if t == NT - 1:
                                mm.then_inc(hb.scores, 1)

                def turn_mix():
                    pe.wait_ge(hb.mixed, h.upto(2))
                    turn_p(hb, mix, FULL_SRC)
                add_steps(steps, u0, HEAD_STEPS, (lambda: turn_qk(hb, h), scores, turn_mix,
                                                  lambda: values(hb, h, z1, h.num(WH, 2 * P), P, FULL)))

            def dil_begin(steps, u0, h, at_units=HEAD_STEPS):
                def scores():
                    pe.wait_ge(ha.qkT, h.upto(2))
                    for t in range(NT):
                        mm = pe.matmul(ps[5][:, t * S:(t + 1) * S], qkT[:, 0, t * P:(t + 1) * P], qkT[:, 1, :],
                                       start=True, stop=True)
                    mm.then_inc(ha.scores, 1)

                def turn_prob():
                    pe.wait_ge(ha.exps, h.upto(2))
                    turn_p(ha, prob, FULL_SRC)
                add_steps(steps, u0, at_units, (lambda: turn_qk(ha, h), scores, turn_prob,
                                                lambda: values(ha, h, z2, h.num(WH, 2 * P), P, FULL)))

            def end(steps, u, s, h):
                add_steps(steps, u, (0,), (lambda: turn_y(s, h, ps[7], S, 1),))

            def heads_turn(name, i, steps, ready=None):
                for g in range(2):
                    group(name, i, 16, g, 8, xT, 0, evac_free(by_act, name, BY_ACT, i, g), WH, ready=ready, after=steps)

            def small_T():
                pe.wait_ge(small_landed, 16 * N_SMALL)
                pe.wait_ge(kt_lo, KT)
                n_late = N_GAIN - G_FFN
                pe.transpose(ps[4][:, 0:n_late], gain_rows[0:n_late, 1, :], ident[0:n_late, 0:n_late]).then_inc(rows_T, 1)
                for j in range(4):
                    mm = pe.transpose(ps[5][:, j * CONV_T:(j + 1) * CONV_T], conv_rows[:, j, :], ident[0:CONV_T, 0:CONV_T])
                mm.then_inc(rows_T, 1)
            xT, yT = (xT_hi, xT_lo), (yT_hi, yT_lo)
            steps = {**{u: [lambda u=u: start_more(2 + u)] for u in range(6)}, 8: [small_T], 10: [lambda: pe.wait_ge(gain_ready, 3)]}
            diff_begin(steps, 10, Head(0, 0, 0))
            heads_turn("in_b", 0, steps, tiles_ready(0))
            with pe.Fori(1, 4) as i:
                steps = {}
                end(steps, 2, hb, Head(i, -2, 2))
                diff_begin(steps, 2, Head(i, -1, 2))
                end(steps, 10, hb, Head(i, -1, 2))
                diff_begin(steps, 10, Head(i, 0, 2))
                heads_turn("in_b", i, steps)
            steps = {}
            end(steps, 2, hb, Head(0, 6, 0))
            diff_begin(steps, 2, Head(0, 7, 0))
            end(steps, 10, hb, Head(0, 7, 0))
            dil_begin(steps, 10, Head(0, 0, 0))
            heads_turn("in_a", 0, steps)
            with pe.Fori(1, 4) as i:
                steps = {}
                end(steps, 2, ha, Head(i, -2, 2))
                dil_begin(steps, 2, Head(i, -1, 2))
                end(steps, 10, ha, Head(i, -1, 2))
                dil_begin(steps, 10, Head(i, 0, 2))
                heads_turn("in_a", i, steps)

            pe.wait_ge(by_act, FREE + PH["out_b"][BY_ACT] - 2)
            pe.wait_ge(hb.y_lo, FREE + HEADS)
            for i in range(2):
                steps = {}
                if i == 0:
                    end(steps, 2, ha, Head(0, 6, 0))
                    dil_begin(steps, 0, Head(0, 7, 0), LAST_DIL_STEPS)
                    end(steps, LAST_DIL_STEPS[-1], ha, Head(0, 7, 0))
                for g in range(2):
                    group("out_b", i, 8, g, 4, yT, HEADS, evac_free(by_dve, "out_b", BY_DVE, i, g), after=steps,
                          also=(by_act, FREE + PH["out_b"][BY_ACT]) if g else None)

            def turn_x(i, g, base, summed):
                pe.wait_ge(*summed)
                pe.wait_ge(kt_lo, at(i, base + 4 * g - 4, 8))
                for b in range(2):
                    for c in range(2):
                        for t in range(NT):
                            kt = 2 * b + c
                            mm = pe.transpose(ps[4 + 2 * g + b][:, c * S + t * P:c * S + (t + 1) * P],
                                              fresh[g][:, t, kt * P:(kt + 1) * P], ident[:])
                    mm.then_inc(kt_T, 1)

            def residual(name, units, src, kt0, base, summed=None, first=(), ready=None, also=None):
                sem_, c0 = summed or (by_dve, FREE + PH[name][BY_DVE])

                def transposes(q):
                    return lambda: turn_x(q // 2, q % 2, base, (sem_, c0 + 2 * q + 2))
                for i in range(2):
                    after = {1: first if i == 0 else [transposes(1)], units + 1: [transposes(2 * i)]}
                    for g in range(2):
                        group(name, i, 2 * units, g, units, src, kt0, evac_free(by_dve, name, BY_DVE, i, g),
                              ready=ready, after=after, also=also if g else None)
                return transposes(3)

            rest = residual("out_a", 4, yT, 0, KT, ready=lambda u: pe.wait_ge(ha.y_lo, FREE + UK * (u + 1)))

            def broadcast_rstd(n):
                pe.wait_ge(r_diag, 2 * n)
                for t in range(NT):
                    mm = pe.matmul(ps[4][:, t * P:(t + 1) * P], ones[:], diag[:, t, :], start=True, stop=True)
                mm.then_inc(r_bc_T, 1)

            def ffn(name, src, act, base, n_norm, fg0, last_base, rest):
                for t, width in enumerate(THIRDS):
                    up, down, n_fg = f"{name}_up{t}", f"{name}_down{t}", width // W

                    def up_groups(i, after={}):
                        for g in range(2):
                            group(up, i, 16, g, 8, src, 0, evac_free(by_dve, up, BY_DVE, i, g), feature=True,
                                  ready=tiles_ready(base), after=after)
                    start = 0
                    if t == 0:
                        up_groups(None, {1: [rest], 4: [lambda: broadcast_rstd(n_norm)]})
                        start = 1

                    def up_turn(i, start=start):
                        up_groups(i)
                    with pe.Fori(start, n_fg) as i:
                        up_turn(i)
                    units = width // (UK * P)

                    def act_ready(u, f=fg0):
                        pe.wait_ge(act_lo, f + u // 2 + 1)
                    fg0 += n_fg
                    if t == 2 and last_base is not None:
                        return residual(down, units, act, 0, last_base, ready=act_ready)
                    else:
                        with pe.Fori(0, 2) as i:
                            for g in range(2):
                                group(down, i, 2 * units, g, units, act, 0, evac_free(by_dve, down, BY_DVE, i, g), ready=act_ready)

            rest = ffn("ffn1", xT, yT, KT, 1, 0, 2 * KT, rest)

            pe.wait_ge(by_dve, FREE + PH["in_m"][BY_DVE] - 2)
            base2 = 2 * KT
            for i in range(2):
                for g in range(2):
                    group("in_m", i, 16, g, 8, xT, 0, evac_free(by_act, "in_m", BY_ACT, i, g), ready=tiles_ready(base2),
                          also=(by_dve, FREE + PH["in_m"][BY_DVE]) if g else None, after={1: [rest]} if i == 0 else {})

            def gates():
                pe.wait_ge(gate_lo, 1)
                o = ps[4][0:NG, 0:S]
                for kt in range(KT):
                    c = slice(kt * S, (kt + 1) * S)
                    pe.matmul(o, gate_w_hi[:, kt, :], xT_hi[:, c], start=kt == 0, stop=False)
                    pe.matmul(o, gate_w_hi[:, kt, :], xT_lo[:, c], start=False, stop=False)
                    mm = pe.matmul(o, gate_w_lo[:, kt, :], xT_hi[:, c], start=False, stop=kt == KT - 1)
                mm.then_inc(gates_done, 1)

            def gates_back():
                pe.wait_ge(gates_copied, 1)
                for t in range(NT):
                    mm = pe.transpose(ps[5][:, t * NG:(t + 1) * NG], gates_T[:, t * P:(t + 1) * P], ident[0:NG, 0:NG])
                mm.then_inc(gates_done, 1)

            def cumulate():
                pe.wait_ge(log_f, 1)
                pe.matmul(ps[5][:, 0:NG], tri[:], lf[:, 0, :], start=True, stop=True)
                pe.matmul(ps[5][:, NG:2 * NG], ones[:], lf[:, 0, :], start=True, stop=False)
                pe.matmul(ps[5][:, NG:2 * NG], tri[:], lf[:, 1, :], start=False, stop=True).then_inc(cum_done, 1)
            for g in range(2):
                group("in_m", 2, 16, g, 8, xT, 0, evac_free(by_act, "in_m", BY_ACT, 2, g),
                      after={0: [gates], 3: [gates_back], 8: [cumulate]})
            pe.wait_ge(cum_read, 1)

            with pe.Fori(0, 4) as i:
                h = Head(i, 0, 1)

                def decay_rows():
                    pe.wait_ge(diag_ready, h.upto(2))
                    for kt in range(2):
                        mm = pe.matmul(ps[5][:, kt * P:(kt + 1) * P], ones[:], diag[:, kt, :], start=True, stop=True)
                    mm.then_inc(decay_bc, 1)

                def scores_mlstm():
                    pe.wait_ge(hm.qkT, h.upto(2))
                    for t, c, n in ((0, 0, P), (1, P, S)):
                        mm = pe.matmul(ps[6][:, c:c + n], qkT[:, 0, t * P:(t + 1) * P], qkT[:, 1, 0:n], start=True, stop=True)
                    mm.then_inc(hm.scores, 1)

                def turn_weights():
                    pe.wait_ge(hm.mixed, h.upto(2))
                    turn_p(hm, mix, CAUSAL_SRC)
                steps = {2: [decay_rows]}
                add_steps(steps, 0, MLSTM_STEPS, (
                    lambda: turn_qk(hm, h), scores_mlstm, turn_weights,
                    lambda: values(hm, h, z1, h.num(M_DV, HALF), M_DV, CAUSAL), lambda: turn_y(hm, h, ps[4], 0, 2)))
                for g in range(2):
                    group("in_f", i, 16, g, 8, xT, 0, evac_free(by_act, "in_f", BY_ACT, i, g), WH, after=steps)

            def fox(steps, u0, h, at_units):
                def scores():
                    pe.wait_ge(hf.qkT, h.upto(2))
                    pe.wait_ge(diag_ready, h.upto(2, 2 * M_HEADS + 2))
                    for t, c, n in ((0, 0, P), (1, P, S)):
                        pe.matmul(ps[6][:, c:c + n], qkT[:, 0, t * P:(t + 1) * P], qkT[:, 1, 0:n], start=True, stop=False)
                        for kt in range(t + 1):
                            mm = pe.matmul(ps[6][:, c + kt * P:c + (kt + 1) * P], ones[:], diag[:, kt, :],
                                           start=False, stop=kt == t)
                    mm.then_inc(hf.scores, 1)

                def turn_fox():
                    pe.wait_ge(hf.exps, h.upto(2))
                    turn_p(hf, prob, CAUSAL_SRC)
                add_steps(steps, u0, at_units, (
                    lambda: turn_qk(hf, h), scores, turn_fox,
                    lambda: values(hf, h, z2, h.num(P, 2 * HALF), P, CAUSAL), lambda: turn_y(hf, h, ps[7], S, 1)))
            pe.wait_ge(hm.y_lo, FREE + 2 * M_HEADS)
            with pe.Fori(0, 4) as i:
                steps = {}
                fox(steps, 0, Head(i, 0, 1), FOX_M_STEPS)
                group("gate_m", i, 12, 0, 8, xT, 0, (by_act, at(i, FREE + PH["gate_m"][BY_ACT] - 2, 2)), after=steps,
                      also=(hf.y_lo, Head(i, 0, 1).num(1, FREE)))
                group("gate_m", i, 12, 1, 4, yT, HEADS, (by_dve, at(i, FREE + PH["gate_m"][BY_DVE], 2)), after=steps, u0=8)
            pe.wait_ge(by_act, FREE + PH["gate_a"][BY_ACT])
            with pe.Fori(0, 2) as i:
                steps = {}
                for g in range(2):
                    fox(steps, 8 * g, Head(i, 4 + g, 2), FOX_A_STEPS)
                for g in range(2):
                    group("gate_a", i, 16, g, 8, xT, 0, evac_free(by_act, "gate_a", BY_ACT, i, g), after=steps,
                          also=(by_dve, FREE + PH["gate_a"][BY_DVE]) if g else None)
            pe.wait_ge(by_act, FREE + PH["proj_a"][BY_ACT] - 2)
            rest = residual("proj_a", 4, yT, 0, 3 * KT, (fresh_ready, 0), (),
                            lambda u: pe.wait_ge(hf.y_lo, FREE + UK * (u + 1)), (by_act, FREE + PH["proj_a"][BY_ACT]))
            rest = residual("out2", 8, xT, 0, 4 * KT, None, [rest], tiles_ready(3 * KT))
            ffn("ffn2", yT, xT, 4 * KT, 2, FF // W, None, rest)

        @block.scalar
        def _(act):
            def split(n, i, step, width=W):
                loads = UK if n < N_SPLIT else 1
                before = 0 if n < N_SPLIT else (UK - 1) * N_SPLIT // NS
                act.wait_ge(raw_landed[n % NS], at(i, 16 * (loads * (n // NS + 1) + before), 16 * loads * step // NS))
                act.wait_ge(slot_used, at(i, n + 1, step))
                nc.scalar.activation(w_hi[n % NS][:, :, 0:width], raw[n % NS][:, :, 0:width], ACT.Copy).then_inc(hi_ready, 1)

            def turn(name, i, units, steps={}, width=W, ahead=True):
                for u in range(units):
                    if ahead or u + NS < units:
                        split(PH[name][0] + NS + u, i, units, width if u + NS < units else W)
                    for step in steps.get(u, ()):
                        step()

            act.wait_ge(const_set, N_CONST)
            nc.scalar.activation(junk[:, 0:4], eps_diff[:], ACT.Exp).then_inc(warm, 1)
            act.wait_ge(warm, 1)

            def start_tile(kt):
                act.wait_ge(kt_T, kt // 2 + 1)
                if kt == 0:
                    act.wait_ge(gain_ready, 1)
                nc.scalar.activation(xT_hi[:, kt * S:(kt + 1) * S], ps[START_BANKS[kt // 2]][:, kt % 2 * S:(kt % 2 + 1) * S],
                                     ACT.Copy, scale=gain[:, G_ATTN + kt:G_ATTN + kt + 1]).then_inc(kt_hi, 1)
            for u in range(NS):
                start_tile(2 * u)
                start_tile(2 * u + 1)
                split(u, None, 0, WH)

            def squares_of_x(t, dst):
                nc.scalar.activation(dst[:, t, :], x[:, t, :], ACT.Square, accum_out=ss[:, t:t + 1]).then_inc(x_sq, 1)

            def evac(name, i, g, dst, col, width, scale, func=ACT.Copy, step=16):
                act.wait_ge(*multiplied(name, i, 8 * (g + 1), step))
                for t in range(NT):
                    o = dst[t] if isinstance(dst, list) else dst[:, t, ds(col, width)]
                    nc.scalar.activation(o, pair[g][t][:, 0:width], func,
                                         scale=scale[:, t:t + 1]).then_inc(by_act, 1)

            def qk_out(s, h, scale):
                act.wait_ge(s.qk_T, h.num(1, FREE + 1))
                nc.scalar.activation(qkT[:, 0, :], ps[4][:, 0:S], ACT.Copy, scale=scale).then_inc(s.qkT, 1)
                nc.scalar.activation(qkT[:, 1, :], ps[4][:, S:2 * S], ACT.Copy).then_inc(s.qkT, 1)

            def p_out(s, h, n):
                act.wait_ge(s.p_T, h.upto())
                nc.scalar.activation(pT[:, 0:n], ps[4][:, 0:n], ACT.Copy).then_inc(s.pT, 1)

            def squares(s, h, width, scale):
                act.wait_ge(s.rden, h.upto())
                act.wait_ge(s.pv, h.upto())
                for t in range(NT):
                    nc.scalar.activation(junk[:, t * width:(t + 1) * width], ps[7][:, t * width:(t + 1) * width], ACT.Square,
                                         scale=scale[:, t:t + 1], accum_out=head_ss[:, t:t + 1]).then_inc(s.sq, 1)

            def y_hi(s, h, bank, c0, tile0, tiles, scale):
                act.wait_ge(s.y_T, h.upto())
                for e in range(tiles):
                    nc.scalar.activation(yT_hi[:, ds(h.num(tiles * S, (tile0 + e) * S), S)], bank[:, c0 + e * S:c0 + (e + 1) * S],
                                         ACT.Copy, scale=scale(e)).then_inc(s.y_hi, 1)

            def diff_begin(steps, u0, h):
                def exps():
                    for c in range(2):
                        act.wait_ge(hb.row_max, h.upto(2, c + 1))
                        for t in range(NT):
                            nc.scalar.activation(prob[:, (2 * t + c) * S:(2 * t + c + 1) * S], ps[5 + c][:, t * S:(t + 1) * S],
                                                 ACT.Exp, bias=neg_max[:, t, c:c + 1],
                                                 accum_out=den[:, c, t:t + 1]).then_inc(hb.exps, 1)
                add_steps(steps, u0, HEAD_STEPS, (lambda: qk_out(hb, h, B_SCALE), exps, lambda: p_out(hb, h, 2 * S),
                                                  lambda: squares(hb, h, P, rden[:, 0])))

            def dil_begin(steps, u0, h, at_units=HEAD_STEPS):
                def exps():
                    act.wait_ge(ha.row_max, h.upto())
                    for t in range(NT):
                        nc.scalar.activation(prob[:, t * S:(t + 1) * S], mix[:, t * S:(t + 1) * S], ACT.Exp,
                                             bias=neg_max[:, 0, t:t + 1], accum_out=den[:, 0, t:t + 1]).then_inc(ha.exps, 1)
                add_steps(steps, u0, at_units, (lambda: qk_out(ha, h, 1.0), exps, lambda: p_out(ha, h, 2 * S)))

            def diff_end(steps, u, h):
                add_steps(steps, u, (0,), (lambda: y_hi(hb, h, ps[7], S, HEADS, 1, lambda e: gain[:, G_SUBLN:G_SUBLN + 1]),))

            def dil_end(steps, u, h):
                add_steps(steps, u, (0,), (lambda: y_hi(ha, h, ps[7], S, 0, 1, lambda e: 1.0),))

            def heads_turn(name, i, steps, z):
                for g in range(2):
                    add_steps(steps, 8 * g, (7,), (lambda g=g: evac(name, i, g, z, at(i, g * WH, 2 * WH), WH, rstd),))
                turn(name, i, 16, steps, WH)

            def lam_exps():
                act.wait_ge(lam_step, 2)
                nc.scalar.activation(lam_t[:, 2:4], lam_t[:, 0:2], ACT.Exp).then_inc(lam_exp, 1)
            start = {u: [lambda u=u: start_tile(2 * (NS + u)), lambda u=u: start_tile(2 * (NS + u) + 1)] for u in range(NS)}
            steps = {**start, 4: [lambda: squares_of_x(0, sq_out0)], 5: [lambda: squares_of_x(1, sq_out0)],
                     6: [lambda: act.wait_ge(rstd_ready, 1)], 9: [lam_exps]}
            diff_begin(steps, 10, Head(0, 0, 0))
            heads_turn("in_b", 0, steps, z1)
            with act.Fori(1, 4) as i:
                steps = {}
                diff_end(steps, 2, Head(i, -2, 2))
                diff_begin(steps, 2, Head(i, -1, 2))
                diff_end(steps, 10, Head(i, -1, 2))
                diff_begin(steps, 10, Head(i, 0, 2))
                heads_turn("in_b", i, steps, z1)
            act.wait_ge(gain_ready, 3)
            steps = {}
            diff_end(steps, 2, Head(0, 6, 0))
            diff_begin(steps, 2, Head(0, 7, 0))
            diff_end(steps, 10, Head(0, 7, 0))
            dil_begin(steps, 10, Head(0, 0, 0))
            heads_turn("in_a", 0, steps, z2)
            with act.Fori(1, 4) as i:
                steps = {}
                dil_end(steps, 2, Head(i, -2, 2))
                dil_begin(steps, 2, Head(i, -1, 2))
                dil_end(steps, 10, Head(i, -1, 2))
                dil_begin(steps, 10, Head(i, 0, 2))
                heads_turn("in_a", i, steps, z2)

            steps = {}
            dil_end(steps, 2, Head(0, 6, 0))
            dil_begin(steps, 0, Head(0, 7, 0), LAST_DIL_STEPS)
            dil_end(steps, LAST_DIL_STEPS[-1], Head(0, 7, 0))
            turn("out_b", 0, 8, steps)
            turn("out_b", 1, 8)

            def row_squares(i, g, e, summed):
                act.wait_ge(*summed)
                for t in range(NT):
                    act.wait_ge(part_sq, at(i, FREE + 8 * e + 2 * g + t, 4))
                    nc.scalar.activation(junk[:], fresh[g][:, t, :], ACT.Square,
                                         accum_out=part_ss[:, t, ds(at(i, g, 2), 1)]).then_inc(part_sq, 1)

            def x_hi(i, g, base, dst, gain0):
                for j in range(4):
                    act.wait_ge(kt_T, at(i, (base + 4 * g) // 2 + j // 2 + 1, 4))
                    scale = 0.5 if gain0 is None else gain[:, ds(at(i, gain0 + 4 * g + j, 8), 1)]
                    nc.scalar.activation(dst[:, ds(at(i, (4 * g + j) * S, 8 * S), S)],
                                         ps[4 + 2 * g + j // 2][:, j % 2 * S:(j % 2 + 1) * S], ACT.Copy, scale=scale)\
                      .then_inc(kt_hi, 1)

            def residual(name, units, base, dst, gain0, e=None, first=(), tail={}):
                def sq(i, g):
                    if e is not None:
                        row_squares(i, g, e, (by_dve, FREE + PH[name][BY_DVE] + 4 * i + 2 * g + 2))
                for i in range(2):
                    steps = {1: first if i == 0 else [lambda: x_hi(0, 1, base, dst, gain0)],
                             units - 1: [lambda: sq(i, 0)], units + 1: [lambda: x_hi(i, 0, base, dst, gain0)],
                             2 * units - 1: [lambda: sq(i, 1)]}
                    turn(name, i, 2 * units, {**steps, **tail} if i == 0 else steps)
                return lambda: x_hi(1, 1, base, dst, gain0)

            rest = residual("out_a", 4, KT, xT_hi, G_FFN, 0)

            def ffn(name, dst, fg0, conv_too, last_base, rest):
                for t, width in enumerate(THIRDS):
                    up, down, n_fg, units = f"{name}_up{t}", f"{name}_down{t}", width // W, width // (UK * P)
                    f0 = fg0 - (FF // W if conv_too else 0)

                    def gate_tanh(i):
                        if conv_too:
                            act.wait_ge(conv_step, at(i, 16 * f0 + 8, 16))
                        else:
                            act.wait_ge(by_dve, at(i, FREE + PH[up][BY_DVE] + 2, 4))
                        nc.scalar.activation(tanh_z, gate_z, ACT.Tanh, scale=0.5).then_inc(tanh_ready, 1)

                    def first_tap(i, g, u, z):
                        act.wait_ge(by_dve, at(i, FREE + PH[up][BY_DVE] + 2 * g + 2, 4))
                        for f in range(4):
                            col = at(i, 4 * f0 + f + g * (CONV_T // 2), 4)
                            nc.scalar.activation(z[:, f, :], u[:, f, PAD:PAD + S], ACT.Identity, scale=conv[:, ds(col + 2 * CONV_T, 1)],
                                                 bias=conv[:, ds(col + 3 * CONV_T, 1)]).then_inc(conv_start, 1)

                    def hi_part(i):
                        if conv_too:
                            act.wait_ge(silu_step, at(i, 2 * (fg0 + 1), 2))
                        else:
                            act.wait_ge(by_dve, at(i, FREE + PH[up][BY_DVE] + 4, 4))
                        nc.scalar.activation(tiles4(dst[:, ds(at(i, 0, 4 * S), 4 * S)], S), up_z, ACT.Copy, scale=0.5).then_inc(act_hi, 1)
                    u_tanh, late = (10, True) if conv_too else (8, False)

                    def own_parts(i):
                        if late:
                            return {7: [lambda: first_tap(i, 0, gate_u, gate_z)], u_tanh: [lambda: gate_tanh(i)],
                                    15: [lambda: first_tap(i, 1, up_u, up_z)]}
                        return {u_tanh: [lambda: gate_tanh(i)], 15: [lambda: hi_part(i)]}

                    def late_parts(i):
                        return {0: [lambda: hi_part(i)]} if late else {}
                    turn(up, 0, 16, {**own_parts(0), **({1: [rest]} if t == 0 else {})})
                    with act.Fori(1, n_fg) as i:
                        turn(up, i, 16, {**late_parts(i - 1), **own_parts(i)})
                    tail = late_parts(n_fg - 1)
                    if t == 2 and last_base is not None:
                        return residual(down, units, last_base, xT_hi, G_NORM1, 1, tail=tail)
                    for i in range(2):
                        turn(down, i, 2 * units, {} if i else tail, ahead=t < 2 or i == 0)
                    fg0 += n_fg

            rest = ffn("ffn1", yT_hi, 0, False, 2 * KT, rest)

            def gate_w_part():
                act.wait_ge(gate_w_landed, 32)
                nc.scalar.activation(gate_w_hi[:], gate_w[:], ACT.Copy).then_inc(gate_hi, 1)

            def x2_squares(t):
                act.wait_ge(x2_ready, t + 1)
                squares_of_x(t, sq_out1)

            def m_turn(i, steps, scales, func):
                for g in range(2):
                    add_steps(steps, 8 * g, (8 if g == 0 else 7,), (
                        lambda g=g: evac("in_m", i, g, z1, at(i, g * W, 2 * W), W, scales, func),))
                turn("in_m", i, 16, steps)
            m_turn(0, {0: [gate_w_part], 1: [rest], 4: [lambda: x2_squares(0)], 6: [lambda: x2_squares(1)],
                       7: [lambda: act.wait_ge(rstd_ready, 4)]}, rstd2, ACT.Copy)
            m_turn(1, {}, rstd2, ACT.Copy)

            def gates_copy():
                act.wait_ge(gates_done, 1)
                nc.scalar.activation(gates_T, ps[4][0:NG, 0:S], ACT.Copy).then_inc(gates_copied, 1)

            def gates_out():
                act.wait_ge(gates_done, 2)
                for t in range(NT):
                    nc.scalar.activation(gz[:, t, :], ps[5][:, t * NG:(t + 1) * NG], ACT.Copy, scale=rstd2[:, t:t + 1]).then_inc(gates_evac, 1)

            def softplus():
                act.wait_ge(gates_step, 2)
                nc.scalar.activation(gt[:], gt[:], ACT.Exp, scale=-1.0).then_inc(gates_act, 1)
                act.wait_ge(gates_act, 1)
                nc.scalar.activation(gt[:], gt[:], ACT.Ln, bias=1.0).then_inc(gates_act, 1)
            m_turn(2, {2: [gates_copy], 3: [gates_out], 5: [softplus]}, half_rstd2, ACT.Tanh)

            with act.Fori(0, 4) as i:
                h = Head(i, 0, 1)

                def decay():
                    act.wait_ge(hm.row_max, h.upto())
                    for t, c, n in ((0, 0, P), (1, P, S)):
                        nc.scalar.activation(prob[:, c:c + n], mix[:, c:c + n], ACT.Exp, bias=neg_max[:, 0, t:t + 1]).then_inc(hm.exps, 1)
                    for t in range(NT):
                        nc.scalar.activation(floor[:, t:t + 1], f_sum[:, t, ds(h.num(1, HEADS + M_HEADS), 1)], ACT.Exp, scale=-1.0,
                                             bias=neg_max[:, 0, t:t + 1]).then_inc(floor_ready, 1)
                steps = {4: [decay]}
                u_qk, _, u_p, u_v, u_y = MLSTM_STEPS
                add_steps(steps, 0, (u_qk, u_p, u_v, u_y), (
                    lambda: qk_out(hm, h, HEAD_SCALE), lambda: p_out(hm, h, 3 * P), lambda: squares(hm, h, M_DV, rden[:, 0]),
                    lambda: y_hi(hm, h, ps[4], 0, HEADS, 2, lambda e: gain[:, ds(h.num(2, G_M + e), 1)])))
                for g in range(2):
                    add_steps(steps, 8 * g, (7,), (lambda g=g: evac("in_f", i, g, z2, at(i, g * WH, 2 * WH), WH, rstd2),))
                turn("in_f", i, 16, steps, WH)

            def fox(steps, u0, h, at_units):
                def qk_squares():
                    act.wait_ge(hf.ms, h.num(1, FREE))
                    for t in range(NT):
                        for c in range(2):
                            nc.scalar.activation(junk[:, (2 * t + c) * P:(2 * t + c + 1) * P], z2[:, t, ds(h.num(P, c * HALF), P)], ACT.Square,
                                                 accum_out=head_ss[:, 2 * t + c:2 * t + c + 1]).then_inc(hf.sq, 1)

                def exps():
                    act.wait_ge(hf.raw_max, h.upto(2))
                    for t, c, n in ((0, 0, P), (1, P, S)):
                        nc.scalar.activation(prob[:, c:c + n], mix[:, c:c + n], ACT.Exp, bias=neg_max[:, 0, t:t + 1],
                                             accum_out=den[:, 0, t:t + 1]).then_inc(hf.exps, 1)
                u_qk, u_s, u_p, _, u_y = at_units
                add_steps(steps, u0, (0, u_qk, u_s, u_p, u_y), (
                    qk_squares, lambda: qk_out(hf, h, gain_qk[:, 1:2]), exps, lambda: p_out(hf, h, 3 * P),
                    lambda: y_hi(hf, h, ps[7], S, 0, 1, lambda e: 1.0)))
            with act.Fori(0, 4) as i:
                steps = {}
                fox(steps, 0, Head(i, 0, 1), FOX_M_STEPS)

                def gate_out():
                    act.wait_ge(by_dve, at(i, FREE + PH["gate_m"][BY_DVE], 2))
                    evac("gate_m", i, 0, gm_buf, 0, W, half_rstd2, ACT.Tanh, 12)
                add_steps(steps, 0, (7,), (gate_out,))
                turn("gate_m", i, 12, steps)

            act.wait_ge(by_dve, FREE + PH["gate_a"][BY_DVE])
            for i in range(2):
                steps = {}
                for g in range(2):
                    fox(steps, 8 * g, Head(i, 4 + g, 2), FOX_A_STEPS)
                    add_steps(steps, 8 * g, (7,), (
                        lambda g=g: evac("gate_a", i, g, ga_buf[2 * i + g], 0, W, half_rstd2, ACT.Tanh),))
                turn("gate_a", i, 16, steps)
            rest = residual("proj_a", 4, 3 * KT, xT_hi, None)
            rest = residual("out2", 8, 4 * KT, yT_hi, G_NORM2, 2, [rest])
            ffn("ffn2", xT_hi, FF // W, True, None, rest)

        @block.vector
        def _(dve):
            v = nc.vector

            def f32(t):
                return t.bitcast(F32)

            def split(n, i, step, width=W):
                dve.wait_ge(hi_ready, at(i, n + 1, step))
                v.tensor_tensor(w_lo[n % NS][:, :, 0:width], raw[n % NS][:, :, 0:width], f32(w_hi[n % NS][:, :, 0:width]),
                                ALU.subtract).then_inc(lo_ready, 1)

            def turn(name, i, units, steps={}, width=W, ahead=True):
                for u in range(units):
                    for step in steps.get(("before", u), ()):
                        step()
                    if ahead or u + NS < units:
                        split(PH[name][0] + NS + u, i, units, width if u + NS < units else W)
                    for step in steps.get(u, ()):
                        step()

            dve.wait_ge(rows_T, 1)
            v.tensor_copy(gain[:, 0:KT], ps[0][:, 0:KT]).then_inc(gain_ready, 1)
            dve.wait_ge(gain_ready, 1)

            def start_tiles(u):
                for kt in (2 * u, 2 * u + 1):
                    dve.wait_ge(kt_hi, 2 * u + 2)
                    c = slice(kt * S, (kt + 1) * S)
                    v.scalar_tensor_tensor(xT_lo[:, c], ps[START_BANKS[kt // 2]][:, kt % 2 * S:(kt % 2 + 1) * S],
                                           gain[:, G_ATTN + kt:G_ATTN + kt + 1], f32(xT_hi[:, c]), ALU.mult, ALU.subtract).then_inc(kt_lo, 1)
            for u in range(NS):
                start_tiles(u)
                split(u, None, 0, WH)

            def parameters():
                dve.wait_ge(small_landed, 16 * N_SMALL)
                v.tensor_tensor(lam_prod, lam_in[:, 0:4:2, :], lam_in[:, 1:4:2, :], ALU.mult).then_inc(lam_step, 1)
                dve.wait_ge(rows_T, 2)
                v.tensor_copy(gain[:, G_FFN:N_GAIN], ps[4][:, 0:N_GAIN - G_FFN]).then_inc(gain_ready, 1)
                dve.wait_ge(rows_T, 3)
                v.tensor_copy(conv[:], ps[5][:, 0:4 * CONV_T]).then_inc(gain_ready, 1)
                dve.wait_ge(lam_step, 1)
                v.tensor_reduce(lam_t[:, 0:2], lam_prod, X, ALU.add).then_inc(lam_step, 1)

            def more_parameters():
                dve.wait_ge(gain_ready, 3)
                v.tensor_tensor(gain[:, G_NORM1:G_NORM1 + KT], gain[:, G_NORM1:G_NORM1 + KT], gain[:, G_FINAL:G_FINAL + KT],
                                ALU.mult).then_inc(gain_step, 1)
                v.tensor_scalar(gain[:, G_SUBLN:G_SUBLN + 1], gain[:, G_SUBLN:G_SUBLN + 1], 1.0 - LAM_INIT, None, ALU.mult).then_inc(gain_step, 1)
                v.tensor_tensor(gain_qk[:, 0:1], gain[:, G_Q:G_Q + 1], gain[:, G_K:G_K + 1], ALU.mult).then_inc(gain_step, 1)
                v.tensor_scalar(gain[:, G_M:N_GAIN], gain[:, G_M:N_GAIN], 0.5, None, ALU.mult).then_inc(gain_step, 1)
                dve.wait_ge(gain_step, 4)
                v.tensor_scalar(gain_qk[:, 1:2], gain_qk[:, 0:1], P * HEAD_SCALE, None, ALU.mult).then_inc(gain_step, 1)
                dve.wait_ge(lam_exp, 1)
                v.tensor_tensor(lam_t[:, 4:5], lam_t[:, 3:4], lam_t[:, 2:3], ALU.subtract).then_inc(lam_step, 1)
                dve.wait_ge(lam_step, 3)
                v.tensor_scalar(minus_lam[:], lam_t[:, 4:5], -LAM_INIT, None, ALU.add).then_inc(lam_ready, 1)
                dve.wait_ge(lam_ready, 1)
                dve.wait_ge(gain_step, 5)

            def y_out(s, h, width, scale):
                for t in range(NT):
                    v.tensor_scalar(y[:, t, 0:width], ps[7][:, t * width:(t + 1) * width], scale[:, t:t + 1], None, ALU.mult).then_inc(s.y, 1)

            def y_lo(s, h, bank, c0, tile0, tiles, scale):
                dve.wait_ge(s.y_hi, h.upto(tiles))
                for e in range(tiles):
                    c = ds(h.num(tiles * S, (tile0 + e) * S), S)
                    v.scalar_tensor_tensor(yT_lo[:, c], bank[:, c0 + e * S:c0 + (e + 1) * S], scale(e), f32(yT_hi[:, c]),
                                           ALU.mult, ALU.subtract).then_inc(s.y_lo, 1)

            def diff_begin(steps, u0, h):
                def maxima():
                    for c in range(2):
                        dve.wait_ge(hb.scores, h.upto(2, c + 1))
                        v.tensor_reduce(neg_max[:, :, c], ps[5 + c][:, :].rearrange("p (t s) -> p t s", t=NT), X, ALU.max,
                                        negate=True).then_inc(hb.row_max, 1)

                def mix_parts():
                    dve.wait_ge(hb.exps, h.upto(4))
                    v.reciprocal(rden[:], den[:]).then_inc(hb.rden, 1)
                    dve.wait_ge(hb.rden, h.upto())
                    v.scalar_tensor_tensor(coef[:], rden[:, 1, :], minus_lam[:], den[:, 0, :], ALU.mult, ALU.mult).then_inc(hb.coef, 1)
                    dve.wait_ge(hb.coef, h.upto(2, 1))
                    for t in range(NT):
                        c0, c1 = (prob[:, (2 * t + c) * S:(2 * t + c + 1) * S] for c in range(2))
                        v.scalar_tensor_tensor(mix[:, t * S:(t + 1) * S], c1, coef[:, t:t + 1], c0, ALU.mult, ALU.add).then_inc(hb.mixed, 1)
                add_steps(steps, u0, (1, 1), (maxima, mix_parts))

            def diff_end(steps, u, h):
                def result():
                    dve.wait_ge(hb.rstd, h.upto())
                    v.scalar_tensor_tensor(coef[:], rden[:, 0, :], P ** 0.5, head_rstd[:, 0:NT], ALU.mult, ALU.mult).then_inc(hb.coef, 1)
                    dve.wait_ge(hb.coef, h.upto(2))
                    y_out(hb, h, P, coef)
                add_steps(steps, u, (-2, 0), (result, lambda: y_lo(hb, h, ps[7], S, HEADS, 1, lambda e: gain[:, G_SUBLN:G_SUBLN + 1])))

            def dil_begin(steps, u0, h):
                def masked_max():
                    dve.wait_ge(ha.scores, h.upto())
                    v.scalar_tensor_tensor(mix[:], ps[5][:], HEAD_SCALE, ln_count[:], ALU.mult, ALU.add).then_inc(ha.masked, 1)
                    dve.wait_ge(ha.masked, h.upto())
                    v.tensor_reduce(neg_max[:, 0, :], mix[:].rearrange("p (t s) -> p t s", t=NT), X, ALU.max,
                                    negate=True).then_inc(ha.row_max, 1)
                add_steps(steps, u0, (1,), (masked_max,))

            def dil_end(steps, u, h):
                def result():
                    dve.wait_ge(ha.exps, h.upto(2))
                    v.reciprocal(rden[:, 0, :], den[:, 0, :]).then_inc(ha.rden, 1)
                    dve.wait_ge(ha.rden, h.upto())
                    dve.wait_ge(ha.pv, h.upto())
                    y_out(ha, h, P, rden[:, 0])
                add_steps(steps, u, (-2, 0), (result, lambda: y_lo(ha, h, ps[7], S, 0, 1, lambda e: 1.0)))

            steps = {**{u: [lambda u=u: start_tiles(NS + u)] for u in range(NS)}, 8: [parameters], 10: [more_parameters]}
            diff_begin(steps, 10, Head(0, 0, 0))
            turn("in_b", 0, 16, steps, WH)
            with dve.Fori(1, 4) as i:
                steps = {}
                diff_end(steps, 2, Head(i, -2, 2))
                diff_begin(steps, 2, Head(i, -1, 2))
                diff_end(steps, 10, Head(i, -1, 2))
                diff_begin(steps, 10, Head(i, 0, 2))
                turn("in_b", i, 16, steps, WH)
            steps = {}
            diff_end(steps, 2, Head(0, 6, 0))
            diff_begin(steps, 2, Head(0, 7, 0))
            diff_end(steps, 10, Head(0, 7, 0))
            dil_begin(steps, 10, Head(0, 0, 0))
            turn("in_a", 0, 16, steps, WH)
            with dve.Fori(1, 4) as i:
                steps = {}
                dil_end(steps, 2, Head(i, -2, 2))
                dil_begin(steps, 2, Head(i, -1, 2))
                dil_end(steps, 10, Head(i, -1, 2))
                dil_begin(steps, 10, Head(i, 0, 2))
                turn("in_a", i, 16, steps, WH)

            def add_in_place(name, i, g, units):
                dve.wait_ge(*multiplied(name, i, units * (g + 1), 2 * units))
                for t in range(NT):
                    c = ds(at(i, g * W, 2 * W), W)
                    v.tensor_tensor(x[:, t, c], x[:, t, c], pair[g][t][:], ALU.add).then_inc(by_dve, 1)

            for i in range(2):
                steps = {}
                if i == 0:
                    dil_end(steps, 2, Head(0, 6, 0))
                    dil_begin(steps, 1, Head(0, 7, 0))
                    dil_end(steps, LAST_DIL_STEPS[-1], Head(0, 7, 0))
                for g in range(2):
                    add_steps(steps, 4 * g, (3,), (lambda g=g: add_in_place("out_b", i, g, 4),))
                turn("out_b", i, 8, steps)

            def add_fresh(name, i, g, e, units):
                dve.wait_ge(*multiplied(name, i, units * (g + 1), 2 * units))
                dve.wait_ge(x_kept, at(i, FREE + 4 * e, 2))
                dve.wait_ge(part_sq, at(i, FREE + 8 * e, 4))
                for t in range(NT):
                    v.tensor_tensor(fresh[g][:, t, :], x[:, t, ds(at(i, g * W, 2 * W), W)], pair[g][t][:], ALU.add).then_inc(by_dve, 1)

            def x_lo(i, g, base, hi, lo, gain0):
                for j in range(4):
                    dve.wait_ge(kt_hi, at(i, base + 4 * g + j // 2 * 2 + 2, 8))
                    c = ds(at(i, (4 * g + j) * S, 8 * S), S)
                    scale = 0.5 if gain0 is None else gain[:, ds(at(i, gain0 + 4 * g + j, 8), 1)]
                    v.scalar_tensor_tensor(lo[:, c], ps[4 + 2 * g + j // 2][:, j % 2 * S:(j % 2 + 1) * S], scale, f32(hi[:, c]),
                                           ALU.mult, ALU.subtract).then_inc(kt_lo, 1)

            def residual(name, units, base, hi, lo, gain0, add, first=(), tail={}):
                for i in range(2):
                    steps = {1: first if i == 0 else [lambda: x_lo(0, 1, base, hi, lo, gain0)],
                             units - 1: [lambda: add(i, 0)], units + 1: [lambda: x_lo(i, 0, base, hi, lo, gain0)],
                             2 * units - 1: [lambda: add(i, 1)]}
                    turn(name, i, 2 * units, {**steps, **tail} if i == 0 else steps)
                return lambda: x_lo(1, 1, base, hi, lo, gain0)

            def sum_squares(e):
                dve.wait_ge(part_sq, FREE + 8 * (e + 1))
                v.tensor_reduce(ss[:], part_ss[:], X, ALU.add).then_inc(ss_ready, 1)

            rest = residual("out_a", 4, KT, xT_hi, xT_lo, G_FFN, lambda i, g: add_fresh("out_a", i, g, 0, 4))

            def rstd_diag(n):
                dve.wait_ge(rstd_ready, n)
                for t in range(NT):
                    v.tensor_scalar(diag[:, t, :], ident[:], rstd[:, t:t + 1], None, ALU.mult).then_inc(r_diag, 1)

            def ffn(name, hi, lo, fg0, conv_too, n_norm, n_rstd, e, rest, last):
                r_both = r_bc.unsqueeze(1).to_broadcast([P, 2, S])

                def copy_r():
                    dve.wait_ge(r_bc_T, n_norm)
                    v.tensor_copy(r_bc, ps[4][:, 0:S]).then_inc(r_bc_ready, 1)
                    dve.wait_ge(r_bc_ready, n_norm)
                for t, width in enumerate(THIRDS):
                    up, down, n_fg, units = f"{name}_up{t}", f"{name}_down{t}", width // W, width // (UK * P)
                    f0 = fg0 - (FF // W if conv_too else 0)

                    def scaled(i, g, dst, factor):
                        dve.wait_ge(*multiplied(up, i, 8 * (g + 1), 16))
                        for b in range(2):
                            o = dst[:, 2 * b:2 * b + 2, PAD:PAD + S] if conv_too else dst[:, 2 * b:2 * b + 2, :]
                            v.tensor_tensor(o, pair[g][b][:].rearrange("p (f s) -> p f s", f=2), factor(b), ALU.mult).then_inc(by_dve, 1)

                    def convolve(i, g, u, z, j):
                        tap = 2 - j
                        for f in range(4):
                            if j == 1:
                                dve.wait_ge(conv_start, at(i, 8 * f0 + 4 * g + f + 1, 8))
                            else:
                                dve.wait_ge(conv_step, at(i, 16 * f0 + 8 * g + f + 1, 16))
                            w = conv[:, ds(at(i, 4 * f0 + f + g * (CONV_T // 2) + tap * CONV_T, 4), 1)]
                            v.scalar_tensor_tensor(z[:, f, :], u[:, f, tap:tap + S], w, z[:, f, :], ALU.mult, ALU.add).then_inc(conv_step, 1)

                    def silu(i):
                        dve.wait_ge(tanh_ready, at(i, fg0 + 1, 1))
                        v.scalar_tensor_tensor(gate_z, tanh_z, 1.0, gate_z, ALU.add, ALU.mult).then_inc(silu_step, 1)
                        dve.wait_ge(silu_step, at(i, 2 * fg0 + 1, 2))
                        if not conv_too:
                            r4 = r_bc.unsqueeze(1).to_broadcast([P, 4, S])
                            v.tensor_tensor(gate_z, gate_z, r4, ALU.mult).then_inc(silu_step, 1)
                            dve.wait_ge(silu_step, at(i, 2 * fg0 + 2, 2))

                    def act_lo_part(i):
                        dve.wait_ge(act_hi, at(i, fg0 + 1, 1))
                        c = ds(at(i, 0, 4 * S), 4 * S)
                        v.scalar_tensor_tensor(tiles4(lo[:, c], S), up_z, 0.5, tiles4(f32(hi[:, c]), S), ALU.mult, ALU.subtract).then_inc(act_lo, 1)

                    def product(i):
                        dve.wait_ge(conv_step, at(i, 16 * f0 + 16, 16))
                        v.tensor_tensor(up_z, up_z, gate_z, ALU.mult).then_inc(silu_step, 1)

                    def own_parts(i):
                        if conv_too:
                            return {7: [lambda: scaled(i, 0, gate_u, lambda b: r_both)], 8: [lambda: convolve(i, 0, gate_u, gate_z, 1)],
                                    9: [lambda: convolve(i, 0, gate_u, gate_z, 2)], 12: [lambda: silu(i)],
                                    ("before", 15): [lambda: scaled(i, 1, up_u, lambda b: r_both)],
                                    15: [lambda: convolve(i, 1, up_u, up_z, 1), lambda: convolve(i, 1, up_u, up_z, 2), lambda: product(i)]}
                        return {7: [lambda: scaled(i, 0, gate_z, lambda b: r_both)], 9: [lambda: silu(i)],
                                15: [lambda: scaled(i, 1, up_z, lambda b: gate_z[:, 2 * b:2 * b + 2, :])]}

                    def late_parts(i):
                        return {0: [lambda: act_lo_part(i)]}
                    norm = {1: [rest, lambda: sum_squares(e)], 3: [lambda: rstd_diag(n_rstd)], 5: [copy_r]} if t == 0 else {}
                    turn(up, 0, 16, {**norm, **own_parts(0)})
                    with dve.Fori(1, n_fg) as i:
                        turn(up, i, 16, {**late_parts(i - 1), **own_parts(i)})
                    tail = late_parts(n_fg - 1)
                    if t == 0:
                        tail[0].append(lambda: dve.wait_ge(x_kept, FREE + 4 * (e + 1)))
                    if t == 2:
                        return last(down, units, tail)
                    plain(down, units, tail)
                    fg0 += n_fg

            def plain(name, units, tail, ahead=True):
                for i in range(2):
                    steps = {units - 1: [lambda: add_in_place(name, i, 0, units)], 2 * units - 1: [lambda: add_in_place(name, i, 1, units)]}
                    turn(name, i, 2 * units, {**steps, **tail} if i == 0 else steps, ahead=ahead or i == 0)

            rest = ffn(
                "ffn1", yT_hi, yT_lo, 0, False, 1, 2, 0, rest,
                lambda name, units, tail: residual(name, units, 2 * KT, xT_hi, xT_lo, G_NORM1,
                                                   lambda i, g: add_fresh(name, i, g, 1, units), tail=tail))

            def gate_w_part():
                dve.wait_ge(gate_hi, 1)
                v.tensor_tensor(gate_w_lo[:], gate_w[:], f32(gate_w_hi[:]), ALU.subtract).then_inc(gate_lo, 1)

            def x2(t):
                if t == 0:
                    dve.wait_ge(x_kept, FREE + 8)
                    dve.wait_ge(final_landed, 16)
                    dve.wait_ge(rstd_ready, 3)
                v.scalar_tensor_tensor(x[:, t, :], x[:, t, :], rstd[:, t:t + 1], gain_final_bc, ALU.mult, ALU.mult).then_inc(x2_ready, 1)
            turn("in_m", 0, 16, {1: [rest, lambda: sum_squares(1)], 2: [gate_w_part], 3: [lambda: x2(0)], 5: [lambda: x2(1)]})
            turn("in_m", 1, 16)

            I_COL, MF_COL = HEADS, HEADS + M_HEADS

            def gates_bias():
                dve.wait_ge(gates_evac, 2)
                v.tensor_tensor(gz[:], gz[:], gate_bias[:].unsqueeze(1).to_broadcast([P, NT, NG]), ALU.add).then_inc(gates_step, 1)
                dve.wait_ge(gates_step, 1)
                v.scalar_tensor_tensor(gt[:], gz[:], -1.0, gz[:], ALU.mult, ALU.max).then_inc(gates_step, 1)

            def log_sigmoid():
                dve.wait_ge(gates_act, 2)
                v.scalar_tensor_tensor(lf[:], gz[:], 0.0, gt[:], ALU.min, ALU.subtract).then_inc(log_f, 1)

            def decays():
                dve.wait_ge(cum_done, 1)
                v.tensor_copy(f_sum[:], ps[5][:, 0:2 * NG].rearrange("p (t n) -> p t n", t=NT)).then_inc(cum_read, 1)
                dve.wait_ge(cum_read, 1)
                v.tensor_tensor(a_gate[:], gz[:, :, I_COL:I_COL + M_HEADS], f_sum[:, :, MF_COL:NG], ALU.subtract).then_inc(decay_ready, 1)
                dve.wait_ge(decay_ready, 1)
            turn("in_m", 2, 16, {4: [gates_bias], 6: [log_sigmoid], 8: [decays]})

            with dve.Fori(0, 4) as i:
                h = Head(i, 0, 1)

                def decay_diag():
                    for t in range(NT):
                        v.tensor_scalar(diag[:, t, :], ident[:], a_gate[:, t, ds(h.num(), 1)], None, ALU.mult).then_inc(diag_ready, 1)

                def decay_max():
                    dve.wait_ge(decay_bc, h.upto())
                    for t, c, n in ((0, 0, P), (1, P, S)):
                        v.tensor_tensor(mix[:, c:c + n], ps[5][:, 0:n], causal[:, c:c + n], ALU.add).then_inc(hm.masked, 1)
                    for t, c, n in ((0, 0, P), (1, P, S)):
                        dve.wait_ge(hm.masked, h.upto(2, t + 1))
                        v.tensor_reduce(top[:, t:t + 1], mix[:, c:c + n], X, ALU.max).then_inc(hm.raw_max, 1)
                    dve.wait_ge(hm.raw_max, h.upto(2))
                    v.tensor_scalar(neg_max[:, 0, :], top[:], 0.0, -1.0, ALU.max, ALU.mult).then_inc(hm.row_max, 1)

                def weigh():
                    dve.wait_ge(hm.exps, h.upto(2))
                    dve.wait_ge(hm.scores, h.upto())
                    for t, c, n in ((0, 0, P), (1, P, S)):
                        v.tensor_tensor_reduce(out=mix[:, c:c + n], in0=ps[6][:, c:c + n], in1=prob[:, c:c + n], scale=1.0, scalar=0.0,
                                               op0=ALU.mult, op1=ALU.add, accum_out=den[:, 0, t:t + 1]).then_inc(hm.mixed, 1)
                    dve.wait_ge(hm.mixed, h.upto(2))
                    dve.wait_ge(floor_ready, h.upto(2))
                    v.scalar_tensor_tensor(den[:, 1, :], den[:, 0, :], -1.0, den[:, 0, :], ALU.mult, ALU.max).then_inc(den_part, 1)
                    dve.wait_ge(den_part, h.upto(2, 1))
                    v.tensor_tensor(den[:, 0, :], den[:, 1, :], floor[:], ALU.max).then_inc(den_part, 1)
                    dve.wait_ge(den_part, h.upto(2))
                    v.reciprocal(rden[:, 0, :], den[:, 0, :]).then_inc(hm.rden, 1)

                def result():
                    dve.wait_ge(hm.rstd, h.upto())
                    v.scalar_tensor_tensor(coef[:], rden[:, 0, :], M_DV ** 0.5, head_rstd[:, 0:NT], ALU.mult, ALU.mult).then_inc(hm.coef, 1)
                    dve.wait_ge(hm.coef, h.upto())
                    for t in range(NT):
                        v.tensor_scalar(h_norm[:, t, :], ps[7][:, t * M_DV:(t + 1) * M_DV], coef[:, t:t + 1], None, ALU.mult).then_inc(norm_step, 1)
                    for t in range(NT):
                        dve.wait_ge(norm_step, h.upto(2, t + 1))
                        v.scalar_tensor_tensor(y[:, t, :], z1[:, t, ds(h.num(M_DV, D), M_DV)], 1.0, h_norm[:, t, :], ALU.add, ALU.mult).then_inc(hm.y, 1)
                u_y = MLSTM_STEPS[-1]
                turn("in_f", i, 16, {
                    0: [decay_diag], 3: [decay_max], 5: [weigh], u_y - 2: [result],
                    u_y: [lambda: y_lo(hm, h, ps[4], 0, HEADS, 2, lambda e: gain[:, ds(h.num(2, G_M + e), 1)])]}, WH)

            def fox(steps, u0, h, at_units):
                def forget_diag():
                    for t in range(NT):
                        v.tensor_scalar(diag[:, t, :], ident[:], f_sum[:, t, ds(h.num(), 1)], -1.0, ALU.mult, ALU.mult).then_inc(diag_ready, 1)

                def masked_max():
                    dve.wait_ge(hf.scores, h.upto())
                    for t, c, n in ((0, 0, P), (1, P, S)):
                        v.scalar_tensor_tensor(mix[:, c:c + n], ps[6][:, c:c + n], f_sum[:, t, ds(h.num(), 1)], causal[:, c:c + n],
                                               ALU.add, ALU.add).then_inc(hf.masked, 1)
                    for t, c, n in ((0, 0, P), (1, P, S)):
                        dve.wait_ge(hf.masked, h.upto(2, t + 1))
                        v.tensor_reduce(neg_max[:, 0, t:t + 1], mix[:, c:c + n], X, ALU.max, negate=True).then_inc(hf.raw_max, 1)

                def result():
                    dve.wait_ge(hf.exps, h.upto(2))
                    v.reciprocal(rden[:, 0, :], den[:, 0, :]).then_inc(hf.rden, 1)
                    dve.wait_ge(hf.rden, h.upto())
                    dve.wait_ge(hf.pv, h.upto())
                    y_out(hf, h, P, rden[:, 0])
                _, u_s, _, u_v, u_y = at_units
                add_steps(steps, u0, (0, u_s, u_v, u_y), (
                    forget_diag, masked_max, result, lambda: y_lo(hf, h, ps[7], S, 0, 1, lambda e: 1.0)))
            with dve.Fori(0, 4) as i:
                steps = {}
                fox(steps, 0, Head(i, 0, 1), FOX_M_STEPS)

                def merge_m():
                    dve.wait_ge(*multiplied("gate_m", i, 12, 12))
                    dve.wait_ge(by_act, at(i, FREE + PH["gate_m"][BY_ACT] + 2, 2))
                    for t in range(NT):
                        v.scalar_tensor_tensor(merged[:, t, ds(i * W, W)], gm_buf[:, t, :], 1.0, pair[1][t][:], ALU.add, ALU.mult).then_inc(by_dve, 1)
                add_steps(steps, 0, (11,), (merge_m,))
                turn("gate_m", i, 12, steps)
            with dve.Fori(0, 2) as i:
                steps = {}
                for g in range(2):
                    fox(steps, 8 * g, Head(i, 4 + g, 2), FOX_A_STEPS)
                turn("gate_a", i, 16, steps)

            def merge_a(i, g):
                dve.wait_ge(by_act, FREE + PH["gate_a"][BY_ACT] + 4 * i + 2 * g + 2)
                dve.wait_ge(*multiplied("proj_a", i, 4 * (g + 1), 8))
                for t in range(NT):
                    v.scalar_tensor_tensor(fresh[g][:, t, :], ga_buf[2 * i + g][t], 1.0, pair[g][t][:], ALU.add, ALU.mult).then_inc(by_dve, 1)
                for t in range(NT):
                    c = ds(at(i, g * W, 2 * W), W)
                    dve.wait_ge(by_dve, at(i, FREE + PH["proj_a"][BY_DVE] + 2 * g + t + 1, 4))
                    v.tensor_tensor(fresh[g][:, t, :], fresh[g][:, t, :], merged[:, t, c], ALU.add).then_inc(fresh_ready, 1)
            rest = residual("proj_a", 4, 3 * KT, xT_hi, xT_lo, None, merge_a)
            rest = residual("out2", 8, 4 * KT, yT_hi, yT_lo, G_NORM2, lambda i, g: add_fresh("out2", i, g, 2, 8), [rest])
            for u in (gate_u, up_u):
                v.memset(u[:, :, 0:PAD], 0.0).then_inc(pad_set, 1)
            dve.wait_ge(pad_set, 2)

            def last_groups(name, units, tail):
                plain(name, units, tail, ahead=False)
            ffn("ffn2", xT_hi, xT_lo, FF // W, True, 2, 5, 2, rest, last_groups)

        @block.gpsimd
        def _(pool):
            g_ = nc.gpsimd
            g_.memset(ones[:], 1.0).then_inc(const_set, 1)
            g_.memset(minus_half[:], -0.5).then_inc(const_set, 1)
            for dst, eps in ((eps_diff, P * SUBLN_EPS), (eps_mlstm, M_DV * RMS_EPS), (eps_fox, P * RMS_EPS)):
                g_.memset(dst[:], eps).then_inc(const_set, 1)
            for j in range(NS):
                g_.memset(raw[j][:, :, WH:W], 0.0).then_inc(const_set, 1)
            pool.sem_inc(lo_ready, NS)
            pool.sem_inc(slot_used, NS)
            for s in (by_act, by_dve, part_sq, x_kept, *(k for h in (hb, ha, hm, hf) for k in (h.qk_T, h.ms, h.y_lo))):
                pool.sem_inc(s, FREE)
            pool.wait_ge(const_set, N_CONST)

            def factor(n, dst):
                g_.tensor_scalar(ms[:], ss[:], 1.0 / D, RMS_EPS, ALU.mult, ALU.add).then_inc(ms_ready, 1)
                pool.wait_ge(ms_ready, n)
                return g_.tensor_tensor(dst[:], ms[:], minus_half[:, 0:NT], ALU.pow)

            pool.wait_ge(x_sq, 2)
            factor(1, rstd).then_inc(rstd_ready, 1)

            def rope_head(s, h, phase, z, table, heads4, rot):
                half = rot // 2
                pool.wait_ge(by_act, h.num(2, FREE + PH[phase][BY_ACT] + 2))
                pool.wait_ge(s.qk_T, h.num(1, FREE))
                g_.tensor_copy(stage[:].rearrange("p t c n -> p t (c n)"), z[:, :, ds(h.num(WH), 2 * P)]).then_inc(s.rope, 1)
                pool.wait_ge(s.rope, h.upto(4, 1))
                r = stage[:].rearrange("p t c (e n) -> p (t c e) n", e=heads4)
                u = rot_u[:].rearrange("p (k n) -> p k n", n=rot)
                w = rot_v[:].rearrange("p (k n) -> p k n", n=rot)
                g_.tensor_tensor(u, r[:, :, 0:rot], table[:, 0], ALU.mult).then_inc(s.rope, 1)
                g_.tensor_tensor(w[:, :, 0:half], r[:, :, half:rot], table[:, 1, :, 0:half], ALU.mult).then_inc(s.rope, 1)
                g_.tensor_tensor(w[:, :, half:rot], r[:, :, 0:half], table[:, 1, :, half:rot], ALU.mult).then_inc(s.rope, 1)
                pool.wait_ge(s.rope, h.upto(4))
                g_.tensor_tensor(r[:, :, 0:rot], u, w, ALU.add).then_inc(s.staged, 1)

            def head_factor(s, h, n, sq, eps):
                pool.wait_ge(s.sq, h.upto(sq))
                g_.tensor_tensor(head_ms[:, 0:n], head_ss[:, 0:n], eps[:, 0:n], ALU.add).then_inc(s.ms, 1)
                pool.wait_ge(s.ms, h.num(1, FREE + 1))
                g_.tensor_tensor(head_rstd[:, 0:n], head_ms[:, 0:n], minus_half[:, 0:n], ALU.pow).then_inc(s.rstd, 1)

            pool.wait_ge(small_landed, 16 * N_SMALL)
            with pool.Fori(0, 8) as i:
                h = Head(i, 0, 1)
                rope_head(hb, h, "in_b", z1, rope_b, 2, 16)
                head_factor(hb, h, NT, 2, eps_diff)
            pool.wait_ge(hb.qk_T, FREE + HEADS)
            with pool.Fori(0, 8) as i:
                rope_head(ha, Head(i, 0, 1), "in_a", z2, rope_a, 1, 32)

            def keep(name):
                with pool.Fori(0, 2) as i:
                    for g in range(2):
                        pool.wait_ge(by_dve, at(i, FREE + PH[name][BY_DVE] + 2 * g + 2, 4))
                        g_.tensor_copy(x[:, :, ds(i * (2 * W) + g * W, W)], fresh[g]).then_inc(x_kept, 1)
            keep("out_a")
            pool.wait_ge(ss_ready, 1)
            factor(2, rstd).then_inc(rstd_ready, 1)
            keep("ffn1_down2")
            pool.wait_ge(ss_ready, 2)
            factor(3, rstd).then_inc(rstd_ready, 1)

            pool.wait_ge(x_sq, 4)
            factor(4, rstd_n).then_inc(norm1_step, 1)
            pool.wait_ge(norm1_step, 1)
            g_.tensor_tensor(rstd2[:], rstd[:], rstd_n[:], ALU.mult).then_inc(norm1_step, 1)
            pool.wait_ge(norm1_step, 2)
            g_.tensor_scalar(half_rstd2[:], rstd2[:], 0.5, None, ALU.mult).then_inc(rstd_ready, 1)
            pool.wait_ge(by_act, FREE + PH["in_f"][BY_ACT])
            pool.wait_ge(ha.qk_T, FREE + HEADS)
            with pool.Fori(0, 4) as i:
                h = Head(i, 0, 1)
                pool.wait_ge(hm.qk_T, h.num(1, FREE))
                src = z1[:, :, 0:2 * M_HEADS * P].rearrange("p t (c n) -> p t c n", c=2)[:, :, :, ds(h.num(P), P)]
                g_.tensor_copy(stage[:], src).then_inc(hm.staged, 1)
                head_factor(hm, h, NT, 2, eps_mlstm)
            pool.wait_ge(hm.qk_T, FREE + M_HEADS)
            with pool.Fori(0, 8) as i:
                h = Head(i, 0, 1)
                head_factor(hf, h, 4, 4, eps_fox)
                pool.wait_ge(hf.rstd, h.upto())
                pool.wait_ge(hf.qk_T, h.num(1, FREE))
                z = z2[:, :, :].rearrange("p t (c n) -> p t c n", c=3)[:, :, 0:2, ds(h.num(P), P)]
                r = head_rstd[:].rearrange("p (t c) -> p t c", t=NT).unsqueeze(3).to_broadcast([P, NT, 2, P])
                g_.tensor_tensor(stage[:], z, r, ALU.mult).then_inc(hf.staged, 1)
            keep("out2")
            pool.wait_ge(ss_ready, 3)
            factor(5, rstd).then_inc(rstd_ready, 1)


_INS = ['x', 'norm_attn', 'w_in', 'lambda_qk', 'subln', 'w_out', 'norm_ffn', 'w_gate', 'w_up', 'w_down', 'norm_final',
        'norm1_g_2', 'w_in_2', 'fox_f_bias_2', 'q_norm_g_2', 'k_norm_g_2', 'm_i_bias_2', 'm_f_bias_2', 'm_norm_g_2',
        'w_proj_a_2', 'w_proj_m_2', 'w_out_2', 'norm2_g_2', 'w_up_2', 'conv_w_2', 'conv_b_2', 'w_down_2']


def _tables():
    import numpy as np
    f = np.float32
    tok = np.arange(S)
    far = f(-1e30)
    dist = tok[:, None] - tok[None, :]
    count = (np.abs(dist) <= 64).astype(f) + (dist % 4 == 0) + (dist % 16 == 0)
    log_count = np.where(count > 0, np.log(np.maximum(count, 1)), far).astype(f)
    mask = np.where(dist >= 0, f(0), far).astype(f)

    def by_tile(m):
        return m.reshape(NT, P, -1).transpose(1, 0, 2)

    def rope(rot, copies):
        inv = np.power(f(500000.0), -np.arange(0, rot, 2, dtype=f) / f(rot), dtype=f)
        ang = tok.astype(f)[:, None] * inv[None, :]
        c, s = np.cos(ang), np.sin(ang)
        both = [np.concatenate([c, c], 1), np.concatenate([-s, s], 1)]
        return np.stack([np.repeat(by_tile(b)[:, :, None], copies, 2).reshape(P, NT * copies, rot) for b in both], 1).astype(f)

    return {
        "c_ident": np.eye(P, dtype=f),
        "c_tri": np.triu(np.ones((P, P), f)),
        "c_causal": np.ascontiguousarray(np.concatenate([mask[:P, :P], mask[P:, :]], 1)),
        "c_count": np.ascontiguousarray(by_tile(log_count)),
        "c_rope_a": np.ascontiguousarray(rope(32, 2)),
        "c_rope_b": np.ascontiguousarray(rope(16, 4)),
    }


def kernel(**inputs):
    import numpy as np
    import concourse.bacc as bacc
    from concourse.bass_utils import run_bass_kernel_spmd

    nc = bacc.Bacc("TRN2", target_bir_lowering=False, num_devices=1)
    arrays = {f"in_{name}": np.ascontiguousarray(inputs[name]) for name in _INS}
    arrays.update(_tables())
    aps = {}
    for name, v in arrays.items():
        aps[name.removeprefix("in_")] = nc.dram_tensor(name, v.shape, mybir.dt.from_np(v.dtype), kind="ExternalInput").ap()
    out = nc.dram_tensor("out_x", (1, S, D), F32, kind="ExternalOutput").ap()
    two_blocks(nc, aps, out)
    r = run_bass_kernel_spmd(nc, [arrays], core_ids=[0])
    return r.results[0]["out_x"]
```

```python
from contextlib import ExitStack
import math

import concourse.bass as bass
from concourse import mybir

F32 = mybir.dt.float32
F32R = mybir.dt.float32r
ALU = mybir.AluOpType
ACT = mybir.ActivationFunctionType
X = mybir.AxisListType.X

P = 128
D = 2048
S = 256
NT = S // P
KT = D // P
HEADS = 8
M_HEADS = 4
M_DV = 256
HALF = HEADS * P
FF = 5632
RMS_EPS = 1e-6
SUBLN_EPS = 1e-5
LAM_INIT = 0.8 - 0.6 * math.exp(-0.3 * 0)
B_SCALE = 64 ** -0.5
HEAD_SCALE = 128 ** -0.5

UK = 2
W = 512
NS = 4
WH = 384
C3 = 3 * HALF
THIRDS = (2048, 2048, FF - 4096)

OFF_GATES_F = C3
OFF_M = OFF_GATES_F + HEADS
OFF_GATES_IF = OFF_M + C3
OFF_GA = OFF_GATES_IF + 2 * M_HEADS
OFF_GM = OFF_GA + D
NG = HEADS + 2 * M_HEADS

G_ATTN, G_FFN, G_FINAL, G_NORM1, G_NORM2 = (KT * j for j in range(5))
G_SUBLN, G_Q, G_K, G_M = 5 * KT, 5 * KT + 1, 5 * KT + 2, 5 * KT + 3
N_GAIN = G_M + 2 * M_HEADS
CONV_T = 2 * FF // P


def plan():
    phases, unit, by_act, by_dve = {}, 0, 0, 0

    def add(name, units, act, dve):
        nonlocal unit, by_act, by_dve
        phases[name] = (unit, by_act, by_dve)
        unit, by_act, by_dve = unit + units, by_act + act, by_dve + dve

    def ffn(name):
        for t, width in enumerate(THIRDS):
            n = width // W
            add(f"{name}_up{t}", 16 * n, 0, 4 * n)
            add(f"{name}_down{t}", 4 * (width // (UK * P)), 0, 8)

    add("in_b", 64, 16, 0)
    add("in_a", 64, 16, 0)
    add("out_b", 16, 0, 8)
    add("out_a", 16, 0, 8)
    ffn("ffn1")
    add("in_m", 48, 12, 0)
    add("in_f", 64, 16, 0)
    add("gate_m", 48, 8, 8)
    add("gate_a", 32, 8, 0)
    add("proj_a", 16, 0, 8)
    add("out2", 32, 0, 8)
    ffn("ffn2")
    add("end", 0, 0, 0)
    return phases


PH = plan()
HEAD_STEPS = (0, 1, 4, 5, 8)
LAST_DIL_STEPS = (1, 2, 4, 5, 7)
MLSTM_STEPS = (1, 3, 7, 8, 12)
FOX_M_STEPS, FOX_A_STEPS = (2, 3, 6, 7, 9), (2, 3, 5, 6, 7)
N_SPLIT = PH["out_b"][0] + NS
N_CONST = 5 + NS
N_SMALL = 21
X_BEHIND = (0, 2, 3)
START_BANKS = (4, 5, 6, 7, 2, 3, 4, 5)
FREE = 3


def at(i, c, step):
    return c if i is None else i * step + c


class Head:

    def __init__(self, i, first, per):
        self.i, self.first, self.per = i, first, per

    def num(self, scale=1, c=0):
        return at(self.i, self.first * scale + c, self.per * scale)

    def upto(self, n=1, k=None):
        return self.num(n, n if k is None else k)


class HeadSems:

    def __init__(self, sem, kind):
        self.staged = sem(kind + "_staged")
        self.rope = sem(kind + "_rope")
        self.qk_T = sem(kind + "_qk_T")
        self.qkT = sem(kind + "_qkT")
        self.scores = sem(kind + "_scores")
        self.masked = sem(kind + "_masked")
        self.raw_max = sem(kind + "_raw_max")
        self.row_max = sem(kind + "_row_max")
        self.exps = sem(kind + "_exps")
        self.rden = sem(kind + "_rden")
        self.coef = sem(kind + "_coef")
        self.mixed = sem(kind + "_mixed")
        self.p_T = sem(kind + "_p_T")
        self.pT = sem(kind + "_pT")
        self.pv = sem(kind + "_pv")
        self.sq = sem(kind + "_sq")
        self.ms = sem(kind + "_ms")
        self.rstd = sem(kind + "_rstd")
        self.y = sem(kind + "_y")
        self.y_T = sem(kind + "_y_T")
        self.y_hi = sem(kind + "_y_hi")
        self.y_lo = sem(kind + "_y_lo")


def two_blocks(nc, a, out):
    ctx = ExitStack()
    with ctx:
        def sb(name, shape, dt=F32):
            return ctx.enter_context(nc.sbuf_tensor(name, [P, *shape], dt))

        def sem(name):
            return ctx.enter_context(nc.semaphore(name))

        x = sb("x", [NT, D])
        xT_hi, xT_lo = sb("xT_hi", [KT * S], F32R), sb("xT_lo", [KT * S], F32R)
        yT_hi, yT_lo = sb("yT_hi", [KT * S], F32R), sb("yT_lo", [KT * S], F32R)
        raw = [sb(f"raw{j}", [UK, W]) for j in range(NS)]
        w_hi = [sb(f"w_hi{j}", [UK, W], F32R) for j in range(NS)]
        w_lo = [sb(f"w_lo{j}", [UK, W], F32R) for j in range(NS)]
        z1, z2 = sb("z1", [NT, C3]), sb("z2", [NT, C3])
        ident, tri, ones = sb("ident", [P]), sb("tri", [P]), sb("ones", [P])
        causal = sb("causal", [3 * P])
        ln_count = sb("ln_count", [NT * S])
        rope_a = sb("rope_a", [2, NT * 2, 32])
        rope_b = sb("rope_b", [2, NT * 4, 16])
        gain = sb("gain", [N_GAIN])
        gain_qk = sb("gain_qk", [2])
        conv = sb("conv", [4 * CONV_T])
        gate_w = sb("gate_w", [KT, NG])
        gate_w_hi, gate_w_lo = sb("gate_w_hi", [KT, NG], F32R), sb("gate_w_lo", [KT, NG], F32R)
        gate_bias = sb("gate_bias", [NG])
        lam_t, minus_lam = sb("lam_t", [8]), sb("minus_lam", [1])
        minus_half = sb("minus_half", [NG])
        stage = sb("stage", [NT, 2, P])
        rot_u, rot_v = sb("rot_u", [P]), sb("rot_v", [P])
        qkT = sb("qkT", [2, S])
        prob = sb("prob", [NT * 2 * S])
        mix = sb("mix", [NT * S])
        pT = sb("pT", [2 * S])
        y = sb("y", [NT, S])
        junk = sb("junk", [W])
        neg_max, top = sb("neg_max", [NT, 2]), sb("top", [NT])
        den, rden = sb("den", [2, NT]), sb("rden", [2, NT])
        coef, floor = sb("coef", [NT]), sb("floor", [NT])
        head_ss, head_ms, head_rstd = sb("head_ss", [4]), sb("head_ms", [4]), sb("head_rstd", [4])
        eps_diff, eps_mlstm, eps_fox = (sb(n, [4]) for n in ("eps_diff", "eps_mlstm", "eps_fox"))
        part_ss = sb("part_ss", [NT, 4])
        ss, ms = sb("ss", [NT]), sb("ms", [NT])
        rstd, rstd_n, rstd2, half_rstd2 = sb("rstd", [NT]), sb("rstd_n", [NT]), sb("rstd2", [NT]), sb("half_rstd2", [NT])
        r_bc = prob[:, 0:S]
        diag = sb("diag", [NT, P])
        gz, lf, f_sum = sb("gz", [NT, NG]), sb("lf", [NT, NG]), sb("f_sum", [NT, NG])
        gt, a_gate = sb("gt", [NT, NG]), sb("a_gate", [NT, M_HEADS])
        gates_T = y[0:NG, 0, :]
        h_norm = prob[:, 2 * S:4 * S].rearrange("p (t n) -> p t n", t=NT)
        ps = [ctx.enter_context(nc.psum_tensor(f"ps{j}", [P, W], F32)) for j in range(8)]
        pair = (ps[0:2], ps[2:4])

        z1f, z2f = (z[:, :, :].rearrange("p t n -> p (t n)") for z in (z1, z2))
        PAD = 2

        def tiles4(v, n):
            return v.rearrange("p (f s) -> p f s", f=4, s=n)
        gate_u = tiles4(z1f[:, 0:4 * (S + PAD)], S + PAD)
        up_u = tiles4(z1f[:, 4 * (S + PAD):8 * (S + PAD)], S + PAD)
        gate_z = tiles4(z1f[:, 8 * (S + PAD):8 * (S + PAD) + 4 * S], S)
        up_z = tiles4(z2f[:, 0:4 * S], S)
        tanh_z = tiles4(z2f[:, 4 * S:8 * S], S)
        gain_final_bc = z2f[:, 8 * S:8 * S + D]
        fresh = [z2f[:, 2 * D + g * NT * W:2 * D + (g + 1) * NT * W].rearrange("p (t n) -> p t n", t=NT) for g in range(2)]
        merged = z1f[:, 0:NT * D].rearrange("p (t n) -> p t n", t=NT)
        gm_buf = z1f[:, NT * D:NT * (D + W)].rearrange("p (t n) -> p t n", t=NT)
        ga_buf = [[z2[:, 0, 0:W], z2[:, 1, 0:W]], [z2[:, 0, HALF:HALF + W], z2[:, 0, 2 * HALF:2 * HALF + W]],
                  [z1f[:, NT * (D + W):][:, t * W:(t + 1) * W] for t in range(NT)], [gm_buf[:, t, :] for t in range(NT)]]
        conv_rows = z2f[0:CONV_T, 0:4 * P].rearrange("p (j c) -> p j c", j=4)
        lam_in = z2f[:, 4 * P:6 * P].rearrange("p (j c) -> p j c", j=4)
        lam_prod = z2f[:, 6 * P:7 * P].rearrange("p (j c) -> p j c", j=2)
        gain_rows = z2f[:, 7 * P:9 * P].rearrange("p (j c) -> p j c", j=2)
        sq_out0, sq_out1 = (v[:, D:3 * D].rearrange("p (t n) -> p t n", t=NT) for v in (z2f, z1f))

        raw_landed = [sem(f"raw_landed{j}") for j in range(NS)]
        hi_ready, lo_ready = sem("hi_ready"), sem("lo_ready")
        slot_used = sem("slot_used")
        by_act, by_dve = sem("evac_by_act"), sem("evac_by_dve")
        x_landed = [sem(f"x_landed{j}") for j in range(4)]
        rows_landed, ident_landed = sem("rows_landed"), sem("ident_landed")
        small_landed, gate_w_landed, final_landed = sem("small_landed"), sem("gate_w_landed"), sem("final_landed")
        const_set = sem("const_set")
        rows_T, gain_ready, gain_step = sem("rows_T"), sem("gain_ready"), sem("gain_step")
        kt_T, kt_hi, kt_lo = sem("kt_T"), sem("kt_hi"), sem("kt_lo")
        x_sq, part_sq, ss_ready = sem("x_sq"), sem("part_sq"), sem("ss_ready")
        ms_ready, rstd_ready, norm1_step = sem("ms_ready"), sem("rstd_ready"), sem("norm1_step")
        x_kept, fresh_ready = sem("x_kept"), sem("fresh_ready")
        lam_step, lam_exp, lam_ready = sem("lam_step"), sem("lam_exp"), sem("lam_ready")
        r_diag, r_bc_T, r_bc_ready = sem("r_diag"), sem("r_bc_T"), sem("r_bc_ready")
        tanh_ready, silu_step, act_hi, act_lo = sem("tanh_ready"), sem("silu_step"), sem("act_hi"), sem("act_lo")
        conv_start, conv_step, pad_set = sem("conv_start"), sem("conv_step"), sem("pad_set")
        gate_hi, gate_lo = sem("gate_hi"), sem("gate_lo")
        gates_done, gates_evac, gates_step, gates_act, log_f = (sem(n) for n in (
            "gates_done", "gates_evac", "gates_step", "gates_act", "log_f"))
        cum_done, cum_read, decay_ready = sem("cum_done"), sem("cum_read"), sem("decay_ready")
        diag_ready, decay_bc, den_part, floor_ready = sem("diag_ready"), sem("decay_bc"), sem("den_part"), sem("floor_ready")
        norm_step, gates_copied = sem("norm_step"), sem("gates_copied")
        x2_ready, warm = sem("x2_ready"), sem("warm")
        stored = sem("stored")
        hb, ha, hm, hf = (HeadSems(sem, k) for k in ("diff", "dil", "mlstm", "fox"))

        block = ctx.enter_context(nc.Block())
        ds = bass.ds

        def rows(w, k0=0, k1=None):
            r = w[k0:w.shape[0] if k1 is None else k1].rearrange("(u k p) n -> u p k n", k=UK, p=P)
            return [r[j] for j in range(r.shape[0])]

        def nothing(u):
            pass

        def multiplied(name, i, units, step):
            return slot_used, at(i, NS + PH[name][0] + units, step)

        def evac_free(sem_, name, col, i, g):
            return sem_, at(i, FREE + PH[name][col] + 2 * g - 2, 4)

        BY_ACT, BY_DVE = 1, 2
        SUMMED = {base: PH[name][BY_DVE] for base, name in ((KT, "out_a"), (2 * KT, "ffn1_down2"), (4 * KT, "out2"))}
        CAUSAL_COLS = ((0, 0, P), (1, P, S))

        @block.sync
        def _(sp):
            sp.dma_start(gain_rows[0:KT, 0, :], a["norm_attn"][0].rearrange("(k c) -> k c", c=P)).then_inc(rows_landed, 16)
            sp.dma_start(ident[:], a["c_ident"]).then_inc(ident_landed, 16)
            x_in = a["x"][0].rearrange("(t p) n -> p t n", p=P)

            def load_x(j):
                cols = slice(j * W, (j + 1) * W)
                sp.dma_start(x[:, :, cols], x_in[:, :, cols]).then_inc(x_landed[j], 16)
            load_x(0)

            def load(n, i, step, src, width):
                sp.wait_ge(lo_ready, at(i, n + 1, step))
                sp.dma_start(raw[n % NS][:, :, 0:width], src).then_inc(raw_landed[n % NS], 16)

            def heads_turn(name, i, c0, behind=None):
                cols = a["w_in"][0][:, c0:c0 + C3].rearrange("(u k p) (c n) -> u k p c n", k=UK, p=P, c=3)
                n = PH[name][0]
                for g in range(2):
                    for u in range(8):
                        src = [cols[u][k][:, :, ds(at(i, g * P, 2 * P), P)] for k in range(UK)]
                        sp.wait_ge(lo_ready, at(i, n + 1, 16))
                        for k in range(UK):
                            sp.dma_start(raw[n % NS][:, k, 0:WH].rearrange("p (c n) -> p c n", c=3), src[k])\
                              .then_inc(raw_landed[n % NS], 16)
                        n += 1
                        if behind:
                            behind(8 * g + u)

            def stream(name, loops, parts):
                step = sum(len(units) for units, _, _ in parts)
                with sp.Fori(0, loops) as i:
                    n = PH[name][0]
                    for units, col, width in parts:
                        c = col(i)
                        for u in units:
                            src = u[:, :, ds(c, width)]
                            load(n, i, step, src, width)
                            n += 1

            def pairs(name, loops, units, c0, width):
                stream(name, loops, [(units, lambda i, g=g: i * (2 * width) + (c0 + g * width), width) for g in range(2)])

            w_in, w_out, w_in2 = a["w_in"][0], a["w_out"][0], a["w_in_2"][0]
            small = [(gain_rows[j * KT:(j + 1) * KT, 1, :], (a[name] if name == "norm_final" else a[name][0]).rearrange("(k c) -> k c", c=P))
                     for j, name in enumerate(("norm_ffn", "norm_final", "norm1_g_2", "norm2_g_2"))]
            late = G_SUBLN - G_FFN
            small += [(gain_rows[late:late + 1, 1, :], a["subln"]), (gain_rows[late + 1:late + 2, 1, :], a["q_norm_g_2"]),
                     (gain_rows[late + 2:late + 3, 1, :], a["k_norm_g_2"]),
                     (gain_rows[late + 3:late + 3 + 2 * M_HEADS, 1, :], a["m_norm_g_2"][0].rearrange("h (e c) -> (h e) c", c=P)),
                     (rope_a[:], a["c_rope_a"]), (rope_b[:], a["c_rope_b"]),
                     (tri[:], a["c_tri"]), (causal[:], a["c_causal"]),
                     (ln_count[:], a["c_count"].rearrange("p t s -> p (t s)")),
                     (lam_in, a["lambda_qk"][0].partition_broadcast(P)),
                     (gate_bias[:, 0:HEADS], a["fox_f_bias_2"][0].partition_broadcast(P)),
                     (gate_bias[:, HEADS:HEADS + M_HEADS], a["m_i_bias_2"][0].partition_broadcast(P)),
                     (gate_bias[:, HEADS + M_HEADS:NG], a["m_f_bias_2"][0].partition_broadcast(P))]
            small += [(conv_rows[:, j, :], a["conv_w_2"][0, j].rearrange("(k c) -> k c", c=P)) for j in range(3)]
            small += [(conv_rows[:, 3, :], a["conv_b_2"][0].rearrange("(k c) -> k c", c=P))]
            assert len(small) == N_SMALL

            def load_small(u):
                if u in X_BEHIND:
                    load_x(X_BEHIND.index(u) + 1)
                for dst, src in small[4 * (u - NS):4 * (u - NS) + 4] if u >= NS else ():
                    sp.dma_start(dst, src).then_inc(small_landed, 16)
            heads_turn("in_b", 0, C3, load_small)
            with sp.Fori(1, 4) as i:
                heads_turn("in_b", i, C3)
            with sp.Fori(0, 4) as i:
                heads_turn("in_a", i, 0)
            for i in range(2):
                for j in range(8):
                    n = PH["out_b"][0] + j
                    src, c = rows(w_out, HALF, D)[j % 4], (2 * i + j // 4) * W
                    if n < N_SPLIT and i == 0:
                        sp.wait_ge(lo_ready, n + 1)
                        for k in range(UK):
                            sp.dma_start(raw[n % NS][:, k, :], src[:, k, c:c + W]).then_inc(raw_landed[n % NS], 16)
                    else:
                        load(n, i, 8, src[:, :, c:c + W], W)
            pairs("out_a", 2, rows(w_out, 0, HALF), 0, W)
            with nc.allow_non_contiguous_dma("a few gate columns"):
                for c, off, n in ((0, OFF_GATES_F, HEADS), (HEADS, OFF_GATES_IF, 2 * M_HEADS)):
                    sp.dma_start(gate_w[:, :, c:c + n], w_in2[:, off:off + n].rearrange("(k p) n -> p k n", p=P))\
                      .then_inc(gate_w_landed, 16)

            def ffn(name, w_gate, w_up, up0, w_down):
                f0 = 0
                for t, width in enumerate(THIRDS):
                    stream(f"{name}_up{t}", width // W, [
                        (rows(w_gate), lambda i: i * W + f0, W), (rows(w_up), lambda i: i * W + (up0 + f0), W)])
                    pairs(f"{name}_down{t}", 2, rows(w_down, f0, f0 + width), 0, W)
                    f0 += width

            ffn("ffn1", a["w_gate"][0], a["w_up"][0], 0, a["w_down"][0])
            sp.dma_start(gain_final_bc, a["norm_final"].partition_broadcast(P)).then_inc(final_landed, 16)
            pairs("in_m", 3, rows(w_in2), OFF_M, W)
            pairs("in_f", 4, rows(w_in2), 0, WH)
            stream("gate_m", 4, [(rows(w_in2), lambda i: i * W + OFF_GM, W),
                                 (rows(a["w_proj_m_2"][0]), lambda i: (i + 1) * W - W, W)])
            pairs("gate_a", 2, rows(w_in2), OFF_GA, W)
            pairs("proj_a", 2, rows(a["w_proj_a_2"][0]), 0, W)
            pairs("out2", 2, rows(a["w_out_2"][0]), 0, W)
            ffn("ffn2", a["w_up_2"][0], a["w_up_2"][0], FF, a["w_down_2"][0])
            out_v = out[0].rearrange("(t p) n -> p t n", p=P)
            for g in range(4):
                cols = slice(g * W, (g + 1) * W)
                sp.wait_ge(by_dve, FREE + PH["ffn2_down2"][BY_DVE] + 2 * g + 2)
                sp.dma_start(out_v[:, :, cols], x[:, :, cols]).then_inc(stored, 16)
            sp.wait_ge(stored, 16 * 4)

        @block.tensor
        def _(pe):
            def by_token(acc, src, kt, n, k, width, first, last):
                hi, lo = src
                for t in range(NT):
                    q = slice(kt * S + t * P, kt * S + (t + 1) * P)
                    o = acc[t][:, 0:width]
                    pe.matmul(o, hi[:, q], w_hi[n % NS][:, k, 0:width], start=first, stop=False)
                    pe.matmul(o, hi[:, q], w_lo[n % NS][:, k, 0:width], start=False, stop=False)
                    mm = pe.matmul(o, lo[:, q], w_hi[n % NS][:, k, 0:width], start=False, stop=last)
                return mm

            def by_feature(acc, src, kt, n, k, first, last):
                hi, lo = (v[:, kt * S:(kt + 1) * S] for v in src)
                for f in range(4):
                    c = slice(f * P, (f + 1) * P)
                    o = acc[f // 2][:, (f % 2) * S:(f % 2 + 1) * S]
                    pe.matmul(o, w_hi[n % NS][:, k, c], hi, start=first and f % 2 == 0, stop=False)
                    pe.matmul(o, w_hi[n % NS][:, k, c], lo, start=False, stop=False)
                    mm = pe.matmul(o, w_lo[n % NS][:, k, c], hi, start=False, stop=last and f % 2 == 1)
                return mm

            def group(name, i, step, g, units, src, kt0, free, width=W, feature=False, ready=None, behind=nothing, u0=None, also=None):
                u0 = g * units if u0 is None else u0
                pe.wait_ge(*free)
                if also:
                    pe.wait_ge(*also)
                for u in range(units):
                    n = PH[name][0] + u0 + u
                    if ready:
                        ready(u)
                    pe.wait_ge(lo_ready, at(i, NS + n + 1, step))
                    for k in range(UK):
                        j = u * UK + k
                        if feature:
                            mm = by_feature(pair[g], src, kt0 + j, n, k, j == 0, j == units * UK - 1)
                        else:
                            mm = by_token(pair[g], src, kt0 + j, n, k, width, j == 0, j == units * UK - 1)
                    mm.then_inc(slot_used, 1)
                    behind(u0 + u)

            def tiles_ready(base):
                return lambda u: pe.wait_ge(kt_lo, base + UK * (u + 1))

            def turn_qk(s, h):
                pe.wait_ge(s.staged, h.upto())
                if s is hm:
                    pe.wait_ge(hm.y_lo, h.num(2, FREE))
                for c in range(2):
                    for t in range(NT):
                        mm = pe.transpose(ps[4][:, c * S + t * P:c * S + (t + 1) * P], stage[:, t, c, :], ident[:])
                mm.then_inc(s.qk_T, 1)

            def turn_p(s, src, blocks):
                for j, c in enumerate(blocks):
                    mm = pe.transpose(ps[4][:, j * P:(j + 1) * P], src[:, c:c + P], ident[:])
                mm.then_inc(s.p_T, 1)

            def values(s, h, z, col, width, blocks):
                pe.wait_ge(s.pT, h.upto())
                if s is not hm:
                    pe.wait_ge(s.y_lo, h.num(1, FREE))
                for t in range(NT):
                    keys = [kt for kt in range(2) if (t, kt) in blocks]
                    for kt in keys:
                        j = blocks[t, kt]
                        mm = pe.matmul(ps[7][:, t * width:(t + 1) * width], pT[:, j * P:(j + 1) * P],
                                       z[:, kt, ds(col, width)], start=kt == keys[0], stop=kt == keys[-1])
                mm.then_inc(s.pv, 1)

            def turn_y(s, h, bank, c0, tiles):
                pe.wait_ge(s.y, h.upto(2))
                for e in range(tiles):
                    for t in range(NT):
                        c = c0 + e * S + t * P
                        mm = pe.transpose(bank[:, c:c + P], y[:, t, e * P:(e + 1) * P], ident[:])
                mm.then_inc(s.y_T, 1)

            FULL = {(t, kt): 2 * kt + t for t in range(NT) for kt in range(2)}
            FULL_SRC = [t * S + kt * P for kt in range(2) for t in range(NT)]
            CAUSAL = {(0, 0): 0, (1, 0): 1, (1, 1): 2}
            CAUSAL_SRC = [0, P, 2 * P]

            def start_T(j):
                for c in range(2):
                    for t in range(NT):
                        kt = 2 * j + c
                        mm = pe.transpose(ps[START_BANKS[j]][:, c * S + t * P:c * S + (t + 1) * P], x[:, t, kt * P:(kt + 1) * P], ident[:])
                mm.then_inc(kt_T, 1)

            def start_more(j):
                pe.wait_ge(x_landed[j // 2], 16)
                if START_BANKS[j] in START_BANKS[:j]:
                    pe.wait_ge(kt_lo, 2 * START_BANKS.index(START_BANKS[j]) + 2)
                start_T(j)
            pe.wait_ge(rows_landed, 16)
            pe.wait_ge(ident_landed, 16)
            pe.transpose(ps[0][:, 0:KT], gain_rows[0:KT, 0, :], ident[0:KT, 0:KT]).then_inc(rows_T, 1)
            pe.wait_ge(x_landed[0], 16)
            for j in range(2):
                start_T(j)
            pe.wait_ge(gain_ready, 1)

            def diff_head(u, h):
                u_qk, u_scores, u_p, u_values, u_y = HEAD_STEPS
                if u == u_qk:
                    turn_qk(hb, h)
                if u == u_scores:
                    pe.wait_ge(hb.qkT, h.upto(2))
                    for t in range(NT):
                        for c in range(2):
                            e = slice(c * 64, (c + 1) * 64)
                            mm = pe.matmul(ps[5 + c][:, t * S:(t + 1) * S], qkT[e, 0, t * P:(t + 1) * P], qkT[e, 1, :],
                                           start=True, stop=True)
                            if t == NT - 1:
                                mm.then_inc(hb.scores, 1)
                if u == u_p:
                    pe.wait_ge(hb.mixed, h.upto(2))
                    turn_p(hb, mix, FULL_SRC)
                if u == u_values:
                    values(hb, h, z1, h.num(WH, 2 * P), P, FULL)
                if u == u_y:
                    turn_y(hb, h, ps[7], S, 1)

            def dil_head(u, h, at_units=HEAD_STEPS):
                u_qk, u_scores, u_p, u_values, u_y = at_units
                if u == u_qk:
                    turn_qk(ha, h)
                if u == u_scores:
                    pe.wait_ge(ha.qkT, h.upto(2))
                    for t in range(NT):
                        mm = pe.matmul(ps[5][:, t * S:(t + 1) * S], qkT[:, 0, t * P:(t + 1) * P], qkT[:, 1, :],
                                       start=True, stop=True)
                    mm.then_inc(ha.scores, 1)
                if u == u_p:
                    pe.wait_ge(ha.exps, h.upto(2))
                    turn_p(ha, prob, FULL_SRC)
                if u == u_values:
                    values(ha, h, z2, h.num(WH, 2 * P), P, FULL)
                if u == u_y:
                    turn_y(ha, h, ps[7], S, 1)

            def heads_turn(name, i, behind, ready=None):
                for g in range(2):
                    group(name, i, 16, g, 8, xT, 0, evac_free(by_act, name, BY_ACT, i, g), WH, ready=ready, behind=behind)

            def small_T():
                pe.wait_ge(small_landed, 16 * N_SMALL)
                pe.wait_ge(kt_lo, KT)
                n_late = N_GAIN - G_FFN
                pe.transpose(ps[4][:, 0:n_late], gain_rows[0:n_late, 1, :], ident[0:n_late, 0:n_late]).then_inc(rows_T, 1)
                for j in range(4):
                    mm = pe.transpose(ps[5][:, j * CONV_T:(j + 1) * CONV_T], conv_rows[:, j, :], ident[0:CONV_T, 0:CONV_T])
                mm.then_inc(rows_T, 1)
            xT, yT = (xT_hi, xT_lo), (yT_hi, yT_lo)

            def behind(u):
                if u < 6:
                    start_more(2 + u)
                if u == 8:
                    small_T()
                if u == 10:
                    pe.wait_ge(gain_ready, 3)
                diff_head(u - 10, Head(0, 0, 0))
            heads_turn("in_b", 0, behind, tiles_ready(0))
            with pe.Fori(1, 4) as i:
                def behind(u):
                    diff_head(u + 6, Head(i, -2, 2))
                    diff_head(u - 2, Head(i, -1, 2))
                    diff_head(u - 10, Head(i, 0, 2))
                heads_turn("in_b", i, behind)

            def behind(u):
                diff_head(u + 6, Head(0, 6, 0))
                diff_head(u - 2, Head(0, 7, 0))
                dil_head(u - 10, Head(0, 0, 0))
            heads_turn("in_a", 0, behind)
            with pe.Fori(1, 4) as i:
                def behind(u):
                    dil_head(u + 6, Head(i, -2, 2))
                    dil_head(u - 2, Head(i, -1, 2))
                    dil_head(u - 10, Head(i, 0, 2))
                heads_turn("in_a", i, behind)

            def behind(u):
                dil_head(u + 6, Head(0, 6, 0))
                dil_head(u, Head(0, 7, 0), LAST_DIL_STEPS)
            pe.wait_ge(by_act, FREE + PH["out_b"][BY_ACT] - 2)
            pe.wait_ge(hb.y_lo, FREE + HEADS)
            for i in range(2):
                for g in range(2):
                    group("out_b", i, 8, g, 4, yT, HEADS, evac_free(by_dve, "out_b", BY_DVE, i, g),
                          behind=behind if i == 0 else nothing, also=(by_act, FREE + PH["out_b"][BY_ACT]) if g else None)

            def turn_x(q, base, summed=None):
                sem_, c0 = summed or (by_dve, FREE + SUMMED[base])
                pe.wait_ge(sem_, c0 + 2 * q + 2)
                pe.wait_ge(kt_lo, base + 4 * q - 4)
                for b in range(2):
                    for c in range(2):
                        for t in range(NT):
                            kt = 2 * b + c
                            mm = pe.transpose(ps[4 + 2 * (q % 2) + b][:, c * S + t * P:c * S + (t + 1) * P],
                                              fresh[q % 2][:, t, kt * P:(kt + 1) * P], ident[:])
                    mm.then_inc(kt_T, 1)

            def residual(name, units, src, kt0, base, summed=None, last=None, ready=None, also=None):
                for i in range(2):
                    def behind(u):
                        if u == 1 and i == 0 and last:
                            turn_x(3, *last)
                        if u == 1 and i == 1:
                            turn_x(1, base, summed)
                        if u == units + 1:
                            turn_x(2 * i, base, summed)
                    for g in range(2):
                        group(name, i, 2 * units, g, units, src, kt0, evac_free(by_dve, name, BY_DVE, i, g),
                              ready=ready, behind=behind, also=also if g else None)

            residual("out_a", 4, yT, 0, KT, ready=lambda u: pe.wait_ge(ha.y_lo, FREE + UK * (u + 1)))

            def broadcast_rstd(n):
                pe.wait_ge(r_diag, 2 * n)
                for t in range(NT):
                    mm = pe.matmul(ps[4][:, t * P:(t + 1) * P], ones[:], diag[:, t, :], start=True, stop=True)
                mm.then_inc(r_bc_T, 1)

            def ffn(name, src, act, base, n_norm, fg0, last_base):
                for t, width in enumerate(THIRDS):
                    up, down, n_fg, units = f"{name}_up{t}", f"{name}_down{t}", width // W, width // (UK * P)

                    def up_turn(i, behind=nothing):
                        for g in range(2):
                            group(up, i, 16, g, 8, src, 0, evac_free(by_dve, up, BY_DVE, i, g), feature=True,
                                  ready=tiles_ready(base), behind=behind)

                    def behind(u):
                        if u == 1:
                            turn_x(3, base)
                        if u == 4:
                            broadcast_rstd(n_norm)
                    if t == 0:
                        up_turn(0, behind)
                    with pe.Fori(1 if t == 0 else 0, n_fg) as i:
                        up_turn(i)

                    def act_ready(u, f=fg0):
                        pe.wait_ge(act_lo, f + u // 2 + 1)
                    fg0 += n_fg
                    if t == 2 and last_base is not None:
                        residual(down, units, act, 0, last_base, ready=act_ready)
                    else:
                        with pe.Fori(0, 2) as i:
                            for g in range(2):
                                group(down, i, 2 * units, g, units, act, 0, evac_free(by_dve, down, BY_DVE, i, g), ready=act_ready)

            ffn("ffn1", xT, yT, KT, 1, 0, 2 * KT)

            pe.wait_ge(by_dve, FREE + PH["in_m"][BY_DVE] - 2)

            def behind(u):
                if u == 1:
                    turn_x(3, 2 * KT)
            for i in range(2):
                for g in range(2):
                    group("in_m", i, 16, g, 8, xT, 0, evac_free(by_act, "in_m", BY_ACT, i, g), ready=tiles_ready(2 * KT),
                          also=(by_dve, FREE + PH["in_m"][BY_DVE]) if g else None, behind=behind if i == 0 else nothing)

            def gates():
                pe.wait_ge(gate_lo, 1)
                o = ps[4][0:NG, 0:S]
                for kt in range(KT):
                    c = slice(kt * S, (kt + 1) * S)
                    pe.matmul(o, gate_w_hi[:, kt, :], xT_hi[:, c], start=kt == 0, stop=False)
                    pe.matmul(o, gate_w_hi[:, kt, :], xT_lo[:, c], start=False, stop=False)
                    mm = pe.matmul(o, gate_w_lo[:, kt, :], xT_hi[:, c], start=False, stop=kt == KT - 1)
                mm.then_inc(gates_done, 1)

            def gates_back():
                pe.wait_ge(gates_copied, 1)
                for t in range(NT):
                    mm = pe.transpose(ps[5][:, t * NG:(t + 1) * NG], gates_T[:, t * P:(t + 1) * P], ident[0:NG, 0:NG])
                mm.then_inc(gates_done, 1)

            def cumulate():
                pe.wait_ge(log_f, 1)
                pe.matmul(ps[5][:, 0:NG], tri[:], lf[:, 0, :], start=True, stop=True)
                pe.matmul(ps[5][:, NG:2 * NG], ones[:], lf[:, 0, :], start=True, stop=False)
                pe.matmul(ps[5][:, NG:2 * NG], tri[:], lf[:, 1, :], start=False, stop=True).then_inc(cum_done, 1)

            def behind(u):
                if u == 0:
                    gates()
                if u == 3:
                    gates_back()
                if u == 8:
                    cumulate()
            for g in range(2):
                group("in_m", 2, 16, g, 8, xT, 0, evac_free(by_act, "in_m", BY_ACT, 2, g), behind=behind)
            pe.wait_ge(cum_read, 1)

            with pe.Fori(0, 4) as i:
                h = Head(i, 0, 1)

                def behind(u):
                    u_qk, u_scores, u_p, u_values, u_y = MLSTM_STEPS
                    if u == u_qk:
                        turn_qk(hm, h)
                    if u == 2:
                        pe.wait_ge(diag_ready, h.upto(2))
                        for kt in range(2):
                            mm = pe.matmul(ps[5][:, kt * P:(kt + 1) * P], ones[:], diag[:, kt, :], start=True, stop=True)
                        mm.then_inc(decay_bc, 1)
                    if u == u_scores:
                        pe.wait_ge(hm.qkT, h.upto(2))
                        for t, c, n in CAUSAL_COLS:
                            mm = pe.matmul(ps[6][:, c:c + n], qkT[:, 0, t * P:(t + 1) * P], qkT[:, 1, 0:n], start=True, stop=True)
                        mm.then_inc(hm.scores, 1)
                    if u == u_p:
                        pe.wait_ge(hm.mixed, h.upto(2))
                        turn_p(hm, mix, CAUSAL_SRC)
                    if u == u_values:
                        values(hm, h, z1, h.num(M_DV, HALF), M_DV, CAUSAL)
                    if u == u_y:
                        turn_y(hm, h, ps[4], 0, 2)
                for g in range(2):
                    group("in_f", i, 16, g, 8, xT, 0, evac_free(by_act, "in_f", BY_ACT, i, g), WH, behind=behind)

            def fox_head(u, h, at_units):
                u_qk, u_scores, u_p, u_values, u_y = at_units
                if u == u_qk:
                    turn_qk(hf, h)
                if u == u_scores:
                    pe.wait_ge(hf.qkT, h.upto(2))
                    pe.wait_ge(diag_ready, h.upto(2, 2 * M_HEADS + 2))
                    for t, c, n in CAUSAL_COLS:
                        pe.matmul(ps[6][:, c:c + n], qkT[:, 0, t * P:(t + 1) * P], qkT[:, 1, 0:n], start=True, stop=False)
                        for kt in range(t + 1):
                            mm = pe.matmul(ps[6][:, c + kt * P:c + (kt + 1) * P], ones[:], diag[:, kt, :],
                                           start=False, stop=kt == t)
                    mm.then_inc(hf.scores, 1)
                if u == u_p:
                    pe.wait_ge(hf.exps, h.upto(2))
                    turn_p(hf, prob, CAUSAL_SRC)
                if u == u_values:
                    values(hf, h, z2, h.num(P, 2 * HALF), P, CAUSAL)
                if u == u_y:
                    turn_y(hf, h, ps[7], S, 1)
            pe.wait_ge(hm.y_lo, FREE + 2 * M_HEADS)
            with pe.Fori(0, 4) as i:
                def behind(u):
                    fox_head(u, Head(i, 0, 1), FOX_M_STEPS)
                group("gate_m", i, 12, 0, 8, xT, 0, (by_act, at(i, FREE + PH["gate_m"][BY_ACT] - 2, 2)), behind=behind,
                      also=(hf.y_lo, Head(i, 0, 1).num(1, FREE)))
                group("gate_m", i, 12, 1, 4, yT, HEADS, (by_dve, at(i, FREE + PH["gate_m"][BY_DVE], 2)), behind=behind, u0=8)
            pe.wait_ge(by_act, FREE + PH["gate_a"][BY_ACT])
            with pe.Fori(0, 2) as i:
                def behind(u):
                    for g in range(2):
                        fox_head(u - 8 * g, Head(i, M_HEADS + g, 2), FOX_A_STEPS)
                for g in range(2):
                    group("gate_a", i, 16, g, 8, xT, 0, evac_free(by_act, "gate_a", BY_ACT, i, g), behind=behind,
                          also=(by_dve, FREE + PH["gate_a"][BY_DVE]) if g else None)
            pe.wait_ge(by_act, FREE + PH["proj_a"][BY_ACT] - 2)
            merge = 3 * KT, (fresh_ready, 0)
            residual("proj_a", 4, yT, 0, *merge, ready=lambda u: pe.wait_ge(hf.y_lo, FREE + UK * (u + 1)),
                     also=(by_act, FREE + PH["proj_a"][BY_ACT]))
            residual("out2", 8, xT, 0, 4 * KT, last=merge, ready=tiles_ready(3 * KT))
            ffn("ffn2", yT, xT, 4 * KT, 2, FF // W, None)

        @block.scalar
        def _(act):
            def split(n, i, step, width=W):
                loads = UK if n < N_SPLIT else 1
                before = 0 if n < N_SPLIT else (UK - 1) * N_SPLIT // NS
                act.wait_ge(raw_landed[n % NS], at(i, 16 * (loads * (n // NS + 1) + before), 16 * loads * step // NS))
                act.wait_ge(slot_used, at(i, n + 1, step))
                nc.scalar.activation(w_hi[n % NS][:, :, 0:width], raw[n % NS][:, :, 0:width], ACT.Copy).then_inc(hi_ready, 1)

            def turn(name, i, units, behind=nothing, width=W, ahead=True):
                for u in range(units):
                    if ahead or u + NS < units:
                        split(PH[name][0] + NS + u, i, units, width if u + NS < units else W)
                    behind(u)

            act.wait_ge(const_set, N_CONST)
            nc.scalar.activation(junk[:, 0:4], eps_diff[:], ACT.Exp).then_inc(warm, 1)
            act.wait_ge(warm, 1)

            def start_tile(kt):
                act.wait_ge(kt_T, kt // 2 + 1)
                if kt == 0:
                    act.wait_ge(gain_ready, 1)
                nc.scalar.activation(xT_hi[:, kt * S:(kt + 1) * S], ps[START_BANKS[kt // 2]][:, kt % 2 * S:(kt % 2 + 1) * S],
                                     ACT.Copy, scale=gain[:, G_ATTN + kt:G_ATTN + kt + 1]).then_inc(kt_hi, 1)
            for u in range(NS):
                start_tile(2 * u)
                start_tile(2 * u + 1)
                split(u, None, 0, WH)

            def squares_of_x(t, dst):
                nc.scalar.activation(dst[:, t, :], x[:, t, :], ACT.Square, accum_out=ss[:, t:t + 1]).then_inc(x_sq, 1)

            def evac(name, i, g, dst, col, width, scale, func=ACT.Copy, step=16):
                act.wait_ge(*multiplied(name, i, 8 * (g + 1), step))
                for t in range(NT):
                    o = dst[t] if isinstance(dst, list) else dst[:, t, ds(col, width)]
                    nc.scalar.activation(o, pair[g][t][:, 0:width], func,
                                         scale=scale[:, t:t + 1]).then_inc(by_act, 1)

            def qk_out(s, h, scale):
                act.wait_ge(s.qk_T, h.num(1, FREE + 1))
                nc.scalar.activation(qkT[:, 0, :], ps[4][:, 0:S], ACT.Copy, scale=scale).then_inc(s.qkT, 1)
                nc.scalar.activation(qkT[:, 1, :], ps[4][:, S:2 * S], ACT.Copy).then_inc(s.qkT, 1)

            def p_out(s, h, n):
                act.wait_ge(s.p_T, h.upto())
                nc.scalar.activation(pT[:, 0:n], ps[4][:, 0:n], ACT.Copy).then_inc(s.pT, 1)

            def squares(s, h, width, scale):
                act.wait_ge(s.rden, h.upto())
                act.wait_ge(s.pv, h.upto())
                for t in range(NT):
                    nc.scalar.activation(junk[:, t * width:(t + 1) * width], ps[7][:, t * width:(t + 1) * width], ACT.Square,
                                         scale=scale[:, t:t + 1], accum_out=head_ss[:, t:t + 1]).then_inc(s.sq, 1)

            def y_hi(s, h, bank, c0, tile0, tiles, scale):
                act.wait_ge(s.y_T, h.upto())
                for e in range(tiles):
                    nc.scalar.activation(yT_hi[:, ds(h.num(tiles * S, (tile0 + e) * S), S)], bank[:, c0 + e * S:c0 + (e + 1) * S],
                                         ACT.Copy, scale=scale(e)).then_inc(s.y_hi, 1)

            def diff_head(u, h):
                u_qk, u_scores, u_p, u_values, u_y = HEAD_STEPS
                if u == u_qk:
                    qk_out(hb, h, B_SCALE)
                if u == u_scores:
                    for c in range(2):
                        act.wait_ge(hb.row_max, h.upto(2, c + 1))
                        for t in range(NT):
                            nc.scalar.activation(prob[:, (2 * t + c) * S:(2 * t + c + 1) * S], ps[5 + c][:, t * S:(t + 1) * S],
                                                 ACT.Exp, bias=neg_max[:, t, c:c + 1],
                                                 accum_out=den[:, c, t:t + 1]).then_inc(hb.exps, 1)
                if u == u_p:
                    p_out(hb, h, 2 * S)
                if u == u_values:
                    squares(hb, h, P, rden[:, 0])
                if u == u_y:
                    y_hi(hb, h, ps[7], S, HEADS, 1, lambda e: gain[:, G_SUBLN:G_SUBLN + 1])

            def dil_head(u, h, at_units=HEAD_STEPS):
                u_qk, u_scores, u_p, _, u_y = at_units
                if u == u_qk:
                    qk_out(ha, h, 1.0)
                if u == u_scores:
                    act.wait_ge(ha.row_max, h.upto())
                    for t in range(NT):
                        nc.scalar.activation(prob[:, t * S:(t + 1) * S], mix[:, t * S:(t + 1) * S], ACT.Exp,
                                             bias=neg_max[:, 0, t:t + 1], accum_out=den[:, 0, t:t + 1]).then_inc(ha.exps, 1)
                if u == u_p:
                    p_out(ha, h, 2 * S)
                if u == u_y:
                    y_hi(ha, h, ps[7], S, 0, 1, lambda e: 1.0)

            def heads_out(u, name, i, z):
                for g in range(2):
                    if u == 8 * g + 7:
                        evac(name, i, g, z, at(i, g * WH, 2 * WH), WH, rstd)

            def behind(u):
                if u < NS:
                    start_tile(2 * (NS + u))
                    start_tile(2 * (NS + u) + 1)
                if u in (3, 4):
                    squares_of_x(u - 3, sq_out0)
                if u == 6:
                    act.wait_ge(rstd_ready, 1)
                if u == 9:
                    act.wait_ge(lam_step, 2)
                    nc.scalar.activation(lam_t[:, 2:4], lam_t[:, 0:2], ACT.Exp).then_inc(lam_exp, 1)
                diff_head(u - 10, Head(0, 0, 0))
                heads_out(u, "in_b", 0, z1)
            turn("in_b", 0, 16, behind, WH)
            with act.Fori(1, 4) as i:
                def behind(u):
                    diff_head(u + 6, Head(i, -2, 2))
                    diff_head(u - 2, Head(i, -1, 2))
                    diff_head(u - 10, Head(i, 0, 2))
                    heads_out(u, "in_b", i, z1)
                turn("in_b", i, 16, behind, WH)
            act.wait_ge(gain_ready, 3)

            def behind(u):
                diff_head(u + 6, Head(0, 6, 0))
                diff_head(u - 2, Head(0, 7, 0))
                dil_head(u - 10, Head(0, 0, 0))
                heads_out(u, "in_a", 0, z2)
            turn("in_a", 0, 16, behind, WH)
            with act.Fori(1, 4) as i:
                def behind(u):
                    dil_head(u + 6, Head(i, -2, 2))
                    dil_head(u - 2, Head(i, -1, 2))
                    dil_head(u - 10, Head(i, 0, 2))
                    heads_out(u, "in_a", i, z2)
                turn("in_a", i, 16, behind, WH)

            def behind(u):
                dil_head(u + 6, Head(0, 6, 0))
                dil_head(u, Head(0, 7, 0), LAST_DIL_STEPS)
            turn("out_b", 0, 8, behind)
            turn("out_b", 1, 8)

            def row_squares(name, q, e):
                act.wait_ge(by_dve, FREE + PH[name][BY_DVE] + 2 * q + 2)
                for t in range(NT):
                    act.wait_ge(part_sq, FREE + 8 * e + 2 * q + t)
                    nc.scalar.activation(junk[:], fresh[q % 2][:, t, :], ACT.Square, accum_out=part_ss[:, t, q:q + 1]).then_inc(part_sq, 1)

            def x_hi(q, base, dst, gain0):
                for j in range(4):
                    kt = 4 * q + j
                    act.wait_ge(kt_T, (base + kt) // 2 + 1)
                    scale = 0.5 if gain0 is None else gain[:, gain0 + kt:gain0 + kt + 1]
                    nc.scalar.activation(dst[:, kt * S:(kt + 1) * S], ps[4 + 2 * (q % 2) + j // 2][:, j % 2 * S:(j % 2 + 1) * S],
                                         ACT.Copy, scale=scale).then_inc(kt_hi, 1)

            def residual(name, units, base, dst, gain0, e=None, also=nothing):
                for i in range(2):
                    def behind(u):
                        if i == 0:
                            also(u)
                        if u == 1 and i == 1:
                            x_hi(1, base, dst, gain0)
                        if u == units + 1:
                            x_hi(2 * i, base, dst, gain0)
                        for g in range(2):
                            if u == (g + 1) * units - 1 and e is not None:
                                row_squares(name, 2 * i + g, e)
                    turn(name, i, 2 * units, behind)

            residual("out_a", 4, KT, xT_hi, G_FFN, 0)

            def ffn(name, x_last, dst, fg0, conv_too, last_base):
                for t, width in enumerate(THIRDS):
                    up, down, n_fg, units = f"{name}_up{t}", f"{name}_down{t}", width // W, width // (UK * P)
                    f0 = fg0 - (FF // W if conv_too else 0)

                    def gate_tanh(i):
                        if conv_too:
                            act.wait_ge(conv_step, at(i, 16 * f0 + 8, 16))
                        else:
                            act.wait_ge(by_dve, at(i, FREE + PH[up][BY_DVE] + 2, 4))
                        nc.scalar.activation(tanh_z, gate_z, ACT.Tanh, scale=0.5).then_inc(tanh_ready, 1)

                    def first_tap(i, g, u, z):
                        act.wait_ge(by_dve, at(i, FREE + PH[up][BY_DVE] + 2 * g + 2, 4))
                        for f in range(4):
                            col = at(i, 4 * f0 + f + g * (CONV_T // 2), 4)
                            nc.scalar.activation(z[:, f, :], u[:, f, PAD:PAD + S], ACT.Identity, scale=conv[:, ds(col + 2 * CONV_T, 1)],
                                                 bias=conv[:, ds(col + 3 * CONV_T, 1)]).then_inc(conv_start, 1)

                    def hi_part(i):
                        if conv_too:
                            act.wait_ge(silu_step, at(i, 2 * (fg0 + 1), 2))
                        else:
                            act.wait_ge(by_dve, at(i, FREE + PH[up][BY_DVE] + 4, 4))
                        nc.scalar.activation(tiles4(dst[:, ds(at(i, 0, 4 * S), 4 * S)], S), up_z, ACT.Copy, scale=0.5).then_inc(act_hi, 1)

                    def own(u, i):
                        if conv_too:
                            if u == 7:
                                first_tap(i, 0, gate_u, gate_z)
                            if u == 10:
                                gate_tanh(i)
                            if u == 15:
                                first_tap(i, 1, up_u, up_z)
                        else:
                            if u == 8:
                                gate_tanh(i)
                            if u == 15:
                                hi_part(i)

                    def late(u, i):
                        if u == 0 and conv_too:
                            hi_part(i)

                    def behind(u):
                        if u == 1 and t == 0:
                            x_hi(3, *x_last)
                        own(u, 0)
                    turn(up, 0, 16, behind)
                    with act.Fori(1, n_fg) as i:
                        def behind(u):
                            late(u, i - 1)
                            own(u, i)
                        turn(up, i, 16, behind)

                    def behind(u):
                        late(u, n_fg - 1)
                    if t == 2 and last_base is not None:
                        residual(down, units, last_base, xT_hi, G_NORM1, 1, also=behind)
                    else:
                        for i in range(2):
                            turn(down, i, 2 * units, behind if i == 0 else nothing, ahead=t < 2 or i == 0)
                    fg0 += n_fg

            ffn("ffn1", (KT, xT_hi, G_FFN), yT_hi, 0, False, 2 * KT)

            def m_out(u, i, scales, func):
                for g in range(2):
                    if u == (8 if g == 0 else 15):
                        evac("in_m", i, g, z1, at(i, g * W, 2 * W), W, scales, func)

            def behind(u):
                if u == 0:
                    act.wait_ge(gate_w_landed, 32)
                    nc.scalar.activation(gate_w_hi[:], gate_w[:], ACT.Copy).then_inc(gate_hi, 1)
                if u == 1:
                    x_hi(3, 2 * KT, xT_hi, G_NORM1)
                for t in range(NT):
                    if u == 4 + 2 * t:
                        act.wait_ge(x2_ready, t + 1)
                        squares_of_x(t, sq_out1)
                if u == 7:
                    act.wait_ge(rstd_ready, 4)
                m_out(u, 0, rstd2, ACT.Copy)
            turn("in_m", 0, 16, behind)
            turn("in_m", 1, 16, lambda u: m_out(u, 1, rstd2, ACT.Copy))

            def gates_copy():
                act.wait_ge(gates_done, 1)
                nc.scalar.activation(gates_T, ps[4][0:NG, 0:S], ACT.Copy).then_inc(gates_copied, 1)

            def gates_out():
                act.wait_ge(gates_done, 2)
                for t in range(NT):
                    nc.scalar.activation(gz[:, t, :], ps[5][:, t * NG:(t + 1) * NG], ACT.Copy, scale=rstd2[:, t:t + 1]).then_inc(gates_evac, 1)

            def softplus():
                act.wait_ge(gates_step, 2)
                nc.scalar.activation(gt[:], gt[:], ACT.Exp, scale=-1.0).then_inc(gates_act, 1)
                act.wait_ge(gates_act, 1)
                nc.scalar.activation(gt[:], gt[:], ACT.Ln, bias=1.0).then_inc(gates_act, 1)

            def behind(u):
                if u == 2:
                    gates_copy()
                if u == 3:
                    gates_out()
                if u == 5:
                    softplus()
                m_out(u, 2, half_rstd2, ACT.Tanh)
            turn("in_m", 2, 16, behind)

            with act.Fori(0, 4) as i:
                h = Head(i, 0, 1)

                def behind(u):
                    u_qk, _, u_p, u_values, u_y = MLSTM_STEPS
                    if u == u_qk:
                        qk_out(hm, h, HEAD_SCALE)
                    if u == 4:
                        act.wait_ge(hm.row_max, h.upto())
                        for t, c, n in CAUSAL_COLS:
                            nc.scalar.activation(prob[:, c:c + n], mix[:, c:c + n], ACT.Exp, bias=neg_max[:, 0, t:t + 1]).then_inc(hm.exps, 1)
                        for t in range(NT):
                            nc.scalar.activation(floor[:, t:t + 1], f_sum[:, t, ds(h.num(1, HEADS + M_HEADS), 1)], ACT.Exp, scale=-1.0,
                                                 bias=neg_max[:, 0, t:t + 1]).then_inc(floor_ready, 1)
                    if u == u_p:
                        p_out(hm, h, 3 * P)
                    if u == u_values:
                        squares(hm, h, M_DV, rden[:, 0])
                    if u == u_y:
                        y_hi(hm, h, ps[4], 0, HEADS, 2, lambda e: gain[:, ds(h.num(2, G_M + e), 1)])
                    for g in range(2):
                        if u == 8 * g + 7:
                            evac("in_f", i, g, z2, at(i, g * WH, 2 * WH), WH, rstd2)
                turn("in_f", i, 16, behind, WH)

            def fox_head(u, h, at_units):
                u_qk, u_scores, u_p, _, u_y = at_units
                if u == 0:
                    act.wait_ge(hf.ms, h.num(1, FREE))
                    for t in range(NT):
                        for c in range(2):
                            nc.scalar.activation(junk[:, (2 * t + c) * P:(2 * t + c + 1) * P], z2[:, t, ds(h.num(P, c * HALF), P)], ACT.Square,
                                                 accum_out=head_ss[:, 2 * t + c:2 * t + c + 1]).then_inc(hf.sq, 1)
                if u == u_qk:
                    qk_out(hf, h, gain_qk[:, 1:2])
                if u == u_scores:
                    act.wait_ge(hf.raw_max, h.upto(2))
                    for t, c, n in CAUSAL_COLS:
                        nc.scalar.activation(prob[:, c:c + n], mix[:, c:c + n], ACT.Exp, bias=neg_max[:, 0, t:t + 1],
                                             accum_out=den[:, 0, t:t + 1]).then_inc(hf.exps, 1)
                if u == u_p:
                    p_out(hf, h, 3 * P)
                if u == u_y:
                    y_hi(hf, h, ps[7], S, 0, 1, lambda e: 1.0)
            with act.Fori(0, 4) as i:
                def behind(u):
                    fox_head(u, Head(i, 0, 1), FOX_M_STEPS)
                    if u == 7:
                        act.wait_ge(by_dve, at(i, FREE + PH["gate_m"][BY_DVE], 2))
                        evac("gate_m", i, 0, gm_buf, 0, W, half_rstd2, ACT.Tanh, 12)
                turn("gate_m", i, 12, behind)

            act.wait_ge(by_dve, FREE + PH["gate_a"][BY_DVE])
            for i in range(2):
                def behind(u):
                    for g in range(2):
                        fox_head(u - 8 * g, Head(i, M_HEADS + g, 2), FOX_A_STEPS)
                        if u == 8 * g + 7:
                            evac("gate_a", i, g, ga_buf[2 * i + g], 0, W, half_rstd2, ACT.Tanh)
                turn("gate_a", i, 16, behind)
            residual("proj_a", 4, 3 * KT, xT_hi, None)

            def behind(u):
                if u == 1:
                    x_hi(3, 3 * KT, xT_hi, None)
            residual("out2", 8, 4 * KT, yT_hi, G_NORM2, 2, also=behind)
            ffn("ffn2", (4 * KT, yT_hi, G_NORM2), xT_hi, FF // W, True, None)

        @block.vector
        def _(dve):
            v = nc.vector

            def f32(t):
                return t.bitcast(F32)

            def split(n, i, step, width=W):
                dve.wait_ge(hi_ready, at(i, n + 1, step))
                v.tensor_tensor(w_lo[n % NS][:, :, 0:width], raw[n % NS][:, :, 0:width], f32(w_hi[n % NS][:, :, 0:width]),
                                ALU.subtract).then_inc(lo_ready, 1)

            def turn(name, i, units, behind=nothing, width=W, ahead=True, before=nothing):
                for u in range(units):
                    before(u)
                    if ahead or u + NS < units:
                        split(PH[name][0] + NS + u, i, units, width if u + NS < units else W)
                    behind(u)

            dve.wait_ge(rows_T, 1)
            v.tensor_copy(gain[:, 0:KT], ps[0][:, 0:KT]).then_inc(gain_ready, 1)
            dve.wait_ge(gain_ready, 1)

            def start_tiles(u):
                for kt in (2 * u, 2 * u + 1):
                    dve.wait_ge(kt_hi, 2 * u + 2)
                    c = slice(kt * S, (kt + 1) * S)
                    v.scalar_tensor_tensor(xT_lo[:, c], ps[START_BANKS[kt // 2]][:, kt % 2 * S:(kt % 2 + 1) * S],
                                           gain[:, G_ATTN + kt:G_ATTN + kt + 1], f32(xT_hi[:, c]), ALU.mult, ALU.subtract).then_inc(kt_lo, 1)
            for u in range(NS):
                start_tiles(u)
                split(u, None, 0, WH)

            def parameters():
                dve.wait_ge(small_landed, 16 * N_SMALL)
                v.tensor_tensor(lam_prod, lam_in[:, 0:4:2, :], lam_in[:, 1:4:2, :], ALU.mult).then_inc(lam_step, 1)
                dve.wait_ge(rows_T, 2)
                v.tensor_copy(gain[:, G_FFN:N_GAIN], ps[4][:, 0:N_GAIN - G_FFN]).then_inc(gain_ready, 1)
                dve.wait_ge(rows_T, 3)
                v.tensor_copy(conv[:], ps[5][:, 0:4 * CONV_T]).then_inc(gain_ready, 1)
                dve.wait_ge(lam_step, 1)
                v.tensor_reduce(lam_t[:, 0:2], lam_prod, X, ALU.add).then_inc(lam_step, 1)

            def more_parameters():
                dve.wait_ge(gain_ready, 3)
                v.tensor_tensor(gain[:, G_NORM1:G_NORM1 + KT], gain[:, G_NORM1:G_NORM1 + KT], gain[:, G_FINAL:G_FINAL + KT],
                                ALU.mult).then_inc(gain_step, 1)
                v.tensor_scalar(gain[:, G_SUBLN:G_SUBLN + 1], gain[:, G_SUBLN:G_SUBLN + 1], 1.0 - LAM_INIT, None, ALU.mult).then_inc(gain_step, 1)
                v.tensor_tensor(gain_qk[:, 0:1], gain[:, G_Q:G_Q + 1], gain[:, G_K:G_K + 1], ALU.mult).then_inc(gain_step, 1)
                v.tensor_scalar(gain[:, G_M:N_GAIN], gain[:, G_M:N_GAIN], 0.5, None, ALU.mult).then_inc(gain_step, 1)
                dve.wait_ge(gain_step, 4)
                v.tensor_scalar(gain_qk[:, 1:2], gain_qk[:, 0:1], P * HEAD_SCALE, None, ALU.mult).then_inc(gain_step, 1)
                dve.wait_ge(lam_exp, 1)
                v.tensor_tensor(lam_t[:, 4:5], lam_t[:, 3:4], lam_t[:, 2:3], ALU.subtract).then_inc(lam_step, 1)
                dve.wait_ge(lam_step, 3)
                v.tensor_scalar(minus_lam[:], lam_t[:, 4:5], -LAM_INIT, None, ALU.add).then_inc(lam_ready, 1)
                dve.wait_ge(lam_ready, 1)
                dve.wait_ge(gain_step, 5)

            def y_out(s, h, width, scale):
                for t in range(NT):
                    v.tensor_scalar(y[:, t, 0:width], ps[7][:, t * width:(t + 1) * width], scale[:, t:t + 1], None, ALU.mult).then_inc(s.y, 1)

            def y_lo(s, h, bank, c0, tile0, tiles, scale):
                dve.wait_ge(s.y_hi, h.upto(tiles))
                for e in range(tiles):
                    c = ds(h.num(tiles * S, (tile0 + e) * S), S)
                    v.scalar_tensor_tensor(yT_lo[:, c], bank[:, c0 + e * S:c0 + (e + 1) * S], scale(e), f32(yT_hi[:, c]),
                                           ALU.mult, ALU.subtract).then_inc(s.y_lo, 1)

            def diff_head(u, h):
                _, u_scores, _, _, u_y = HEAD_STEPS
                if u == u_scores:
                    for c in range(2):
                        dve.wait_ge(hb.scores, h.upto(2, c + 1))
                        v.tensor_reduce(neg_max[:, :, c], ps[5 + c][:, :].rearrange("p (t s) -> p t s", t=NT), X, ALU.max,
                                        negate=True).then_inc(hb.row_max, 1)
                    dve.wait_ge(hb.exps, h.upto(4))
                    v.reciprocal(rden[:], den[:]).then_inc(hb.rden, 1)
                    dve.wait_ge(hb.rden, h.upto())
                    v.scalar_tensor_tensor(coef[:], rden[:, 1, :], minus_lam[:], den[:, 0, :], ALU.mult, ALU.mult).then_inc(hb.coef, 1)
                    dve.wait_ge(hb.coef, h.upto(2, 1))
                    for t in range(NT):
                        c0, c1 = (prob[:, (2 * t + c) * S:(2 * t + c + 1) * S] for c in range(2))
                        v.scalar_tensor_tensor(mix[:, t * S:(t + 1) * S], c1, coef[:, t:t + 1], c0, ALU.mult, ALU.add).then_inc(hb.mixed, 1)
                if u == u_y - 2:
                    dve.wait_ge(hb.rstd, h.upto())
                    v.scalar_tensor_tensor(coef[:], rden[:, 0, :], P ** 0.5, head_rstd[:, 0:NT], ALU.mult, ALU.mult).then_inc(hb.coef, 1)
                    dve.wait_ge(hb.coef, h.upto(2))
                    y_out(hb, h, P, coef)
                if u == u_y:
                    y_lo(hb, h, ps[7], S, HEADS, 1, lambda e: gain[:, G_SUBLN:G_SUBLN + 1])

            def dil_head(u, h, at_units=HEAD_STEPS):
                _, u_scores, _, _, u_y = at_units
                if u == u_scores:
                    dve.wait_ge(ha.scores, h.upto())
                    v.scalar_tensor_tensor(mix[:], ps[5][:], HEAD_SCALE, ln_count[:], ALU.mult, ALU.add).then_inc(ha.masked, 1)
                    dve.wait_ge(ha.masked, h.upto())
                    v.tensor_reduce(neg_max[:, 0, :], mix[:].rearrange("p (t s) -> p t s", t=NT), X, ALU.max,
                                    negate=True).then_inc(ha.row_max, 1)
                if u == u_y - 2:
                    dve.wait_ge(ha.exps, h.upto(2))
                    v.reciprocal(rden[:, 0, :], den[:, 0, :]).then_inc(ha.rden, 1)
                    dve.wait_ge(ha.rden, h.upto())
                    dve.wait_ge(ha.pv, h.upto())
                    y_out(ha, h, P, rden[:, 0])
                if u == u_y:
                    y_lo(ha, h, ps[7], S, 0, 1, lambda e: 1.0)

            def behind(u):
                if u < NS:
                    start_tiles(NS + u)
                if u == 8:
                    parameters()
                if u == 10:
                    more_parameters()
                diff_head(u - 10, Head(0, 0, 0))
            turn("in_b", 0, 16, behind, WH)
            with dve.Fori(1, 4) as i:
                def behind(u):
                    diff_head(u + 6, Head(i, -2, 2))
                    diff_head(u - 2, Head(i, -1, 2))
                    diff_head(u - 10, Head(i, 0, 2))
                turn("in_b", i, 16, behind, WH)

            def behind(u):
                diff_head(u + 6, Head(0, 6, 0))
                diff_head(u - 2, Head(0, 7, 0))
                dil_head(u - 10, Head(0, 0, 0))
            turn("in_a", 0, 16, behind, WH)
            with dve.Fori(1, 4) as i:
                def behind(u):
                    dil_head(u + 6, Head(i, -2, 2))
                    dil_head(u - 2, Head(i, -1, 2))
                    dil_head(u - 10, Head(i, 0, 2))
                turn("in_a", i, 16, behind, WH)

            def add_in_place(name, i, g, units):
                dve.wait_ge(*multiplied(name, i, units * (g + 1), 2 * units))
                for t in range(NT):
                    c = ds(at(i, g * W, 2 * W), W)
                    v.tensor_tensor(x[:, t, c], x[:, t, c], pair[g][t][:], ALU.add).then_inc(by_dve, 1)

            for i in range(2):
                def behind(u):
                    if i == 0:
                        dil_head(u + 6, Head(0, 6, 0))
                        dil_head(u, Head(0, 7, 0), LAST_DIL_STEPS)
                    for g in range(2):
                        if u == 4 * g + 3:
                            add_in_place("out_b", i, g, 4)
                turn("out_b", i, 8, behind)

            def add_fresh(name, q, units, e):
                i, g = q // 2, q % 2
                dve.wait_ge(*multiplied(name, i, units * (g + 1), 2 * units))
                dve.wait_ge(x_kept, FREE + 4 * e + 2 * i)
                dve.wait_ge(part_sq, FREE + 8 * e + 4 * i)
                for t in range(NT):
                    v.tensor_tensor(fresh[g][:, t, :], x[:, t, q * W:(q + 1) * W], pair[g][t][:], ALU.add).then_inc(by_dve, 1)

            def x_lo(q, base, hi, lo, gain0):
                for j in range(4):
                    kt = 4 * q + j
                    dve.wait_ge(kt_hi, base + kt // 2 * 2 + 2)
                    c = slice(kt * S, (kt + 1) * S)
                    scale = 0.5 if gain0 is None else gain[:, gain0 + kt:gain0 + kt + 1]
                    v.scalar_tensor_tensor(lo[:, c], ps[4 + 2 * (q % 2) + j // 2][:, j % 2 * S:(j % 2 + 1) * S], scale, f32(hi[:, c]),
                                           ALU.mult, ALU.subtract).then_inc(kt_lo, 1)

            def residual(name, units, base, hi, lo, gain0, add, also=nothing):
                for i in range(2):
                    def behind(u):
                        if i == 0:
                            also(u)
                        if u == 1 and i == 1:
                            x_lo(1, base, hi, lo, gain0)
                        if u == units + 1:
                            x_lo(2 * i, base, hi, lo, gain0)
                        for g in range(2):
                            if u == (g + 1) * units - 1:
                                add(2 * i + g)
                    turn(name, i, 2 * units, behind)

            def sum_squares(e):
                dve.wait_ge(part_sq, FREE + 8 * (e + 1))
                v.tensor_reduce(ss[:], part_ss[:], X, ALU.add).then_inc(ss_ready, 1)

            residual("out_a", 4, KT, xT_hi, xT_lo, G_FFN, lambda q: add_fresh("out_a", q, 4, 0))

            def rstd_diag(n):
                dve.wait_ge(rstd_ready, n)
                for t in range(NT):
                    v.tensor_scalar(diag[:, t, :], ident[:], rstd[:, t:t + 1], None, ALU.mult).then_inc(r_diag, 1)

            def ffn(name, x_last, hi, lo, fg0, conv_too, n_norm, n_rstd, e, last_base):
                r_both = r_bc.unsqueeze(1).to_broadcast([P, 2, S])

                def copy_r():
                    dve.wait_ge(r_bc_T, n_norm)
                    v.tensor_copy(r_bc, ps[4][:, 0:S]).then_inc(r_bc_ready, 1)
                    dve.wait_ge(r_bc_ready, n_norm)
                for t, width in enumerate(THIRDS):
                    up, down, n_fg, units = f"{name}_up{t}", f"{name}_down{t}", width // W, width // (UK * P)
                    f0 = fg0 - (FF // W if conv_too else 0)

                    def scaled(i, g, dst, factor):
                        dve.wait_ge(*multiplied(up, i, 8 * (g + 1), 16))
                        for b in range(2):
                            o = dst[:, 2 * b:2 * b + 2, PAD:PAD + S] if conv_too else dst[:, 2 * b:2 * b + 2, :]
                            v.tensor_tensor(o, pair[g][b][:].rearrange("p (f s) -> p f s", f=2), factor(b), ALU.mult).then_inc(by_dve, 1)

                    def convolve(i, g, u, z, j):
                        tap = 2 - j
                        for f in range(4):
                            if j == 1:
                                dve.wait_ge(conv_start, at(i, 8 * f0 + 4 * g + f + 1, 8))
                            else:
                                dve.wait_ge(conv_step, at(i, 16 * f0 + 8 * g + f + 1, 16))
                            w = conv[:, ds(at(i, 4 * f0 + f + g * (CONV_T // 2) + tap * CONV_T, 4), 1)]
                            v.scalar_tensor_tensor(z[:, f, :], u[:, f, tap:tap + S], w, z[:, f, :], ALU.mult, ALU.add).then_inc(conv_step, 1)

                    def silu(i):
                        dve.wait_ge(tanh_ready, at(i, fg0 + 1, 1))
                        v.scalar_tensor_tensor(gate_z, tanh_z, 1.0, gate_z, ALU.add, ALU.mult).then_inc(silu_step, 1)
                        dve.wait_ge(silu_step, at(i, 2 * fg0 + 1, 2))
                        if not conv_too:
                            r4 = r_bc.unsqueeze(1).to_broadcast([P, 4, S])
                            v.tensor_tensor(gate_z, gate_z, r4, ALU.mult).then_inc(silu_step, 1)
                            dve.wait_ge(silu_step, at(i, 2 * fg0 + 2, 2))

                    def act_lo_part(i):
                        dve.wait_ge(act_hi, at(i, fg0 + 1, 1))
                        c = ds(at(i, 0, 4 * S), 4 * S)
                        v.scalar_tensor_tensor(tiles4(lo[:, c], S), up_z, 0.5, tiles4(f32(hi[:, c]), S), ALU.mult, ALU.subtract).then_inc(act_lo, 1)

                    def product(i):
                        dve.wait_ge(conv_step, at(i, 16 * f0 + 16, 16))
                        v.tensor_tensor(up_z, up_z, gate_z, ALU.mult).then_inc(silu_step, 1)

                    def before(u, i):
                        if u == 15 and conv_too:
                            scaled(i, 1, up_u, lambda b: r_both)

                    def own(u, i):
                        if conv_too:
                            if u == 7:
                                scaled(i, 0, gate_u, lambda b: r_both)
                            if u == 8:
                                convolve(i, 0, gate_u, gate_z, 1)
                            if u == 9:
                                convolve(i, 0, gate_u, gate_z, 2)
                            if u == 12:
                                silu(i)
                            if u == 15:
                                convolve(i, 1, up_u, up_z, 1)
                                convolve(i, 1, up_u, up_z, 2)
                                product(i)
                        else:
                            if u == 7:
                                scaled(i, 0, gate_z, lambda b: r_both)
                            if u == 9:
                                silu(i)
                            if u == 15:
                                scaled(i, 1, up_z, lambda b: gate_z[:, 2 * b:2 * b + 2, :])

                    def late(u, i):
                        if u == 0:
                            act_lo_part(i)

                    def behind(u):
                        if t == 0:
                            if u == 1:
                                x_lo(3, *x_last)
                                sum_squares(e)
                            if u == 3:
                                rstd_diag(n_rstd)
                            if u == 5:
                                copy_r()
                        own(u, 0)
                    turn(up, 0, 16, behind, before=lambda u: before(u, 0))
                    with dve.Fori(1, n_fg) as i:
                        def behind(u):
                            late(u, i - 1)
                            own(u, i)
                        turn(up, i, 16, behind, before=lambda u: before(u, i))

                    def first(u):
                        late(u, n_fg - 1)
                        if u == 0 and t == 0:
                            dve.wait_ge(x_kept, FREE + 4 * (e + 1))
                    if t == 2 and last_base is not None:
                        residual(down, units, last_base, xT_hi, xT_lo, G_NORM1, lambda q: add_fresh(down, q, units, e + 1), also=first)
                    else:
                        for i in range(2):
                            def behind(u):
                                if i == 0:
                                    first(u)
                                for g in range(2):
                                    if u == (g + 1) * units - 1:
                                        add_in_place(down, i, g, units)
                            turn(down, i, 2 * units, behind, ahead=t < 2 or i == 0)
                    fg0 += n_fg

            ffn("ffn1", (KT, xT_hi, xT_lo, G_FFN), yT_hi, yT_lo, 0, False, 1, 2, 0, 2 * KT)

            def behind(u):
                if u == 1:
                    x_lo(3, 2 * KT, xT_hi, xT_lo, G_NORM1)
                    sum_squares(1)
                if u == 2:
                    dve.wait_ge(gate_hi, 1)
                    v.tensor_tensor(gate_w_lo[:], gate_w[:], f32(gate_w_hi[:]), ALU.subtract).then_inc(gate_lo, 1)
                if u == 3:
                    dve.wait_ge(x_kept, FREE + 8)
                    dve.wait_ge(final_landed, 16)
                    dve.wait_ge(rstd_ready, 3)
                for t in range(NT):
                    if u == 3 + 2 * t:
                        v.scalar_tensor_tensor(x[:, t, :], x[:, t, :], rstd[:, t:t + 1], gain_final_bc, ALU.mult, ALU.mult).then_inc(x2_ready, 1)
            turn("in_m", 0, 16, behind)
            turn("in_m", 1, 16)

            I_COL, MF_COL = HEADS, HEADS + M_HEADS

            def gates_bias():
                dve.wait_ge(gates_evac, 2)
                v.tensor_tensor(gz[:], gz[:], gate_bias[:].unsqueeze(1).to_broadcast([P, NT, NG]), ALU.add).then_inc(gates_step, 1)
                dve.wait_ge(gates_step, 1)
                v.scalar_tensor_tensor(gt[:], gz[:], -1.0, gz[:], ALU.mult, ALU.max).then_inc(gates_step, 1)

            def log_sigmoid():
                dve.wait_ge(gates_act, 2)
                v.scalar_tensor_tensor(lf[:], gz[:], 0.0, gt[:], ALU.min, ALU.subtract).then_inc(log_f, 1)

            def decays():
                dve.wait_ge(cum_done, 1)
                v.tensor_copy(f_sum[:], ps[5][:, 0:2 * NG].rearrange("p (t n) -> p t n", t=NT)).then_inc(cum_read, 1)
                dve.wait_ge(cum_read, 1)
                v.tensor_tensor(a_gate[:], gz[:, :, I_COL:I_COL + M_HEADS], f_sum[:, :, MF_COL:NG], ALU.subtract).then_inc(decay_ready, 1)
                dve.wait_ge(decay_ready, 1)

            def behind(u):
                if u == 4:
                    gates_bias()
                if u == 6:
                    log_sigmoid()
                if u == 8:
                    decays()
            turn("in_m", 2, 16, behind)

            with dve.Fori(0, 4) as i:
                h = Head(i, 0, 1)

                def decay_diag():
                    for t in range(NT):
                        v.tensor_scalar(diag[:, t, :], ident[:], a_gate[:, t, ds(h.num(), 1)], None, ALU.mult).then_inc(diag_ready, 1)

                def decay_max():
                    dve.wait_ge(decay_bc, h.upto())
                    for t, c, n in CAUSAL_COLS:
                        v.tensor_tensor(mix[:, c:c + n], ps[5][:, 0:n], causal[:, c:c + n], ALU.add).then_inc(hm.masked, 1)
                    for t, c, n in CAUSAL_COLS:
                        dve.wait_ge(hm.masked, h.upto(2, t + 1))
                        v.tensor_reduce(top[:, t:t + 1], mix[:, c:c + n], X, ALU.max).then_inc(hm.raw_max, 1)
                    dve.wait_ge(hm.raw_max, h.upto(2))
                    v.tensor_scalar(neg_max[:, 0, :], top[:], 0.0, -1.0, ALU.max, ALU.mult).then_inc(hm.row_max, 1)

                def weigh():
                    dve.wait_ge(hm.exps, h.upto(2))
                    dve.wait_ge(hm.scores, h.upto())
                    for t, c, n in CAUSAL_COLS:
                        v.tensor_tensor_reduce(out=mix[:, c:c + n], in0=ps[6][:, c:c + n], in1=prob[:, c:c + n], scale=1.0, scalar=0.0,
                                               op0=ALU.mult, op1=ALU.add, accum_out=den[:, 0, t:t + 1]).then_inc(hm.mixed, 1)
                    dve.wait_ge(hm.mixed, h.upto(2))
                    dve.wait_ge(floor_ready, h.upto(2))
                    v.scalar_tensor_tensor(den[:, 1, :], den[:, 0, :], -1.0, den[:, 0, :], ALU.mult, ALU.max).then_inc(den_part, 1)
                    dve.wait_ge(den_part, h.upto(2, 1))
                    v.tensor_tensor(den[:, 0, :], den[:, 1, :], floor[:], ALU.max).then_inc(den_part, 1)
                    dve.wait_ge(den_part, h.upto(2))
                    v.reciprocal(rden[:, 0, :], den[:, 0, :]).then_inc(hm.rden, 1)

                def result():
                    dve.wait_ge(hm.rstd, h.upto())
                    v.scalar_tensor_tensor(coef[:], rden[:, 0, :], M_DV ** 0.5, head_rstd[:, 0:NT], ALU.mult, ALU.mult).then_inc(hm.coef, 1)
                    dve.wait_ge(hm.coef, h.upto())
                    for t in range(NT):
                        v.tensor_scalar(h_norm[:, t, :], ps[7][:, t * M_DV:(t + 1) * M_DV], coef[:, t:t + 1], None, ALU.mult).then_inc(norm_step, 1)
                    for t in range(NT):
                        dve.wait_ge(norm_step, h.upto(2, t + 1))
                        v.scalar_tensor_tensor(y[:, t, :], z1[:, t, ds(h.num(M_DV, D), M_DV)], 1.0, h_norm[:, t, :], ALU.add, ALU.mult).then_inc(hm.y, 1)

                def behind(u):
                    u_y = MLSTM_STEPS[-1]
                    if u == 0:
                        decay_diag()
                    if u == 3:
                        decay_max()
                    if u == 5:
                        weigh()
                    if u == u_y - 2:
                        result()
                    if u == u_y:
                        y_lo(hm, h, ps[4], 0, HEADS, 2, lambda e: gain[:, ds(h.num(2, G_M + e), 1)])
                turn("in_f", i, 16, behind, WH)

            def fox_head(u, h, at_units):
                _, u_scores, _, u_values, u_y = at_units
                if u == 0:
                    for t in range(NT):
                        v.tensor_scalar(diag[:, t, :], ident[:], f_sum[:, t, ds(h.num(), 1)], -1.0, ALU.mult, ALU.mult).then_inc(diag_ready, 1)
                if u == u_scores:
                    dve.wait_ge(hf.scores, h.upto())
                    for t, c, n in CAUSAL_COLS:
                        v.scalar_tensor_tensor(mix[:, c:c + n], ps[6][:, c:c + n], f_sum[:, t, ds(h.num(), 1)], causal[:, c:c + n],
                                               ALU.add, ALU.add).then_inc(hf.masked, 1)
                    for t, c, n in CAUSAL_COLS:
                        dve.wait_ge(hf.masked, h.upto(2, t + 1))
                        v.tensor_reduce(neg_max[:, 0, t:t + 1], mix[:, c:c + n], X, ALU.max, negate=True).then_inc(hf.raw_max, 1)
                if u == u_values:
                    dve.wait_ge(hf.exps, h.upto(2))
                    v.reciprocal(rden[:, 0, :], den[:, 0, :]).then_inc(hf.rden, 1)
                    dve.wait_ge(hf.rden, h.upto())
                    dve.wait_ge(hf.pv, h.upto())
                    y_out(hf, h, P, rden[:, 0])
                if u == u_y:
                    y_lo(hf, h, ps[7], S, 0, 1, lambda e: 1.0)
            with dve.Fori(0, 4) as i:
                def behind(u):
                    fox_head(u, Head(i, 0, 1), FOX_M_STEPS)
                    if u == 11:
                        dve.wait_ge(*multiplied("gate_m", i, 12, 12))
                        dve.wait_ge(by_act, at(i, FREE + PH["gate_m"][BY_ACT] + 2, 2))
                        for t in range(NT):
                            v.scalar_tensor_tensor(merged[:, t, ds(i * W, W)], gm_buf[:, t, :], 1.0, pair[1][t][:], ALU.add, ALU.mult).then_inc(by_dve, 1)
                turn("gate_m", i, 12, behind)
            with dve.Fori(0, 2) as i:
                def behind(u):
                    for g in range(2):
                        fox_head(u - 8 * g, Head(i, M_HEADS + g, 2), FOX_A_STEPS)
                turn("gate_a", i, 16, behind)

            def merge_a(q):
                i, g = q // 2, q % 2
                dve.wait_ge(by_act, FREE + PH["gate_a"][BY_ACT] + 2 * q + 2)
                dve.wait_ge(*multiplied("proj_a", i, 4 * (g + 1), 8))
                for t in range(NT):
                    v.scalar_tensor_tensor(fresh[g][:, t, :], ga_buf[q][t], 1.0, pair[g][t][:], ALU.add, ALU.mult).then_inc(by_dve, 1)
                for t in range(NT):
                    dve.wait_ge(by_dve, FREE + PH["proj_a"][BY_DVE] + 2 * q + t + 1)
                    v.tensor_tensor(fresh[g][:, t, :], fresh[g][:, t, :], merged[:, t, q * W:(q + 1) * W], ALU.add).then_inc(fresh_ready, 1)
            residual("proj_a", 4, 3 * KT, xT_hi, xT_lo, None, merge_a)

            def behind(u):
                if u == 1:
                    x_lo(3, 3 * KT, xT_hi, xT_lo, None)
            residual("out2", 8, 4 * KT, yT_hi, yT_lo, G_NORM2, lambda q: add_fresh("out2", q, 8, 2), also=behind)
            for u in (gate_u, up_u):
                v.memset(u[:, :, 0:PAD], 0.0).then_inc(pad_set, 1)
            dve.wait_ge(pad_set, 2)
            ffn("ffn2", (4 * KT, yT_hi, yT_lo, G_NORM2), xT_hi, xT_lo, FF // W, True, 2, 5, 2, None)

        @block.gpsimd
        def _(pool):
            g_ = nc.gpsimd
            g_.memset(ones[:], 1.0).then_inc(const_set, 1)
            g_.memset(minus_half[:], -0.5).then_inc(const_set, 1)
            for dst, eps in ((eps_diff, P * SUBLN_EPS), (eps_mlstm, M_DV * RMS_EPS), (eps_fox, P * RMS_EPS)):
                g_.memset(dst[:], eps).then_inc(const_set, 1)
            for j in range(NS):
                g_.memset(raw[j][:, :, WH:W], 0.0).then_inc(const_set, 1)
            pool.sem_inc(lo_ready, NS)
            pool.sem_inc(slot_used, NS)
            for s in (by_act, by_dve, part_sq, x_kept, *(k for h in (hb, ha, hm, hf) for k in (h.qk_T, h.ms, h.y_lo))):
                pool.sem_inc(s, FREE)
            pool.wait_ge(const_set, N_CONST)

            def factor(n, dst):
                g_.tensor_scalar(ms[:], ss[:], 1.0 / D, RMS_EPS, ALU.mult, ALU.add).then_inc(ms_ready, 1)
                pool.wait_ge(ms_ready, n)
                return g_.tensor_tensor(dst[:], ms[:], minus_half[:, 0:NT], ALU.pow)

            pool.wait_ge(x_sq, 2)
            factor(1, rstd).then_inc(rstd_ready, 1)

            def rope_head(s, h, phase, z, table, heads4, rot):
                half = rot // 2
                pool.wait_ge(by_act, h.num(2, FREE + PH[phase][BY_ACT] + 2))
                pool.wait_ge(s.qk_T, h.num(1, FREE))
                g_.tensor_copy(stage[:].rearrange("p t c n -> p t (c n)"), z[:, :, ds(h.num(WH), 2 * P)]).then_inc(s.rope, 1)
                pool.wait_ge(s.rope, h.upto(4, 1))
                r = stage[:].rearrange("p t c (e n) -> p (t c e) n", e=heads4)
                u = rot_u[:].rearrange("p (k n) -> p k n", n=rot)
                w = rot_v[:].rearrange("p (k n) -> p k n", n=rot)
                g_.tensor_tensor(u, r[:, :, 0:rot], table[:, 0], ALU.mult).then_inc(s.rope, 1)
                g_.tensor_tensor(w[:, :, 0:half], r[:, :, half:rot], table[:, 1, :, 0:half], ALU.mult).then_inc(s.rope, 1)
                g_.tensor_tensor(w[:, :, half:rot], r[:, :, 0:half], table[:, 1, :, half:rot], ALU.mult).then_inc(s.rope, 1)
                pool.wait_ge(s.rope, h.upto(4))
                g_.tensor_tensor(r[:, :, 0:rot], u, w, ALU.add).then_inc(s.staged, 1)

            def head_factor(s, h, n, sq, eps):
                pool.wait_ge(s.sq, h.upto(sq))
                g_.tensor_tensor(head_ms[:, 0:n], head_ss[:, 0:n], eps[:, 0:n], ALU.add).then_inc(s.ms, 1)
                pool.wait_ge(s.ms, h.num(1, FREE + 1))
                g_.tensor_tensor(head_rstd[:, 0:n], head_ms[:, 0:n], minus_half[:, 0:n], ALU.pow).then_inc(s.rstd, 1)

            pool.wait_ge(small_landed, 16 * N_SMALL)
            with pool.Fori(0, 8) as i:
                h = Head(i, 0, 1)
                rope_head(hb, h, "in_b", z1, rope_b, 2, 16)
                head_factor(hb, h, NT, 2, eps_diff)
            pool.wait_ge(hb.qk_T, FREE + HEADS)
            with pool.Fori(0, 8) as i:
                rope_head(ha, Head(i, 0, 1), "in_a", z2, rope_a, 1, 32)

            def keep(name):
                with pool.Fori(0, 2) as i:
                    for g in range(2):
                        pool.wait_ge(by_dve, at(i, FREE + PH[name][BY_DVE] + 2 * g + 2, 4))
                        g_.tensor_copy(x[:, :, ds(i * (2 * W) + g * W, W)], fresh[g]).then_inc(x_kept, 1)
            keep("out_a")
            pool.wait_ge(ss_ready, 1)
            factor(2, rstd).then_inc(rstd_ready, 1)
            keep("ffn1_down2")
            pool.wait_ge(ss_ready, 2)
            factor(3, rstd).then_inc(rstd_ready, 1)

            pool.wait_ge(x_sq, 4)
            factor(4, rstd_n).then_inc(norm1_step, 1)
            pool.wait_ge(norm1_step, 1)
            g_.tensor_tensor(rstd2[:], rstd[:], rstd_n[:], ALU.mult).then_inc(norm1_step, 1)
            pool.wait_ge(norm1_step, 2)
            g_.tensor_scalar(half_rstd2[:], rstd2[:], 0.5, None, ALU.mult).then_inc(rstd_ready, 1)
            pool.wait_ge(by_act, FREE + PH["in_f"][BY_ACT])
            pool.wait_ge(ha.qk_T, FREE + HEADS)
            with pool.Fori(0, 4) as i:
                h = Head(i, 0, 1)
                pool.wait_ge(hm.qk_T, h.num(1, FREE))
                src = z1[:, :, 0:2 * M_HEADS * P].rearrange("p t (c n) -> p t c n", c=2)[:, :, :, ds(h.num(P), P)]
                g_.tensor_copy(stage[:], src).then_inc(hm.staged, 1)
                head_factor(hm, h, NT, 2, eps_mlstm)
            pool.wait_ge(hm.qk_T, FREE + M_HEADS)
            with pool.Fori(0, 8) as i:
                h = Head(i, 0, 1)
                head_factor(hf, h, 4, 4, eps_fox)
                pool.wait_ge(hf.rstd, h.upto())
                pool.wait_ge(hf.qk_T, h.num(1, FREE))
                z = z2[:, :, :].rearrange("p t (c n) -> p t c n", c=3)[:, :, 0:2, ds(h.num(P), P)]
                r = head_rstd[:].rearrange("p (t c) -> p t c", t=NT).unsqueeze(3).to_broadcast([P, NT, 2, P])
                g_.tensor_tensor(stage[:], z, r, ALU.mult).then_inc(hf.staged, 1)
            keep("out2")
            pool.wait_ge(ss_ready, 3)
            factor(5, rstd).then_inc(rstd_ready, 1)


_INS = ['x', 'norm_attn', 'w_in', 'lambda_qk', 'subln', 'w_out', 'norm_ffn', 'w_gate', 'w_up', 'w_down', 'norm_final',
        'norm1_g_2', 'w_in_2', 'fox_f_bias_2', 'q_norm_g_2', 'k_norm_g_2', 'm_i_bias_2', 'm_f_bias_2', 'm_norm_g_2',
        'w_proj_a_2', 'w_proj_m_2', 'w_out_2', 'norm2_g_2', 'w_up_2', 'conv_w_2', 'conv_b_2', 'w_down_2']


def _tables():
    import numpy as np
    f = np.float32
    tok = np.arange(S)
    far = f(-1e30)
    dist = tok[:, None] - tok[None, :]
    count = (np.abs(dist) <= 64).astype(f) + (dist % 4 == 0) + (dist % 16 == 0)
    log_count = np.where(count > 0, np.log(np.maximum(count, 1)), far).astype(f)
    mask = np.where(dist >= 0, f(0), far).astype(f)

    def by_tile(m):
        return m.reshape(NT, P, -1).transpose(1, 0, 2)

    def rope(rot, copies):
        inv = np.power(f(500000.0), -np.arange(0, rot, 2, dtype=f) / f(rot), dtype=f)
        ang = tok.astype(f)[:, None] * inv[None, :]
        c, s = np.cos(ang), np.sin(ang)
        both = [np.concatenate([c, c], 1), np.concatenate([-s, s], 1)]
        return np.stack([np.repeat(by_tile(b)[:, :, None], copies, 2).reshape(P, NT * copies, rot) for b in both], 1).astype(f)

    return {
        "c_ident": np.eye(P, dtype=f),
        "c_tri": np.triu(np.ones((P, P), f)),
        "c_causal": np.ascontiguousarray(np.concatenate([mask[:P, :P], mask[P:, :]], 1)),
        "c_count": np.ascontiguousarray(by_tile(log_count)),
        "c_rope_a": np.ascontiguousarray(rope(32, 2)),
        "c_rope_b": np.ascontiguousarray(rope(16, 4)),
    }


def kernel(**inputs):
    import numpy as np
    import concourse.bacc as bacc
    from concourse.bass_utils import run_bass_kernel_spmd

    nc = bacc.Bacc("TRN2", target_bir_lowering=False, num_devices=1)
    arrays = {f"in_{name}": np.ascontiguousarray(inputs[name]) for name in _INS}
    arrays.update(_tables())
    aps = {}
    for name, v in arrays.items():
        aps[name.removeprefix("in_")] = nc.dram_tensor(name, v.shape, mybir.dt.from_np(v.dtype), kind="ExternalInput").ap()
    out = nc.dram_tensor("out_x", (1, S, D), F32, kind="ExternalOutput").ap()
    two_blocks(nc, aps, out)
    r = run_bass_kernel_spmd(nc, [arrays], core_ids=[0])
    return r.results[0]["out_x"]
```
